# Optimizing a Trainium2 kernel written in Bass

```python
import math
import functools
import jax
import jax.numpy as jnp
from jax import lax
import numpy as np

D_MODEL = 1024
BATCH = 1
SEQ = 256
DEPTH = 1
DEC_BATCH = 1
DEC_SEQ = 64
PAST_LEN = 128

CHUNK = 64
Q_BLOCK = 128
RET_HEADS = 4
RET_QK_DIM = 128
RET_V_DIM = 256
ROPE_BASE = 10000.0
FOX_HEADS = 16
FOX_HEAD_DIM = 64
N_GROUPS = 4
EXPERTS_PER_GROUP = 8
N_EXPERTS = N_GROUPS * EXPERTS_PER_GROUP
TOP_K = 2
EXPERT_DIM = 512
MOE_BLOCK = 256
RET_QK_W = RET_HEADS * RET_QK_DIM
RET_V_W = RET_HEADS * RET_V_DIM
FOX_W = FOX_HEADS * FOX_HEAD_DIM
FGATE_OFFSET = 2 * RET_QK_W + 2 * RET_V_W + 3 * FOX_W
N_IN = FGATE_OFFSET + FOX_HEADS + 2 * D_MODEL
DEEPNORM_ALPHA = (2 * DEPTH) ** 0.25
DEEPNORM_BETA = (8 * DEPTH) ** -0.25
LN_EPS = 1e-5
GN_EPS = 1e-6

kernel_name = "hybrid_retention_fox_hmoe_stream_step"

def _split_in(z):
    sizes = (RET_QK_W, RET_QK_W, RET_V_W, RET_V_W, FOX_W, FOX_W, FOX_W, FOX_HEADS, D_MODEL, D_MODEL)
    cuts = [int(c) for c in np.cumsum(sizes)[:-1]]
    return jnp.split(z, cuts, axis=-1)

def layer_norm(x, w, b):
    xf = x.astype(jnp.float32)
    mu = jnp.mean(xf, axis=-1, keepdims=True)
    var = jnp.mean(jnp.square(xf - mu), axis=-1, keepdims=True)
    return ((xf - mu) * lax.rsqrt(var + LN_EPS) * w + b).astype(x.dtype)

def head_group_norm(o, w, b):
    mu = jnp.mean(o, axis=-1, keepdims=True)
    var = jnp.mean(jnp.square(o - mu), axis=-1, keepdims=True)
    on = (o - mu) * lax.rsqrt(var + GN_EPS)
    return on.reshape(o.shape[0], o.shape[1], -1) * w + b

def rotary(x, pos):
    half = x.shape[-1] // 2
    inv = ROPE_BASE ** (-jnp.linspace(0.0, 1.0, half, dtype=jnp.float32))
    ang = pos.astype(jnp.float32)[:, None] * inv[None, :]
    cos = jnp.cos(ang)[None, :, None, :]
    sin = jnp.sin(ang)[None, :, None, :]
    x1, x2 = x[..., :half], x[..., half:]
    return jnp.concatenate([x1 * cos - x2 * sin, x1 * sin + x2 * cos], axis=-1)

def retention_log_decay():
    return jnp.log1p(-jnp.exp(jnp.linspace(math.log(1.0 / 32), math.log(1.0 / 512), RET_HEADS, dtype=jnp.float32)))

def ret_chunk(q, k, v, state, log_gamma):
    L = q.shape[1]
    n = jnp.arange(L, dtype=jnp.float32)
    diff = n[:, None] - n[None, :]
    decay = jnp.where(diff[None] >= 0, jnp.exp(jnp.maximum(diff, 0.0)[None] * log_gamma[:, None, None]), 0.0)
    scores = jnp.einsum('bnhk,bmhk->bhnm', q, k) * decay
    inner = jnp.einsum('bhnm,bmhv->bnhv', scores, v)
    q_decay = jnp.exp((n + 1.0)[:, None] * log_gamma[None, :])
    cross = jnp.einsum('bnhk,bhkv->bnhv', q, state) * q_decay[None, :, :, None]
    k_decay = jnp.exp((L - 1.0 - n)[:, None] * log_gamma[None, :])
    new_state = (jnp.exp(L * log_gamma)[None, :, None, None] * state
                 + jnp.einsum('bmhk,bmhv->bhkv', k * k_decay[None, :, :, None], v))
    return inner + cross, new_state

def retention_prompt(q, k, v, log_gamma):
    B, S, H, dk = q.shape
    dv = v.shape[-1]
    nc = S // CHUNK

    def to_chunks(t):
        return t.reshape(B, nc, CHUNK, *t.shape[2:]).swapaxes(0, 1)

    def step(state, qkv):
        o, state = ret_chunk(qkv[0], qkv[1], qkv[2], state, log_gamma)
        return state, o

    state0 = jnp.zeros((B, H, dk, dv), jnp.float32)
    state, o = lax.scan(step, state0, (to_chunks(q), to_chunks(k), to_chunks(v)))
    return o.swapaxes(0, 1).reshape(B, S, H, dv), state

def fox_attend(q, k, v, F_q, F_k, q_pos, k_pos):
    s = jnp.einsum('bqhd,bkhd->bhqk', q, k, preferred_element_type=jnp.float32) * (FOX_HEAD_DIM ** -0.5)
    bias = F_q.transpose(0, 2, 1)[:, :, :, None] - F_k.transpose(0, 2, 1)[:, :, None, :]
    s = jnp.where((q_pos[:, None] >= k_pos[None, :])[None, None], s + bias, -jnp.inf)
    p = jax.nn.softmax(s, axis=-1)
    return jnp.einsum('bhqk,bkhd->bqhd', p.astype(v.dtype), v)

def fox_prompt(q, k, v, logf):
    S = q.shape[1]
    F = jnp.cumsum(logf, axis=1)
    pos = jnp.arange(S, dtype=jnp.int32)
    outs = []
    for i in range(S // Q_BLOCK):
        a, e = i * Q_BLOCK, (i + 1) * Q_BLOCK
        outs.append(fox_attend(q[:, a:e], k[:, :e], v[:, :e], F[:, a:e], F[:, :e], pos[a:e], pos[:e]))
    return jnp.concatenate(outs, axis=1)

def fox_sample(q, k, v, logf, cache_k, cache_v, cache_logf):
    past = cache_k.shape[1]
    L = q.shape[1]
    k_all = jnp.concatenate([cache_k.astype(k.dtype), k], axis=1)
    v_all = jnp.concatenate([cache_v.astype(v.dtype), v], axis=1)
    F = jnp.cumsum(jnp.concatenate([cache_logf.astype(jnp.float32), logf], axis=1), axis=1)
    q_pos = past + jnp.arange(L, dtype=jnp.int32)
    k_pos = jnp.arange(past + L, dtype=jnp.int32)
    return fox_attend(q, k_all, v_all, F[:, past:], F, q_pos, k_pos)

def moe_ffn(h, w_rg, b_rg, w_re, b_re, w_e_in, w_e_out):
    M, D = h.shape
    hf = h.astype(jnp.float32)
    g_prob = jax.nn.softmax(hf @ w_rg.astype(jnp.float32) + b_rg.astype(jnp.float32), axis=-1)
    g_p, g_i = lax.top_k(g_prob, 1)
    e_logits = (hf @ w_re.astype(jnp.float32) + b_re.astype(jnp.float32)).reshape(M, N_GROUPS, EXPERTS_PER_GROUP)
    e_logits = jnp.take_along_axis(e_logits, g_i[:, :, None], axis=1)[:, 0]
    e_p, e_i = lax.top_k(jax.nn.softmax(e_logits, axis=-1), TOP_K)
    gate = g_p * e_p / jnp.sum(e_p, axis=-1, keepdims=True)
    expert = g_i * EXPERTS_PER_GROUP + e_i
    A = M * TOP_K
    flat_e = expert.reshape(A)
    flat_g = gate.reshape(A).astype(h.dtype)
    flat_t = jnp.repeat(jnp.arange(M, dtype=jnp.int32), TOP_K)
    order = jnp.argsort(flat_e)
    se = flat_e[order]
    counts = jnp.bincount(flat_e, length=N_EXPERTS)
    starts = jnp.cumsum(counts) - counts
    pcounts = (counts + MOE_BLOCK - 1) // MOE_BLOCK * MOE_BLOCK
    pends = jnp.cumsum(pcounts)
    pstarts = pends - pcounts
    dest = pstarts[se] + jnp.arange(A, dtype=jnp.int32) - starts[se]
    n_blocks = -(-(A + N_EXPERTS * (MOE_BLOCK - 1)) // MOE_BLOCK)
    P = n_blocks * MOE_BLOCK
    slot_t = jnp.zeros((P,), jnp.int32).at[dest].set(flat_t[order])
    slot_g = jnp.zeros((P,), h.dtype).at[dest].set(flat_g[order])
    block_e = jnp.minimum(jnp.searchsorted(pends, jnp.arange(n_blocks, dtype=jnp.int32) * MOE_BLOCK, side='right'),
                          N_EXPERTS - 1).astype(jnp.int32)

    def expert_block(args):
        e, t, g = args
        a, u = jnp.split(h[t] @ w_e_in[e], 2, axis=-1)
        return ((jax.nn.silu(a) * u) @ w_e_out[e]) * g[:, None]

    y = lax.map(expert_block, (block_e, slot_t.reshape(n_blocks, MOE_BLOCK), slot_g.reshape(n_blocks, MOE_BLOCK)))
    return jnp.zeros_like(h).at[slot_t].add(y.reshape(P, D))

def layer_forward(x, c, pos, ret_fn, fox_fn, w_ada, b_ada, w_in, b_in, ret_gn_w, ret_gn_b, w_ret_proj,
                  w_fox_proj, w_o, ln1_w, ln1_b, w_rg, b_rg, w_re, b_re, w_e_in, w_e_out, ln2_w, ln2_b):
    B, L, _ = x.shape
    mod = jax.nn.silu(c) @ w_ada + b_ada
    sh1, sc1, g1, sh2, sc2, g2 = jnp.split(mod[:, None, :], 6, axis=-1)
    h = x * (1 + sc1) + sh1
    rq, rk, rv, rg, fq, fk, fv, ff, ga, gb = _split_in(h @ w_in + b_in)
    rq = rotary(rq.reshape(B, L, RET_HEADS, RET_QK_DIM), pos).astype(jnp.float32)
    rk = (rotary(rk.reshape(B, L, RET_HEADS, RET_QK_DIM), pos) * (RET_QK_DIM ** -0.5)).astype(jnp.float32)
    rv = rv.reshape(B, L, RET_HEADS, RET_V_DIM).astype(jnp.float32)
    o_ret, ret_state = ret_fn(rq, rk, rv)
    y_ret = (jax.nn.silu(rg) * head_group_norm(o_ret, ret_gn_w, ret_gn_b).astype(x.dtype)) @ w_ret_proj
    fq = fq.reshape(B, L, FOX_HEADS, FOX_HEAD_DIM)
    fk = fk.reshape(B, L, FOX_HEADS, FOX_HEAD_DIM)
    fv = fv.reshape(B, L, FOX_HEADS, FOX_HEAD_DIM)
    logf = jax.nn.log_sigmoid(ff.astype(jnp.float32))
    y_fox = fox_fn(fq, fk, fv, logf).reshape(B, L, FOX_W) @ w_fox_proj
    mixed = (jax.nn.sigmoid(ga) * y_ret + jax.nn.sigmoid(gb) * y_fox) @ w_o
    x = layer_norm(DEEPNORM_ALPHA * x + (1 + g1) * mixed, ln1_w, ln1_b)
    h = x * (1 + sc2) + sh2
    y_moe = moe_ffn(h.reshape(B * L, D_MODEL), w_rg, b_rg, w_re, b_re, w_e_in, w_e_out).reshape(B, L, D_MODEL)
    x = layer_norm(DEEPNORM_ALPHA * x + (1 + g2) * y_moe, ln2_w, ln2_b)
    return x, ret_state, fk, fv, logf

def setup_inputs(seed: int = 0) -> dict:
    key = jax.random.key(seed)
    ks = jax.random.split(key, 32)
    f32 = jnp.float32
    D = D_MODEL
    NL = DEPTH

    def nrm(k, shape, scale):
        return scale * jax.random.normal(k, shape, f32)

    fgate_init = jnp.linspace(1.0, 5.0, FOX_HEADS, dtype=f32)
    x_prompt = nrm(ks[0], (BATCH, SEQ, D), 1.0)
    x_sample = nrm(ks[1], (DEC_BATCH, DEC_SEQ, D), 1.0)
    state_ret = nrm(ks[2], (NL, DEC_BATCH, RET_HEADS, RET_QK_DIM, RET_V_DIM), 0.5)
    cache_fox_k = nrm(ks[3], (NL, DEC_BATCH, PAST_LEN, FOX_HEADS, FOX_HEAD_DIM), 1.0)
    cache_fox_v = nrm(ks[4], (NL, DEC_BATCH, PAST_LEN, FOX_HEADS, FOX_HEAD_DIM), 1.0)
    cache_fox_logf = jax.nn.log_sigmoid(fgate_init + nrm(ks[5], (NL, DEC_BATCH, PAST_LEN, FOX_HEADS), 1.0))
    c_prompt = nrm(ks[6], (BATCH, D), 1.0)
    c_sample = nrm(ks[7], (DEC_BATCH, D), 1.0)
    w_ada = nrm(ks[8], (NL, D, 6 * D), 0.1 * D ** -0.5)
    b_ada = nrm(ks[9], (NL, 6 * D), 0.02)
    w_in = nrm(ks[10], (NL, D, N_IN), D ** -0.5)
    b_in = nrm(ks[11], (NL, N_IN), 0.02).at[:, FGATE_OFFSET:FGATE_OFFSET + FOX_HEADS].add(fgate_init)
    ret_gn_w = 1.0 + nrm(ks[12], (NL, RET_V_W), 0.02)
    ret_gn_b = nrm(ks[13], (NL, RET_V_W), 0.02)
    w_ret_proj = nrm(ks[14], (NL, RET_V_W, D), RET_V_W ** -0.5)
    w_fox_proj = nrm(ks[15], (NL, FOX_W, D), FOX_W ** -0.5)
    w_o = nrm(ks[16], (NL, D, D), DEEPNORM_BETA * D ** -0.5)
    ln1_w = 1.0 + nrm(ks[17], (NL, D), 0.02)
    ln1_b = nrm(ks[18], (NL, D), 0.02)
    w_rg = nrm(ks[19], (NL, D, N_GROUPS), D ** -0.5)
    b_rg = nrm(ks[20], (NL, N_GROUPS), 0.01)
    w_re = nrm(ks[21], (NL, D, N_EXPERTS), D ** -0.5)
    b_re = nrm(ks[22], (NL, N_EXPERTS), 0.01)
    w_e_in = nrm(ks[23], (NL, N_EXPERTS, D, 2 * EXPERT_DIM), D ** -0.5)
    w_e_out = nrm(ks[24], (NL, N_EXPERTS, EXPERT_DIM, D), DEEPNORM_BETA * EXPERT_DIM ** -0.5)
    ln2_w = 1.0 + nrm(ks[25], (NL, D), 0.02)
    ln2_b = nrm(ks[26], (NL, D), 0.02)
    return {"x_prompt": x_prompt, "x_sample": x_sample, "state_ret": state_ret,
            "cache_fox_k": cache_fox_k, "cache_fox_v": cache_fox_v, "cache_fox_logf": cache_fox_logf,
            "c_prompt": c_prompt, "c_sample": c_sample, "w_ada": w_ada, "b_ada": b_ada,
            "w_in": w_in, "b_in": b_in, "ret_gn_w": ret_gn_w, "ret_gn_b": ret_gn_b,
            "w_ret_proj": w_ret_proj, "w_fox_proj": w_fox_proj, "w_o": w_o, "ln1_w": ln1_w, "ln1_b": ln1_b,
            "w_rg": w_rg, "b_rg": b_rg, "w_re": w_re, "b_re": b_re, "w_e_in": w_e_in, "w_e_out": w_e_out,
            "ln2_w": ln2_w, "ln2_b": ln2_b}

def reference(x_prompt, x_sample, state_ret, cache_fox_k, cache_fox_v, cache_fox_logf, c_prompt, c_sample,
              w_ada, b_ada, w_in, b_in, ret_gn_w, ret_gn_b, w_ret_proj, w_fox_proj, w_o, ln1_w, ln1_b,
              w_rg, b_rg, w_re, b_re, w_e_in, w_e_out, ln2_w, ln2_b):
    log_gamma = retention_log_decay()
    past = cache_fox_k.shape[2]
    pos_p = jnp.arange(x_prompt.shape[1], dtype=jnp.int32)
    pos_s = past + jnp.arange(x_sample.shape[1], dtype=jnp.int32)
    ret_p = functools.partial(retention_prompt, log_gamma=log_gamma)
    xp, xs = x_prompt, x_sample
    p_ret, p_k, p_v, p_f, s_ret, s_k, s_v, s_f = [], [], [], [], [], [], [], []
    for l in range(DEPTH):
        lw = (w_ada[l], b_ada[l], w_in[l], b_in[l], ret_gn_w[l], ret_gn_b[l], w_ret_proj[l], w_fox_proj[l],
              w_o[l], ln1_w[l], ln1_b[l], w_rg[l], b_rg[l], w_re[l], b_re[l], w_e_in[l], w_e_out[l],
              ln2_w[l], ln2_b[l])
        xp, st, kk, vv, ff = layer_forward(xp, c_prompt, pos_p, ret_p, fox_prompt, *lw)
        p_ret.append(st); p_k.append(kk); p_v.append(vv); p_f.append(ff)
        ret_s = functools.partial(ret_chunk, state=state_ret[l].astype(jnp.float32), log_gamma=log_gamma)
        fox_s = functools.partial(fox_sample, cache_k=cache_fox_k[l], cache_v=cache_fox_v[l],
                                  cache_logf=cache_fox_logf[l])
        xs, st, kk, vv, ff = layer_forward(xs, c_sample, pos_s, ret_s, fox_s, *lw)
        s_ret.append(st); s_k.append(kk); s_v.append(vv); s_f.append(ff)
    return (xp, xs, jnp.stack(p_ret), jnp.stack(p_k), jnp.stack(p_v), jnp.stack(p_f),
            jnp.stack(s_ret), jnp.stack(s_k), jnp.stack(s_v), jnp.stack(s_f))


_drawn_inputs = setup_inputs


def setup_inputs(seed=0):
    import zlib

    import numpy as np

    out = dict(_drawn_inputs(seed))
    spreads = {}
    factors = {'ret_gn_w': 15.231,
     'ret_gn_b': 35.046,
     'b_rg': 22.139,
     'b_re': 22.432,
     'ln2_w': 22.011,
     'ln2_b': 21.913,
     'cache_fox_k': 3.263}
    for name, (base, spread) in spreads.items():
        noise = np.random.default_rng([zlib.crc32(name.encode()), seed]).standard_normal(out[name].shape)
        drawn = base * np.exp(spread * noise) if base else spread * noise
        out[name] = jnp.asarray(drawn.astype(out[name].dtype))
    for name, factor in factors.items():
        out[name] = (out[name] * factor).astype(out[name].dtype)
    return out
```

```python
import math
from contextlib import ExitStack

import numpy as np

import concourse.bass as bass
from concourse import mybir

F32 = mybir.dt.float32
F32R = mybir.dt.float32r
BF16 = mybir.dt.bfloat16
I32 = mybir.dt.int32
U32 = mybir.dt.uint32
ALU = mybir.AluOpType
ACT = mybir.ActivationFunctionType
AX = mybir.AxisListType

D = 1024
SEQ, DEC, PAST = 256, 64, 128
T = SEQ + DEC
P = 128
KD = D // P
RH, DK, DV = 4, 128, 256
FH, DH = 16, 64
NG, EG, NE = 4, 8, 32
FE = 512
FGATE = 2 * RH * DK + 2 * RH * DV + 3 * FH * DH
NIN = FGATE + FH + 2 * D
ALPHA = 2.0 ** 0.25
LN_EPS, GN_EPS = 1e-5, 1e-6
SLOTS = 64
EXTRA = 2 * T // SLOTS
ITEMS = NE + EXTRA
SKIP = 1.0e6
NEG = -3.0e38

PACK = {}
_at = 0
for _name, _w in (("ident", P), ("causal", P), ("before", P), ("rot", 3 * 2 * 64), ("qdec", RH * 64),
                  ("kdec", 3 * RH), ("iota", SLOTS), ("tok1", 3), ("valid", 3)):
    PACK[_name] = (_at, _at + _w)
    _at += _w
PACK_W = _at


def log_gamma():
    return np.log1p(-np.exp(np.linspace(math.log(1.0 / 32), math.log(1.0 / 512), RH, dtype=np.float32))).astype(np.float64)


def shape_tables():
    pack = np.zeros((P, PACK_W), np.float32)

    def put(name, value):
        a, b = PACK[name]
        pack[:, a:b] = np.asarray(value, np.float32).reshape(P, b - a)

    p = np.arange(P)
    put("ident", np.eye(P))
    put("causal", np.where(p[:, None] >= p[None, :], 0.0, NEG))
    put("before", p[:, None] < p[None, :])
    half = DK // 2
    inv = np.float32(10000.0) ** (-np.linspace(0.0, 1.0, half, dtype=np.float32))
    pos = np.stack([p, P + p, PAST + p], 1).astype(np.float32)
    ang = (pos[:, :, None] * inv[None, None, :]).astype(np.float32).astype(np.float64)
    put("rot", np.stack([np.cos(ang), np.sin(ang)], 2))
    g = log_gamma()
    put("qdec", np.broadcast_to(np.exp((np.arange(DEC) + 1.0)[None, :] * g[:, None])[None], (P, RH, DEC)))
    back = np.stack([SEQ - 1 - p, SEQ - 1 - P - p, DEC - 1 - np.minimum(p, DEC - 1)], 1)
    put("kdec", np.exp(back[:, :, None] * g[None, None, :]) * DK ** -0.5)
    put("iota", np.broadcast_to(np.arange(SLOTS), (P, SLOTS)))
    put("tok1", np.stack([1 + p, 1 + P + p, 1 + SEQ + p], 1))
    put("valid", np.stack([p >= 0, p >= 0, p < DEC], 1))
    n = np.arange(SEQ)[None, :] - p[:, None]
    decay = np.where(n[:, None] >= 0, np.exp(np.maximum(n, 0)[:, None] * g[None, :, None]), 0.0) * DK ** -0.5
    return pack, decay.astype(np.float32)


class Steps:

    def __init__(self, eng, own):
        self.eng, self.own, self.count, self.last = eng, own, {}, None

    def __call__(self, ins, sem=None):
        if isinstance(sem, tuple):
            ins.then_inc(sem[0], 1)
            self.last = sem
            return
        sem = self.own if sem is None else sem
        ins.then_inc(sem, 1)
        self.count[sem.name] = self.count.get(sem.name, 0) + 1
        self.last = (sem, self.count[sem.name])

    def settle(self):
        self.eng.wait_ge(*self.last)


def build_layer(nc, i, o, scratch):
    ctx = ExitStack()
    base = 16512
    off = {"next": base}

    def fixed(name, shape, dt):
        size = int(np.prod(shape[1:])) * (2 if dt == BF16 else 4)
        t = nc.alloc_sbuf_tensor_at(name, shape, dt, offset=off["next"])
        off["next"] += (size + 31) // 32 * 32
        return t

    NRAW, NSPL = 6, 3
    raw = [fixed(f"w_raw{s}", [P, 4, 512], F32) for s in range(NRAW)]
    whi = [fixed(f"w_hi{s}", [P, 4, 512], F32R) for s in range(NSPL)]
    wlo = [fixed(f"w_lo{s}", [P, 4, 512], F32R) for s in range(NSPL)]
    pack = fixed("pack", [P, PACK_W], F32)
    identb = fixed("identb", [P, P], BF16)
    causalb = fixed("causalb", [P, P], BF16)
    bias = fixed("bias_rows", [P, 2, 512], F32)
    low_s = fixed("low_sum", [DEC, 512], F32)
    f_tok = fixed("forget_sums", [P, 4, FH], F32)
    lf_tok = fixed("log_forgets", [P, 3, FH], F32)
    PH = off["next"]
    END = 229368

    def at(name, shape, dt, offset):
        size = int(np.prod(shape[1:])) * (2 if dt == BF16 else 4)
        assert PH + offset + size <= END, (name, PH, offset, size)
        return nc.alloc_sbuf_tensor_at(name, shape, dt, offset=PH + offset)

    def const(name, rows=P):
        a, b = PACK[name]
        return pack[0:rows, a:b]

    ident = const("ident")
    actH = at("h_hi", [P, KD, 384], F32R, 0)
    actL = at("h_lo", [P, KD, 256], F32R, 12288)
    gate = at("gate", [P, 3, D], F32, 20480)
    rqk = at("ret_qk", [P, 3, D], F32, 32768)
    o_ret = at("o_ret", [P, 3, D], F32, 32768)
    rg = at("ret_gate", [P, 3, D], F32, 45056)
    rot = at("ret_rot", [P, 3, D], F32, 65536)
    rv = at("ret_v", [P, 3, D], F32, 77824)
    decay = at("decay", [P, RH, SEQ], F32, 57344)
    s0 = at("state_in", [P, RH, DV], F32, 61440)
    gnw = at("gn_w", [P, D], F32, 57344)
    gnb = at("gn_b", [P, D], F32, 61440)
    qT = at("ret_qT", [P, RH, T], F32, 90112)
    kT = at("ret_kT", [P, RH, T], F32, 95232)
    qdT = at("ret_qdT", [P, RH, DEC], F32, 100352)
    sT = at("ret_sT", [P, 384], F32, 101376)
    small = PACK["rot"][0]
    stats = pack[:, small:small + 192]
    sTs = pack[0:DEC, small + 192:small + 256]
    rot_t = at("rot_tmp", [P, 2, 512], F32, 20480)
    retH = at("ret_hi", [P, KD, 384], F32R, 45056)
    retL = at("ret_lo", [P, KD, 256], F32R, 57344)
    x_tok = at("x_tok", [P, 3, D], F32, 32768)
    hT = at("hT", [P, KD, T], F32, 45056)
    cst = at("c_parts", [P, KD, 64], F32R, 57344)
    c2 = at("c_rows", [2, D], F32, 90112)
    cs2 = at("c_silu", [2, D], F32, 94208)
    mod = at("mod_rows", [2, 6 * D], F32, 65536)
    modT = at("mod_cols", [P, 2, KD, 2], F32, 59392)
    wf_raw = at("wf_raw", [P, KD, FH], F32, 90112)
    wf_hi = at("wf_hi", [P, KD, FH], F32R, 90624)
    wf_lo = at("wf_lo", [P, KD, FH], F32R, 91136)
    zf = at("zf", [FH, T], F32, 91648)
    za = at("zf_abs", [FH, T], F32, 92928)
    zl = at("zf_log", [FH, T], F32, 94208)
    lfT = at("lfT", [FH, T], F32, 95488)
    fsT = at("fsT", [FH, T + PAST], F32, 96768)
    onesT = at("onesT", [FH, T], F32, 98560)
    cf_tok = at("cache_lf", [P, FH], F32, 99840)
    cfT = at("cache_lfT", [FH, PAST], F32, 99904)
    bf_col = at("b_f", [FH, 1], F32, 100416)
    kaug = at("fox_k", [P, 4, FH, DH + 2], F32, 65536)
    qaug = at("fox_q", [P, 3, FH, DH + 2], F32, 82432)
    fv = at("fox_v", [P, 4, D], F32, 32768)
    qst = at("q_head", [P, 3, DH + 2], F32, 49152)
    kst = at("k_head", [P, 4, DH + 2], F32, 49152 + 800)
    vst = at("v_head", [P, 4, DH], F32, 49152 + 1888)
    qTh = at("qT_head", [DH + 2, T], F32, 49152 + 2912)
    kTh = at("kT_head", [DH + 2, T + PAST], F32, 49152 + 4192)
    pr = at("probs", [P, 3, SEQ], F32, 49152 + 5984)
    prT = at("probsT", [P, 512], F32, 49152 + 9056)
    nmax = at("neg_max", [P, 3], F32, 49152 + 11104)
    psums = at("prob_sums", [P, 3], F32, 49152 + 11136)
    pinv = at("prob_inv", [P, 3], F32, 49152 + 11168)
    foxH = at("fox_hi", [P, KD, 384], F32R, 49152)
    foxL = at("fox_lo", [P, KD, 256], F32R, 65536)
    gate_b = at("gate_b", [P, 3, D], F32, 82432)
    mixH = at("mix_hi", [P, KD, 384], F32R, 82432)
    mixL = at("mix_lo", [P, KD, 256], F32R, 94720)
    x1 = at("x1", [P, 3, D], F32, 32768)
    xres = at("x_again", [P, 3, D], F32, 45056)
    h2 = at("h2", [P, 3, D], F32, 45056)
    g1p = at("g1_prompt", [P, D], F32, 57344)
    g1s = at("g1_sample", [DEC, D], F32, 61440)
    l1w = at("ln1_w", [P, D], F32, 65536)
    l1b = at("ln1_b", [P, D], F32, 69632)
    m2p = at("mod2_prompt", [P, 2, D], F32, 0)
    m2s = at("mod2_sample", [DEC, 2, D], F32, 8192)
    h2T = at("h2T", [P, KD, T], F32, 73728)
    R0 = 20480
    ro = {"n": R0}

    def rt(name, shape, dt=F32):
        t = at(name, shape, dt, ro["n"])
        ro["n"] += (int(np.prod(shape[1:])) * (2 if dt == BF16 else 4) + 31) // 32 * 32
        assert ro["n"] <= 32768
        return t

    wr = rt("w_router", [P, KD, NG + NE])
    br = rt("b_router", [P, NG + NE])
    lgT = rt("logitsT", [NG + NE, T])
    lg = rt("logits", [P, 3, NG + NE])
    g8 = rt("group8", [P, 3, 8])
    gmx = rt("group_max", [P, 3, 8])
    gix = rt("group_ix", [P, 3, 8], U32)
    gid = rt("group_id", [P, 3, 1])
    gex = rt("group_exp", [P, 3, NG])
    gpr = rt("group_p", [P, 3, 1])
    goh = rt("group_onehot", [P, 3, NG])
    el = rt("expert_logits", [P, 3, EG])
    elt = rt("expert_tmp", [P, 3, EG])
    emx = rt("expert_max", [P, 3, 8])
    eix = rt("expert_ix", [P, 3, 8], U32)
    eid = rt("expert_id", [P, 3, 2])
    gates = rt("gates", [P, 3, 2])
    ga_t = rt("gates_tmp", [P, 3, 2])
    oh = rt("expert_onehot", [P, 3, 2, NE])
    oht = rt("onehot_tmp", [P, 3, 2, NE])
    msk = rt("expert_mask", [P, 3, NE], BF16)
    befb = rt("before_b", [P, P], BF16)
    oneb = rt("ones_b", [P, P], BF16)
    pos = rt("positions", [P, 3, NE])
    cnt = rt("counts", [P, NE])
    ext = rt("extra_items", [P, NE])
    extt = rt("extra_tmp", [P, NE])
    one32 = rt("ones32", [P, NE])
    cum = rt("extra_cum", [P, NE])
    exc = rt("extra_before", [P, NE])
    ch_pos = rt("choice_pos", [P, 3, 2])
    ch_exc = rt("choice_before", [P, 3, 2])
    ch_q = rt("choice_q", [P, 3, 2])
    ch_t = rt("choice_tmp", [P, 3, 2])
    item = rt("choice_item", [P, 3, 2])
    slt = rt("slot_tokens", [SLOTS, 2, ITEMS])
    slt2 = rt("slot_tmp", [SLOTS, 2, ITEMS])
    idx = rt("slot_token", [SLOTS, ITEMS], I32)
    idx1 = rt("slot_token_now", [SLOTS, 1], I32)
    row = rt("slot_row", [SLOTS, ITEMS], I32)
    row1 = rt("slot_row_now", [SLOTS, 1], I32)
    exm = rt("item_expert_cmp", [1, EXTRA, NE])
    exf = rt("item_expert_f", [1, ITEMS])
    exi = rt("item_expert", [1, ITEMS], I32)
    nit = rt("n_extra", [1, 1], I32)
    turn = rt("turn", [1, 3])
    st1 = rt("ln_stats", [P, 2, 6])
    mv = rt("ln_mean_var", [P, 3, 2])
    oh_s = at("slot_onehot", [P, 3, 2, SLOTS], F32, 65536)
    oh_i = at("item_onehot", [P, 3, 2, ITEMS], F32, 65536 + 1536)
    xg = at("x_item", [SLOTS, D], F32, 0)
    xT = at("xT_item", [P, KD, 2 * SLOTS], F32R, 4096)
    aLo = at("a_low", [SLOTS, FE], F32, 8192)
    uLo = at("u_low", [SLOTS, FE], F32, 10240)
    aS = at("a_sum", [SLOTS, FE], F32, 12288)
    aA = at("a_silu", [SLOTS, FE], F32, 14336)
    uS = at("u_sum", [SLOTS, FE], F32, 16384)
    hid = at("hidden", [SLOTS, FE], F32, 18432)
    hdT = at("hiddenT", [P, 4, 2 * SLOTS], F32R, 45056)
    yLo = at("y_low", [SLOTS, 2, 512], F32, 47104)
    ySb = at("y_item", [SLOTS, 2, 512], F32, 51200)
    yg = at("y_choice", [P, 3, 2, D], F32, 57344)
    g2p = at("g2_prompt", [P, D], F32, 81920)
    g2s = at("g2_sample", [DEC, D], F32, 86016)
    l2w = at("ln2_w", [P, D], F32, 90112)
    l2b = at("ln2_b", [P, D], F32, 94208)

    bank = [ctx.enter_context(nc.psum_tensor(f"bank{b}", [P, 512], F32)) for b in range(8)]

    def sem(name):
        return ctx.enter_context(nc.semaphore(name))

    raw_landed = [sem(f"raw_landed{s}") for s in range(NRAW)]
    hi_done, lo_done, used = sem("hi_done"), sem("lo_done"), sem("stream_used")
    filled = [sem(f"bank_filled{b}") for b in range(8)]
    drained = [sem(f"bank_drained{b}") for b in range(8)]
    evacuated = sem("chunk_evacuated")
    bias_landed = [sem("bias_landed0"), sem("bias_landed1")]
    own_act, own_dve, own_pool = sem("own_act"), sem("own_dve"), sem("own_pool")
    pack_in, x_in, c_in, modb_in, wf_in, cf_in = (sem(n) for n in ("pack_in", "x_in", "c_in", "modb_in", "wf_in", "cf_in"))
    consts_ready, c_silu, c_hi, c_parts = sem("consts_ready"), sem("c_silu"), sem("c_hi"), sem("c_parts")
    xT_done, modT_done, h_ready, h_hi, h_split = sem("xT_done"), sem("modT_done"), sem("h_ready"), sem("h_hi"), sem("h_split")
    mod_out = sem("mod_out")
    wf_h, wf_l, zf_done, zf_act, lf_ready, cfT_done, fs_ready, ftok_done = (
        sem(n) for n in ("wf_h", "wf_l", "zf_done", "zf_act", "lf_ready", "cfT_done", "fs_ready", "ftok_done"))
    rot_done, kdec_done, qkT_done, qd_done = sem("rot_done"), sem("kdec_done"), sem("qkT_done"), sem("qd_done")
    dec_in, sT_done, oret_act, state_done, ret_out = sem("dec_in"), sem("sT_done"), sem("oret_act"), sem("state_done"), sem("ret_out")
    gact, gn_in, gn_var, gn_std, ret_ready = sem("gate_act"), sem("gn_in"), sem("gn_var"), sem("gn_std"), sem("ret_ready")
    ts_hi, r_fox = sem("split_hi"), sem("prob_inverse")
    cachek_in, cachev_in, aug_ready, fox_out = sem("cachek_in"), sem("cachev_in"), sem("aug_ready"), sem("fox_out")
    q_st, k_st, v_st, qk_tr, qT_cp, kT_cp, scored, maxed, exped, p_tr, pT_a, pT_d, pv_ok, o_ok = (
        sem(n) for n in ("q_staged", "k_staged", "v_staged", "qk_transposed", "qT_copied", "kT_copied", "scored",
                         "maxed", "exped", "p_transposed", "pT_copied_a", "pT_copied_d", "pv_done", "o_done"))
    res_in, g1_ready, ln_in, ln_var, ln_std, h2_ready, h2_out, h2T_done = (
        sem(n) for n in ("res_in", "g1_ready", "ln_in", "ln_var", "ln_std", "h2_ready", "h2_out", "h2T_done"))
    m2_in, m2_ready, wr_in, lgT_done, lg_done, r_dve, r_act, msk_done, pos_done, slots_ready, slt_done, idx_ready = (
        sem(n) for n in ("m2_in", "m2_ready", "wr_in", "lgT_done", "lg_done", "r_dve", "r_act", "mask_done",
                         "pos_done", "slots_ready", "slt_done", "idx_ready"))
    row_cp = sem("row_copied")
    idx_cp, x_landed, x_trans, x_hi, x_split, a_lo, u_lo, a_drained, u_drained, silu_ok, hid_ok = (
        sem(n) for n in ("idx_copied", "x_landed", "x_transposed", "x_hi", "x_split", "a_low_copied",
                         "u_low_copied", "a_drained", "u_drained", "silu_done", "hidden_done"))
    h_tr, hh_hi, hh_split, y_lo, y_drained, y_written, xg_zero = (
        sem(n) for n in ("hidden_transposed", "hidden_hi", "hidden_split", "y_low_copied", "y_drained", "y_written", "xg_zero"))
    tail_in, g2_ready, yg_in, comb, fin_std, fin_ready, y_out = (
        sem(n) for n in ("tail_in", "g2_ready", "yg_in", "comb", "fin_std", "fin_ready", "y_out"))

    CH = [f"ada{j}" for j in range(12)] + ["rq", "rk", "rv0", "rv1", "rg0", "rg1", "ga0", "ga1", "fq0", "fq1",
                                           "fk0", "fk1", "pr0", "pr1", "fv0", "fv1", "gb0", "gb1", "pf0", "pf1",
                                           "wo0", "wo1"]
    CI = {n: c for c, n in enumerate(CH)}
    zcol = {}
    for n, c0 in (("rq", 0), ("rk", 512), ("rv", 1024), ("rg", 2048), ("fq", 3072), ("fk", 4096), ("fv", 5120),
                  ("ga", FGATE + FH), ("gb", FGATE + FH + D)):
        if n in ("rq", "rk"):
            zcol[n] = c0
        else:
            zcol[n + "0"], zcol[n + "1"] = c0, c0 + 512
    ZCH = [n for n in CH if n in zcol]
    N0 = 2 * len(CH)

    use, free_at, fills, drains = {}, {}, [0] * 8, [0] * 8

    def plan(key, b, filled_at=None, drained_at=None):
        before = free_at.get(b)
        if filled_at is None:
            fills[b] += 1
            filled_at = (filled[b], fills[b])
        if drained_at is None:
            drains[b] += 1
            drained_at = (drained[b], drains[b])
        use[key] = (bank[b], before, filled_at, drained_at)
        free_at[b] = drained_at

    def dense_banks(c):
        return (0, 1, 2) if c % 2 == 0 else (3, 4, 5)

    def plan_dense(n):
        c = CI[n]
        b = dense_banks(c)
        if n.startswith("ada"):
            plan((n, 0), b[0], (used, 2 * c + 2), (evacuated, c + 1))
            return
        plan((n, 0), b[0])
        plan((n, 1), b[1])
        plan((n, 2), b[2], (used, 2 * c + 2), (evacuated, c + 1))

    def spare(after):
        return tuple(dense_banks(CI[after] + 1)) + (6, 7)

    for k in range(KD):
        plan(("xT", k), k % 6)
    plan("cT", 6, drained_at=(c_parts, 1))
    for j in range(5):
        plan_dense(f"ada{j}")
    plan("modT", 7)
    for j in range(5, 12):
        plan_dense(f"ada{j}")
    sp_ = spare("ada11")
    plan("zf", 6)
    plan("cfT", 7)
    for n in ("rq", "rk"):
        plan_dense(n)
    plan("ftok", 6, drained_at=(ftok_done, 2))
    for n in ("rv0", "rv1"):
        plan_dense(n)
    for j in range(2 * RH):
        plan(("qkT", j), spare("rv1")[j % 5], drained_at=(qkT_done, j + 1))
    for n in ("rg0", "rg1", "ga0"):
        plan_dense(n)
    for h in range(RH):
        s = spare("ga0")
        plan(("sc", h), s[3 + h % 2])
        plan(("op", h), s[0])
        plan(("os", h), s[1], drained_at=(state_done, 2 * h + 1))
        plan(("ss", h), s[2], drained_at=(state_done, 2 * h + 2))
    for n in ("ga1", "fq0", "fq1", "fk0", "fk1"):
        plan_dense(n)
    for k in range(KD):
        plan(("ret", k), spare("fk1")[k % 5])
    for n in ("pr0", "pr1", "fv0", "fv1"):
        plan_dense(n)
    fox_start = dict(free_at)
    for b in range(8):
        free_at[b] = (o_ok, FH)
    for k in range(KD):
        plan(("fox", k), k)
    for n in ("gb0", "gb1", "pf0", "pf1"):
        plan_dense(n)
    for k in range(KD):
        plan(("mix", k), spare("pf1")[k % 5])
    for n in ("wo0", "wo1"):
        plan_dense(n)
    for t in range(3):
        for q in range(2):
            plan(("h2T", t, q), (6, 7)[q], drained_at=(h2T_done, 2 * t + q + 1))
    plan("lgT", 0)
    plan("lg", 3)
    plan("pos", 6)
    plan("cnt", 7)
    plan("slt", 0, drained_at=(slt_done, 1))

    block = ctx.enter_context(nc.Block())

    def weight_source(n):
        if n.startswith("ada"):
            w, c0 = i["w_ada"][0], 512 * int(n[3:])
        elif n in zcol:
            w, c0 = i["w_in"][0], zcol[n]
        else:
            w, c0 = i[{"pr": "w_ret_proj", "pf": "w_fox_proj", "wo": "w_o"}[n[:2]]][0], 512 * int(n[2])
        return w.rearrange("(k p) n -> p k n", p=P)[:, :, c0:c0 + 512]

    def bcast(ap1d, rows):
        return ap1d.partition_broadcast(rows)

    w_in_e = i["w_e_in"][0].rearrange("e (k p) n -> e p k n", p=P)
    w_out_e = i["w_e_out"][0].rearrange("e (k p) n -> e p k n", p=P)
    E0 = N0 + 4

    def sub(e, j):
        return E0 + 6 * (e - 1) + j

    def slot_of(j):
        return (E0 + j) % NRAW, (E0 + j) % NSPL

    @block.sync
    def _(sp):
        sp.dma_start(pack[:], i["pack"][:, :]).then_inc(pack_in, 16)
        sp.dma_start(c2[0:1, :], i["c_prompt"][0:1, :]).then_inc(c_in, 16)
        sp.dma_start(c2[1:2, :], i["c_sample"][0:1, :]).then_inc(c_in, 16)
        sp.dma_start(mod[0:1, :], i["b_ada"][0:1, :]).then_inc(modb_in, 16)
        sp.dma_start(mod[1:2, :], i["b_ada"][0:1, :]).then_inc(modb_in, 16)
        sp.dma_start(x_tok[:, 0:2, :], i["x_prompt"][0].rearrange("(t p) d -> p t d", p=P)).then_inc(x_in, 16)
        sp.dma_start(x_tok[0:DEC, 2, :], i["x_sample"][0]).then_inc(x_in, 16)

        def send(n, src):
            if n >= NRAW:
                sp.wait_ge(lo_done, n - NRAW + 1)
            sp.dma_start(raw[n % NRAW][:], src).then_inc(raw_landed[n % NRAW], 16)

        for c, name in enumerate(CH):
            src = weight_source(name)
            if name in zcol:
                m = ZCH.index(name)
                if m >= 2:
                    sp.wait_ge(evacuated, CI[ZCH[m - 2]] + 1)
                sp.dma_start(bias[:, m % 2, :], bcast(i["b_in"][0, zcol[name]:zcol[name] + 512], P)).then_inc(bias_landed[m % 2], 16)
            for s in range(2):
                send(2 * c + s, src[:, 4 * s:4 * s + 4, :])
            if name == "ada11":
                sp.wait_ge(c_hi, 1)
                sp.wait_ge(c_parts, 1)
                sp.dma_start(wf_raw[:], i["w_in"][0].rearrange("(k p) n -> p k n", p=P)[:, :, FGATE:FGATE + FH]).then_inc(wf_in, 16)
                sp.dma_start(cf_tok[:], i["cache_fox_logf"][0, 0]).then_inc(cf_in, 16)
                sp.dma_start(bf_col[:], i["b_in"][0, FGATE:FGATE + FH].rearrange("(p a) -> p a", a=1)).then_inc(wf_in, 16)
        for n in range(4):
            send(N0 + n, w_in_e[0, :, 4 * (n % 2):4 * (n % 2) + 4, 512 * (n // 2):512 * (n // 2) + 512])

        def item_weights(e, expert, before):
            for j in range(6):
                src = (w_in_e[expert, :, 4 * (j % 2):4 * (j % 2) + 4, 512 * (j // 2):512 * (j // 2) + 512] if j < 4
                       else w_out_e[before, :, :, 512 * (j - 4):512 * (j - 4) + 512])
                if not isinstance(e, int):
                    src = src.rearrange("e p k n -> (e p) k n")
                sp.wait_ge(lo_done, sub(e, j) - NRAW + 1)
                sp.dma_start(raw[slot_of(j)[0]][:], src).then_inc(raw_landed[slot_of(j)[0]], 16)

        item_weights(1, 1, 0)
        with sp.Fori(2, NE) as e:
            item_weights(e, bass.ds(e, 1), bass.ds(e - 1, 1))
        sp.wait_ge(idx_ready, 1)
        items = NE + sp.value_load(nit[0:1, 0:1], min_val=0, max_val=EXTRA - 1)
        with sp.If(items > NE):
            with sp.Fori(NE, items) as e:
                ex = sp.value_load(exi[0:1, bass.ds(e, 1)], min_val=0, max_val=NE - 1)
                bf = sp.value_load(exi[0:1, bass.ds(e - 1, 1)], min_val=0, max_val=NE - 1)
                item_weights(e, bass.ds(ex, 1), bass.ds(bf, 1))
        last = sp.value_load(exi[0:1, bass.ds(items - 1, 1)], min_val=0, max_val=NE - 1)
        for j in range(2):
            sp.wait_ge(lo_done, sub(items, j) - NRAW + 1)
            sp.dma_start(raw[slot_of(j)[0]][:],
                         w_out_e[bass.ds(last, 1), :, :, 512 * j:512 * j + 512].rearrange("e p k n -> (e p) k n")
                         ).then_inc(raw_landed[slot_of(j)[0]], 16)
        sp.wait_ge(ret_out, 32)
        sp.wait_ge(fox_out, 16 * 6)
        sp.wait_ge(y_out, 32)

    @block.gpsimd
    def _(pool):
        st = Steps(pool, own_pool)
        nc.gpsimd.memset(cst[:].bitcast(F32), 0.0).then_inc(xg_zero, 1)
        nc.gpsimd.memset(onesT[:], 1.0).then_inc(xg_zero, 1)
        pool.wait_ge(evacuated, CI["ada11"] + 1)
        pool.dma_start(scratch["mod"][:, :], mod[:, :]).then_inc(mod_out, 16)
        pool.wait_ge(h_split, KD)
        pool.wait_ge(used, 2 * CI["ada11"] + 2)
        pool.dma_start(decay[:], i["decay"][:, :, :]).then_inc(dec_in, 16)
        pool.dma_start(s0[:], i["state_ret"][0, 0].rearrange("h k v -> k h v")).then_inc(dec_in, 16)
        pool.wait_ge(ftok_done, 2)
        pool.dma_start(o["p_f"][0, 0].rearrange("(t p) h -> p t h", p=P), lf_tok[:, 0:2, :]).then_inc(fox_out, 16)
        pool.dma_start(o["s_f"][0, 0], lf_tok[0:DEC, 2, :]).then_inc(fox_out, 16)
        pool.wait_ge(qkT_done, 2 * RH)
        a, b = PACK["kdec"]
        for t in range(3):
            rows = P if t < 2 else DEC
            kk = rot[0:rows, t, 512:1024].rearrange("p (h d) -> p h d", h=RH)
            dd = pack[0:rows, a + RH * t:a + RH * t + RH].unsqueeze(2).to_broadcast([rows, RH, DK])
            st(nc.gpsimd.tensor_tensor(kk, kk, dd, ALU.mult), kdec_done)
        pool.wait_ge(state_done, 2 * RH)
        pool.dma_start(o["p_s"][0, 0].rearrange("h k v -> k h v"), qT[:, :, 0:DV]).then_inc(ret_out, 16)
        pool.dma_start(o["s_s"][0, 0].rearrange("h k v -> k h v"), s0[:]).then_inc(ret_out, 16)
        pool.wait_ge(ret_out, 32)
        pool.dma_start(gnw[:], bcast(i["ret_gn_w"][0], P)).then_inc(gn_in, 16)
        pool.dma_start(gnb[:], bcast(i["ret_gn_b"][0], P)).then_inc(gn_in, 16)
        pool.dma_start(kaug[:, 2, :, 0:DH], i["cache_fox_k"][0, 0]).then_inc(cachek_in, 16)
        st(nc.gpsimd.memset(qaug[DEC:P, 2, :, :], 0.0))
        st.settle()
        st(nc.gpsimd.memset(kaug[DEC:P, 3, :, :], 0.0))
        st.settle()
        st(nc.gpsimd.memset(qaug[:, 0:2, :, DH + 1:DH + 2], 8.0))
        st(nc.gpsimd.memset(qaug[0:DEC, 2, :, DH + 1:DH + 2], 8.0))
        st(nc.gpsimd.memset(kaug[:, 0:3, :, DH:DH + 1], 1.0))
        st(nc.gpsimd.memset(kaug[0:DEC, 3, :, DH:DH + 1], 1.0))
        st.settle()
        q_slots = (0, 1, 3)
        for t in range(3):
            rows = P if t < 2 else DEC
            st(nc.gpsimd.tensor_scalar(qaug[0:rows, t, :, DH], f_tok[0:rows, q_slots[t], :], 8.0, None, ALU.mult))
        for t in range(4):
            rows = P if t < 3 else DEC
            st(nc.gpsimd.tensor_scalar(kaug[0:rows, t, :, DH + 1], f_tok[0:rows, t, :], -1.0, None, ALU.mult),
               aug_ready if t == 3 else None)
        pool.wait_ge(used, 2 * CI["pr1"] + 2)
        pool.dma_start(fv[:, 2, :], i["cache_fox_v"][0, 0].rearrange("t h d -> t (h d)")).then_inc(cachev_in, 16)
        st(nc.gpsimd.memset(fv[DEC:P, 3, :], 0.0))
        st.settle()
        st(nc.gpsimd.memset(psums[:], 1.0), aug_ready)
        pool.wait_ge(evacuated, CI["fk1"] + 1)
        pool.dma_start(o["p_k"][0, 0].rearrange("(t p) h d -> p t h d", p=P)[:, 0], kaug[:, 0, :, 0:DH]).then_inc(fox_out, 16)
        pool.dma_start(o["p_k"][0, 0].rearrange("(t p) h d -> p t h d", p=P)[:, 1], kaug[:, 1, :, 0:DH]).then_inc(fox_out, 16)
        pool.dma_start(o["s_k"][0, 0], kaug[0:DEC, 3, :, 0:DH]).then_inc(fox_out, 16)
        pool.wait_ge(evacuated, CI["fv1"] + 1)
        pool.dma_start(o["p_v"][0, 0].rearrange("(t p) h d -> p t (h d)", p=P), fv[:, 0:2, :]).then_inc(ret_out, 16)
        pool.dma_start(o["s_v"][0, 0].rearrange("p h d -> p (h d)"), fv[0:DEC, 3, :]).then_inc(fox_out, 16)
        pool.wait_ge(cachev_in, 16)
        with pool.Fori(0, FH) as h:
            nc.gpsimd.tensor_copy(vst[:], fv[:, :, bass.ds(h * DH, DH)]).then_inc(v_st, 1)
            pool.wait_ge(pv_ok, h + 1)
        pool.wait_ge(fox_out, 16 * 6)
        pool.wait_ge(ret_out, 48)
        pool.wait_ge(used, 2 * CI["pf1"] + 2)
        pool.wait_ge(mod_out, 16)
        pool.dma_start(xres[:, 0:2, :], i["x_prompt"][0].rearrange("(t p) d -> p t d", p=P)).then_inc(res_in, 16)
        pool.dma_start(xres[0:DEC, 2, :], i["x_sample"][0]).then_inc(res_in, 16)
        md = scratch["mod"]
        pool.dma_start(g1p[:], bcast(md[0, 2 * D:3 * D], P)).then_inc(res_in, 16)
        pool.dma_start(g1s[:], bcast(md[1, 2 * D:3 * D], DEC)).then_inc(res_in, 16)
        pool.wait_ge(res_in, 64)
        st(nc.gpsimd.tensor_scalar(g1p[:], g1p[:], 1.0, None, ALU.add), g1_ready)
        st(nc.gpsimd.tensor_scalar(g1s[:], g1s[:], 1.0, None, ALU.add), g1_ready)
        pool.wait_ge(evacuated, CI["pf1"] + 1)
        pool.dma_start(l1w[:], bcast(i["ln1_w"][0], P)).then_inc(ln_in, 16)
        pool.dma_start(l1b[:], bcast(i["ln1_b"][0], P)).then_inc(ln_in, 16)
        pool.dma_start(m2p[:, :, :], bcast(md[0, 3 * D:5 * D].rearrange("(a d) -> a d", a=2), P)).then_inc(m2_in, 16)
        pool.dma_start(m2s[:, :, :], bcast(md[1, 3 * D:5 * D].rearrange("(a d) -> a d", a=2), DEC)).then_inc(m2_in, 16)
        pool.wait_ge(m2_in, 32)
        st(nc.gpsimd.tensor_scalar(m2p[:, 1, :], m2p[:, 1, :], 1.0, None, ALU.add), m2_ready)
        st(nc.gpsimd.tensor_scalar(m2s[:, 1, :], m2s[:, 1, :], 1.0, None, ALU.add), m2_ready)
        pool.wait_ge(evacuated, CI["wo0"] + 1)
        pool.dma_start(wr[:, :, 0:NG], i["w_rg"][0].rearrange("(k p) n -> p k n", p=P)).then_inc(wr_in, 16)
        pool.dma_start(wr[:, :, NG:], i["w_re"][0].rearrange("(k p) n -> p k n", p=P)).then_inc(wr_in, 16)
        pool.dma_start(br[:, 0:NG], bcast(i["b_rg"][0], P)).then_inc(wr_in, 16)
        pool.dma_start(br[:, NG:], bcast(i["b_re"][0], P)).then_inc(wr_in, 16)
        h2d = scratch["h2"]
        pool.wait_ge(h2_ready, 2)
        pool.dma_start(h2d[0:SEQ, :].rearrange("(t p) d -> p t d", p=P), h2[:, 0:2, :]).then_inc(h2_out, 16)
        pool.wait_ge(h2_ready, 3)
        pool.dma_start(h2d[SEQ:T, :], h2[0:DEC, 2, :]).then_inc(h2_out, 16)
        st(nc.gpsimd.memset(xg[:], 0.0))
        st.settle()
        pool.wait_ge(h2_out, 32)
        pool.wait_ge(idx_ready, 1)
        n_items = NE + pool.value_load(nit[0:1, 0:1], min_val=0, max_val=EXTRA - 1)

        def gather(col):
            nc.gpsimd.tensor_copy(idx1[:], idx[:, col]).then_inc(idx_cp, 1)

        gather(slice(0, 1))
        pool.wait_ge(idx_cp, 1)
        nc.gpsimd.indirect_dma_start(xg[:], None, h2d[:, :], bass.IndirectOffsetOnAxis(ap=idx1[:, 0:1], axis=0),
                                     bounds_check=T - 1, oob_is_err=False).then_inc(x_landed, 16)
        pool.wait_ge(h2T_done, 6)
        pool.wait_ge(slt_done, 1)
        pool.dma_start(g2p[:], bcast(md[0, 5 * D:6 * D], P)).then_inc(tail_in, 16)
        pool.dma_start(g2s[:], bcast(md[1, 5 * D:6 * D], DEC)).then_inc(tail_in, 16)
        pool.dma_start(l2w[:], bcast(i["ln2_w"][0], P)).then_inc(tail_in, 16)
        pool.dma_start(l2b[:], bcast(i["ln2_b"][0], P)).then_inc(tail_in, 16)
        pool.wait_ge(tail_in, 64)
        st(nc.gpsimd.tensor_scalar(g2p[:], g2p[:], 1.0, None, ALU.add), g2_ready)
        st(nc.gpsimd.tensor_scalar(g2s[:], g2s[:], 1.0, None, ALU.add), g2_ready)
        yd = scratch["y"]

        def hold(place=0):
            nc.gpsimd.tensor_tensor(turn[:, place:place + 1], ident[0:1, 0:1], ident[0:1, 0:1], ALU.mult)

        def next_gather(e):
            pool.wait_ge(x_landed, 16 * (e + 1))
            nc.gpsimd.tensor_copy(idx1[:], idx[:, bass.ds(e + 1, 1)]).then_inc(idx_cp, 1)
            pool.wait_ge(idx_cp, e + 2)
            pool.wait_ge(x_trans, e + 1)
            hold()
            nc.gpsimd.indirect_dma_start(xg[:], None, h2d[:, :], bass.IndirectOffsetOnAxis(ap=idx1[:, 0:1], axis=0),
                                         bounds_check=T - 1, oob_is_err=False).then_inc(x_landed, 16)

        def store_item(e):
            if not isinstance(e, int) or e > 0:
                pool.wait_ge(y_written, 16 * e)
            nc.gpsimd.tensor_copy(row1[:], row[:, bass.ds(e, 1)]).then_inc(row_cp, 1)
            pool.wait_ge(row_cp, e + 1)
            pool.wait_ge(y_drained, 2 * (e + 1))
            hold(1)
            nc.gpsimd.indirect_dma_start(yd[:, :], bass.IndirectOffsetOnAxis(ap=row1[:, 0:1], axis=0),
                                         ySb[:].rearrange("p a b -> p (a b)"), None,
                                         bounds_check=2 * T - 1, oob_is_err=False).then_inc(y_written, 16)

        next_gather(0)
        next_gather(1)
        with pool.Fori(2, n_items) as e:
            next_gather(e)
            store_item(e - 2)
        store_item(n_items - 2)
        store_item(n_items - 1)
        pool.wait_ge(y_written, n_items * 16)
        hold(2)
        y3 = yd.rearrange("(t c) d -> t c d", c=2)
        pool.dma_start(yg[:, 0:2, :, :], y3[0:SEQ].rearrange("(t p) c d -> p t c d", p=P)).then_inc(yg_in, 16)
        pool.dma_start(yg[0:DEC, 2, :, :], y3[SEQ:T]).then_inc(yg_in, 16)
        pool.wait_ge(fin_ready, 2)
        pool.dma_start(o["y_p"][0].rearrange("(t p) d -> p t d", p=P), x1[:, 0:2, :]).then_inc(y_out, 16)
        pool.wait_ge(fin_ready, 3)
        pool.dma_start(o["y_s"][0], x1[0:DEC, 2, :]).then_inc(y_out, 16)

    TS = [("ret", 0), ("fox", 1), ("mix", 2)]

    @block.scalar
    def _(act):
        st = Steps(act, own_act)

        def hi(n):
            act.wait_ge(raw_landed[n % NRAW], 16 * (n // NRAW + 1))
            if n >= NSPL:
                act.wait_ge(used, n - NSPL + 1)
            nc.scalar.activation(whi[n % NSPL][:], raw[n % NRAW][:], ACT.Copy).then_inc(hi_done, 1)

        def chunk(name):
            hi(2 * CI[name])
            hi(2 * CI[name] + 1)

        def copy_bank(key, dst, src):
            b, _, f, d = use[key]
            act.wait_ge(*f)
            st(nc.scalar.activation(dst, src(b), ACT.Copy), d)

        def gate_fn(name, buf, fn):
            act.wait_ge(evacuated, CI[name] + 1)
            h = slice(512 * int(name[2]), 512 * int(name[2]) + 512)
            st(nc.scalar.activation(buf[:, 0:2, h], buf[:, 0:2, h], fn), gact)
            st(nc.scalar.activation(buf[0:DEC, 2, h], buf[0:DEC, 2, h], fn), gact)

        def split_hi(kind, dst):
            for k in range(KD):
                b, _, f, _ = use[(kind, k)]
                act.wait_ge(*f)
                st(nc.scalar.activation(dst[:, k, 0:T], b[:, 0:T], ACT.Copy), ts_hi)

        hi(0)
        act.wait_ge(c_in, 32)
        st(nc.scalar.activation(cs2[:], c2[:], ACT.Silu), c_silu)
        hi(1)
        hi(2)
        for k in range(KD):
            b, _, f, d = use[("xT", k)]
            act.wait_ge(*f)
            st(nc.scalar.activation(hT[:, k, :], b[:, 0:T], ACT.Copy), d)
        b, _, f, _ = use["cT"]
        act.wait_ge(*f)
        act.wait_ge(xg_zero, 1)
        st(nc.scalar.activation(cst[:, :, 0:2], b[:, 0:2 * KD].rearrange("p (k c) -> p k c", c=2), ACT.Copy), c_hi)
        hi(3)
        for j in range(2, 5):
            chunk(f"ada{j}")
        for k in range(KD):
            act.wait_ge(h_ready, 2 * k + 2)
            st(nc.scalar.activation(actH[:, k, 0:T], hT[:, k, :], ACT.Copy), h_hi)
        for j in range(5, 12):
            chunk(f"ada{j}")
        act.wait_ge(wf_in, 32)
        st(nc.scalar.activation(wf_hi[:], wf_raw[:], ACT.Copy), wf_h)
        chunk("rq")
        act.wait_ge(zf_done, 1)
        st(nc.scalar.activation(zl[:], za[:], ACT.Exp, scale=-1.0))
        st.settle()
        st(nc.scalar.activation(zl[:], zl[:], ACT.Ln, bias=1.0), zf_act)
        chunk("rk")
        copy_bank("cfT", cfT[:], lambda b: b[0:FH, 0:PAST])
        chunk("rv0")
        chunk("rv1")
        chunk("rg0")
        for j in range(2 * RH):
            dst = (qT if j < RH else kT)[:, j % RH, :]
            b, _, f, d = use[("qkT", j)]
            act.wait_ge(*f)
            act.wait_ge(ftok_done, 2)
            act.wait_ge(fox_out, 16 * 2)
            st(nc.scalar.activation(dst, b[:, 0:T], ACT.Copy), qkT_done)
        chunk("rg1")
        gate_fn("rg0", rg, ACT.Silu)
        chunk("ga0")
        gate_fn("rg1", rg, ACT.Silu)
        for h in range(RH):
            hs = slice(DV * h, DV * h + DV)
            copy_bank(("op", h), o_ret[:, 0:2, hs], lambda b: b[:, 0:512].rearrange("p (t v) -> p t v", t=2))
            b, _, f, _ = use[("os", h)]
            act.wait_ge(*f)
            st(nc.scalar.activation(o_ret[0:DEC, 2, hs], b[0:DEC, 0:DV], ACT.Copy), oret_act)
        chunk("ga1")
        gate_fn("ga0", gate, ACT.Sigmoid)
        chunk("fq0")
        gate_fn("ga1", gate, ACT.Sigmoid)
        act.wait_ge(gn_var, 1)
        st(nc.scalar.activation(stats[:, 120:132], stats[:, 108:120], ACT.Sqrt), gn_std)
        for n in ("fq1", "fk0", "fk1"):
            chunk(n)
        split_hi("ret", retH)
        for n in ("pr0", "pr1", "fv0", "fv1"):
            chunk(n)
        hi(2 * CI["gb0"])
        act.wait_ge(aug_ready, 2)
        act.wait_ge(evacuated, CI["fv1"] + 1)
        with act.Fori(0, FH) as h:
            nc.scalar.activation(qst[:], qaug[:, :, bass.ds(h, 1), :].rearrange("p t a d -> p t (a d)"), ACT.Copy,
                                 scale=DH ** -0.5).then_inc(q_st, 1)
            act.wait_ge(qk_tr, h + 1)
            nc.scalar.activation(qTh[:], bank[0][0:DH + 2, 0:T], ACT.Copy).then_inc(qT_cp, 1)
            act.wait_ge(maxed, h + 1)
            nc.scalar.activation(pr[:, 0, 0:P], bank[2][:, 0:P], ACT.Exp, bias=nmax[:, 0:1], accum_out=psums[:, 0:1])
            nc.scalar.activation(pr[:, 1, :], bank[2][:, P:384], ACT.Exp, bias=nmax[:, 1:2], accum_out=psums[:, 1:2])
            nc.scalar.activation(pr[0:DEC, 2, 0:192], bank[3][0:DEC, 0:192], ACT.Exp, bias=nmax[0:DEC, 2:3],
                                 accum_out=psums[0:DEC, 2:3]).then_inc(exped, 1)
            act.wait_ge(p_tr, h + 1)
            nc.scalar.activation(prT[:, 0:256], bank[4][:, 0:256], ACT.Copy).then_inc(pT_a, 1)
        hi(2 * CI["gb0"] + 1)
        split_hi("fox", foxH)
        chunk("gb1")
        gate_fn("gb0", gate_b, ACT.Sigmoid)
        chunk("pf0")
        gate_fn("gb1", gate_b, ACT.Sigmoid)
        chunk("pf1")
        hi(2 * CI["wo0"])
        split_hi("mix", mixH)
        hi(2 * CI["wo0"] + 1)
        chunk("wo1")
        hi(N0)
        act.wait_ge(ln_var, 1)
        st(nc.scalar.activation(mv[:, :, 1], mv[:, :, 1], ACT.Sqrt), ln_std)
        for t in range(3):
            for q in range(2):
                b, _, f, d = use[("h2T", t, q)]
                rows = P if t < 2 else DEC
                act.wait_ge(*f)
                st(nc.scalar.activation(h2T[:, 4 * q:4 * q + 4, P * t:P * t + rows],
                                        b[:, 0:4 * rows].rearrange("p (k c) -> p k c", k=4), ACT.Copy), h2T_done)
        copy_bank("lgT", lgT[:], lambda b: b[0:NG + NE, 0:T])
        act.wait_ge(r_dve, 1)
        st(nc.scalar.activation(gex[:], gex[:], ACT.Exp), r_act)
        act.wait_ge(r_dve, 2)
        st(nc.scalar.activation(ga_t[:, :, 1:2], ga_t[:, :, 0:1], ACT.Exp), r_act)

        def item_hi(e, j):
            rs, ss = slot_of(j)
            act.wait_ge(raw_landed[rs], 16 * ((E0 + j - rs) // NRAW + e))
            act.wait_ge(used, sub(e, j) - NSPL + 1)
            nc.scalar.activation(whi[ss][:], raw[rs][:], ACT.Copy).then_inc(hi_done, 1)

        def x_high(e):
            act.wait_ge(x_trans, e + 1)
            nc.scalar.activation(xT[:, :, 0:SLOTS], bank[4][:, :].rearrange("p (k c) -> p k c", k=KD), ACT.Copy).then_inc(x_hi, 1)

        def silu(e):
            act.wait_ge(a_drained, e + 1)
            nc.scalar.activation(aA[:], aS[:], ACT.Silu).then_inc(silu_ok, 1)

        def y_low(e, first_sub):
            for j in range(2):
                act.wait_ge(used, first_sub + j + 1)
                nc.scalar.activation(yLo[:, j, :], bank[2 + j][SLOTS:P, :], ACT.Copy).then_inc(y_lo, 1)

        def hidden_high(e):
            act.wait_ge(h_tr, e + 1)
            nc.scalar.activation(hdT[:, :, 0:SLOTS], bank[5][:, 0:4 * SLOTS].rearrange("p (k c) -> p k c", k=4), ACT.Copy).then_inc(hh_hi, 1)

        def low_copy(after, dst, b, done):
            act.wait_ge(used, after + 1)
            nc.scalar.activation(dst[:], bank[b][SLOTS:P, :], ACT.Copy).then_inc(done, 1)

        x_high(0)
        for n in range(1, 4):
            hi(N0 + n)
        low_copy(N0 + 1, aLo, 0, a_lo)
        low_copy(N0 + 3, uLo, 1, u_lo)
        x_high(1)

        def item(e, second):
            item_hi(e, 0)
            silu(e - 1)
            item_hi(e, 1)
            if second:
                y_low(e - 2, sub(e - 1, 4))
            item_hi(e, 2)
            hidden_high(e - 1)
            item_hi(e, 3)
            act.wait_ge(a_drained, e)
            low_copy(sub(e, 1), aLo, 0, a_lo)
            item_hi(e, 4)
            item_hi(e, 5)
            act.wait_ge(u_drained, e)
            low_copy(sub(e, 3), uLo, 1, u_lo)
            x_high(e + 1)

        item(1, False)
        act.wait_ge(idx_ready, 1)
        n_items = NE + act.value_load(nit[0:1, 0:1], min_val=0, max_val=EXTRA - 1)
        with act.Fori(2, n_items) as e:
            item(e, True)
        item_hi(n_items, 0)
        silu(n_items - 1)
        item_hi(n_items, 1)
        y_low(n_items - 2, sub(n_items - 1, 4))
        hidden_high(n_items - 1)
        act.wait_ge(y_drained, (n_items - 1) * 2)
        y_low(n_items - 1, sub(n_items, 0))
        act.wait_ge(fin_std, 1)
        nc.scalar.activation(mv[:, :, 1], mv[:, :, 1], ACT.Sqrt).then_inc(ln_std, 1)

    @block.vector
    def _(dve):
        st = Steps(dve, own_dve)
        V = nc.vector

        def lo(n):
            dve.wait_ge(hi_done, n + 1)
            V.tensor_tensor(wlo[n % NSPL][:], raw[n % NRAW][:], whi[n % NSPL][:].bitcast(F32), ALU.subtract).then_inc(lo_done, 1)

        def chunk(name):
            lo(2 * CI[name])
            lo(2 * CI[name] + 1)

        def filled_of(key):
            b, _, f, d = use[key]
            dve.wait_ge(*f)
            return b, d

        def destination(name):
            h = int(name[2]) if name[2:] else 0
            cols = slice(512 * h, 512 * h + 512)
            if name == "rq":
                return [rqk[:, t, 0:512] for t in range(3)]
            if name == "rk":
                return [rqk[:, t, 512:1024] for t in range(3)]
            if name[:2] == "fq":
                return [qaug[:, t, 8 * h:8 * h + 8, 0:DH] for t in range(3)]
            if name[:2] == "fk":
                return [kaug[:, t, 8 * h:8 * h + 8, 0:DH] for t in (0, 1, 3)]
            if name[:2] == "fv":
                return [fv[:, t, cols] for t in (0, 1, 3)]
            buf = {"rv": rv, "rg": rg, "ga": gate, "gb": gate_b}[name[:2]]
            return [buf[:, t, cols] for t in range(3)]

        def like(ap, dst):
            return ap.rearrange("p (h d) -> p h d", d=DH) if len(dst.shape) == 3 else ap

        def evac_z(name):
            m = ZCH.index(name)
            dst = destination(name)
            dve.wait_ge(evacuated, CI[name])
            dve.wait_ge(bias_landed[m % 2], 16 * (m // 2 + 1))
            for t in range(2):
                b, d = filled_of((name, t))
                st(V.tensor_tensor(dst[t], like(b[:, :], dst[t]), like(bias[:, m % 2, :], dst[t]), ALU.add), d)
            b, d = filled_of((name, 2))
            st(V.tensor_tensor(low_s[:], b[DEC:P, :], bias[0:DEC, m % 2, :], ALU.add))
            st.settle()
            ds = dst[2][0:DEC]
            st(V.tensor_tensor(ds, like(b[0:DEC, :], ds), like(low_s[:], ds), ALU.add), evacuated)

        def sample_sum(name):
            b, d = filled_of((name, 2))
            st(V.tensor_copy(low_s[:], b[DEC:P, :]))
            st.settle()
            st(V.tensor_tensor(low_s[:], b[0:DEC, :], low_s[:], ALU.add))
            st.settle()

        def evac_ret_proj(name):
            cols = slice(512 * int(name[2]), 512 * int(name[2]) + 512)
            dve.wait_ge(gact, 4 + 4)
            dve.wait_ge(evacuated, CI[name])
            for t in range(2):
                b, d = filled_of((name, t))
                st(V.tensor_tensor(gate[:, t, cols], b[:, :], gate[:, t, cols], ALU.mult), d)
            sample_sum(name)
            st(V.tensor_tensor(gate[0:DEC, 2, cols], low_s[:], gate[0:DEC, 2, cols], ALU.mult), evacuated)

        def evac_fox_proj(name):
            cols = slice(512 * int(name[2]), 512 * int(name[2]) + 512)
            dve.wait_ge(gact, 8 + 4)
            dve.wait_ge(evacuated, CI[name])
            for t in range(2):
                b, d = filled_of((name, t))
                st(V.tensor_tensor(bias[:, t, :], b[:, :], gate_b[:, t, cols], ALU.mult), d)
                st.settle()
                st(V.tensor_tensor(gate[:, t, cols], bias[:, t, :], gate[:, t, cols], ALU.add))
            sample_sum(name)
            st(V.tensor_tensor(low_s[:], low_s[:], gate_b[0:DEC, 2, cols], ALU.mult))
            st.settle()
            st(V.tensor_tensor(gate[0:DEC, 2, cols], low_s[:], gate[0:DEC, 2, cols], ALU.add), evacuated)

        def evac_wo(name):
            cols = slice(512 * int(name[2]), 512 * int(name[2]) + 512)
            dve.wait_ge(res_in, 64)
            dve.wait_ge(g1_ready, 2)
            dve.wait_ge(evacuated, CI[name])
            for t in range(2):
                b, d = filled_of((name, t))
                st(V.tensor_tensor(x1[:, t, cols], b[:, :], g1p[:, cols], ALU.mult), d)
                st.settle()
                st(V.scalar_tensor_tensor(x1[:, t, cols], xres[:, t, cols], ALPHA, x1[:, t, cols], ALU.mult, ALU.add))
            sample_sum(name)
            st(V.tensor_tensor(low_s[:], low_s[:], g1s[:, cols], ALU.mult))
            st.settle()
            st(V.scalar_tensor_tensor(x1[0:DEC, 2, cols], xres[0:DEC, 2, cols], ALPHA, low_s[:], ALU.mult, ALU.add), evacuated)

        def evac_ada(j):
            cols = slice(512 * j, 512 * j + 512)
            b, d = filled_of((f"ada{j}", 0))
            st(V.tensor_tensor(mod[:, cols], b[32:34, :], mod[:, cols], ALU.add))
            st.settle()
            st(V.tensor_tensor(mod[:, cols], b[0:2, :], mod[:, cols], ALU.add), evacuated)

        def split_lo(kind, index, hi_, lo_):
            for k in range(KD):
                b, _, f, d = use[(kind, k)]
                dve.wait_ge(ts_hi, KD * index + k + 1)
                st(V.tensor_tensor(lo_[:, k, :], b[:, 0:SEQ], hi_[:, k, 0:SEQ].bitcast(F32), ALU.subtract))
                st(V.tensor_tensor(hi_[:, k, T:384], b[:, SEQ:T], hi_[:, k, SEQ:T].bitcast(F32), ALU.subtract), d)

        dve.wait_ge(pack_in, 16)
        st(V.tensor_copy(identb[:], ident))
        st(V.tensor_copy(causalb[:], const("causal")), consts_ready)
        lo(0)
        b, d = filled_of("cT")
        dve.wait_ge(c_hi, 1)
        st(V.tensor_tensor(cst[:, :, 32:34], b[:, 0:2 * KD].rearrange("p (k c) -> p k c", c=2),
                           cst[:, :, 0:2].bitcast(F32), ALU.subtract), c_parts)
        lo(1)
        dve.wait_ge(modb_in, 32)
        for j in range(1, 5):
            chunk(f"ada{j}")
            evac_ada(j - 1)
        b, d = filled_of("modT")
        bm = b[:, 0:4 * KD].rearrange("p (a k c) -> p a k c", a=2, k=KD)
        st(V.tensor_copy(modT[:, 0], bm[:, 0]))
        st(V.tensor_scalar(modT[:, 1], bm[:, 1], 1.0, None, ALU.add), d)
        st.settle()
        for k in range(KD):
            dve.wait_ge(*use[("xT", k)][3])
            st(V.tensor_scalar(hT[:, k, 0:SEQ], hT[:, k, 0:SEQ], modT[:, 1, k, 0:1], modT[:, 0, k, 0:1], ALU.mult, ALU.add), h_ready)
            st(V.tensor_scalar(hT[:, k, SEQ:T], hT[:, k, SEQ:T], modT[:, 1, k, 1:2], modT[:, 0, k, 1:2], ALU.mult, ALU.add), h_ready)
        for k in range(KD):
            dve.wait_ge(h_hi, k + 1)
            st(V.tensor_tensor(actL[:, k, :], hT[:, k, 0:SEQ], actH[:, k, 0:SEQ].bitcast(F32), ALU.subtract))
            st(V.tensor_tensor(actH[:, k, T:384], hT[:, k, SEQ:T], actH[:, k, SEQ:T].bitcast(F32), ALU.subtract), h_split)
        for j in range(5, 12):
            chunk(f"ada{j}")
            evac_ada(j - 1)
        dve.wait_ge(wf_h, 1)
        st(V.tensor_tensor(wf_lo[:], wf_raw[:], wf_hi[:].bitcast(F32), ALU.subtract), wf_l)
        chunk("rq")
        evac_ada(11)
        b, d = filled_of("zf")
        st(V.tensor_scalar(zf[:], b[0:FH, 0:T], bf_col[:, 0:1], None, ALU.add), d)
        st.settle()
        st(V.scalar_tensor_tensor(za[:], zf[:], -1.0, zf[:], ALU.mult, ALU.max), zf_done)
        chunk("rk")
        evac_z("rq")
        dve.wait_ge(zf_act, 1)
        st(V.tensor_scalar(lfT[:], zf[:], 0.0, None, ALU.min))
        st.settle()
        st(V.tensor_tensor(lfT[:], lfT[:], zl[:], ALU.subtract), lf_ready)
        st.settle()
        dve.wait_ge(xg_zero, 2)
        dve.wait_ge(use["cfT"][3][0], use["cfT"][3][1])
        st(V.tensor_tensor_scan(fsT[:, 0:SEQ], onesT[:, 0:SEQ], lfT[:, 0:SEQ], 0.0, ALU.mult, ALU.add))
        st(V.tensor_tensor_scan(fsT[:, SEQ:SEQ + PAST], onesT[:, 0:PAST], cfT[:], 0.0, ALU.mult, ALU.add))
        st.settle()
        st(V.tensor_tensor_scan(fsT[:, T + PAST - DEC:T + PAST], onesT[:, 0:DEC], lfT[:, SEQ:T],
                                fsT[:, SEQ + PAST - 1:SEQ + PAST], ALU.mult, ALU.add), fs_ready)
        chunk("rv0")
        evac_z("rk")
        b, d = filled_of("ftok")
        bt = b[:, 0:7 * FH].rearrange("p (t h) -> p t h", h=FH)
        st(V.tensor_copy(f_tok[:, 0:3, :], bt[:, 0:3, :]))
        st(V.tensor_copy(f_tok[0:DEC, 3, :], bt[0:DEC, 3, :]))
        st(V.tensor_copy(lf_tok[:, 0:2, :], bt[:, 4:6, :]), ftok_done)
        st(V.tensor_copy(lf_tok[0:DEC, 2, :], bt[0:DEC, 6, :]), ftok_done)
        dve.wait_ge(mod_out, 16)
        rr = const("rot").rearrange("p (t f c) -> p t f c", t=3, f=2)
        for rows, t0, t1 in ((P, 0, 1), (P, 1, 2), (DEC, 2, 3)):
            src = rqk[0:rows, t0, :].rearrange("p (h a c) -> p h a c", h=2 * RH, a=2)
            out = rot[0:rows, t0, :].rearrange("p (h a c) -> p h a c", h=2 * RH, a=2)
            tmp = rot_t[0:rows, :, :].rearrange("p a (h c) -> p a h c", h=2 * RH)
            cos = rr[0:rows, t0, 0, :].unsqueeze(1).to_broadcast([rows, 2 * RH, 64])
            sin = rr[0:rows, t0, 1, :].unsqueeze(1).to_broadcast([rows, 2 * RH, 64])
            st(V.tensor_tensor(out[:, :, 0, :], src[:, :, 0, :], cos, ALU.mult))
            st(V.tensor_tensor(tmp[:, 0], src[:, :, 1, :], sin, ALU.mult))
            st(V.tensor_tensor(out[:, :, 1, :], src[:, :, 0, :], sin, ALU.mult))
            st(V.tensor_tensor(tmp[:, 1], src[:, :, 1, :], cos, ALU.mult))
            st.settle()
            st(V.tensor_tensor(out[:, :, 0, :], out[:, :, 0, :], tmp[:, 0], ALU.subtract))
            st(V.tensor_tensor(out[:, :, 1, :], out[:, :, 1, :], tmp[:, 1], ALU.add), rot_done)
            st.settle()
        chunk("rv1")
        evac_z("rv0")
        chunk("rg0")
        evac_z("rv1")
        dve.wait_ge(qkT_done, 2 * RH)
        st(V.tensor_tensor(qdT[:], qT[:, :, SEQ:T], const("qdec").rearrange("p (h n) -> p h n", h=RH), ALU.mult), qd_done)
        chunk("rg1")
        evac_z("rg0")
        chunk("ga0")
        evac_z("rg1")
        dve.wait_ge(dec_in, 32)
        gam = [float(np.exp(DEC * g)) for g in log_gamma()]

        def decayed(h):
            b, d = filled_of(("sc", h))
            if h:
                dve.wait_ge(*use[("op", h - 1)][2])
                dve.wait_ge(*use[("os", h - 1)][2])
            st(V.tensor_tensor(sT[:, 0:SEQ], b[:, 0:SEQ], decay[:, h, :], ALU.mult))
            st(V.tensor_tensor(sT[:, SEQ:384], b[:, SEQ:384], decay[:, h, 0:P], ALU.mult))
            st(V.tensor_tensor(sTs, b[0:DEC, 384:448], decay[0:DEC, h, 0:DEC], ALU.mult), d)

        def states(h):
            b, d = filled_of(("os", h))
            dve.wait_ge(oret_act, h + 1)
            st(V.tensor_copy(qT[:, h, 0:DV], b[:, DV:2 * DV]), state_done)
            b2, d2 = filled_of(("ss", h))
            st(V.scalar_tensor_tensor(s0[:, h, :], s0[:, h, :], gam[h], b2[:, 0:DV], ALU.mult, ALU.add), state_done)

        for h in range(RH):
            decayed(h)
            states(h)
        chunk("ga1")
        evac_z("ga0")
        for t in range(3):
            rows = P if t < 2 else DEC
            for h in range(RH):
                st(V.bn_stats(stats[0:rows, 6 * (RH * t + h):6 * (RH * t + h) + 6], o_ret[0:rows, t, DV * h:DV * h + DV]))
        st(V.memset(stats[:, 84:120], 1.0))
        st.settle()
        for t in range(3):
            rows = P if t < 2 else DEC
            for h in range(RH):
                q = RH * t + h
                st(V.bn_aggr(stats[0:rows, 84 + 2 * q:86 + 2 * q], stats[0:rows, 6 * q:6 * q + 6]))
        st.settle()
        mvs = stats[:, 84:108].rearrange("p (q c) -> p q c", c=2)
        st(V.tensor_scalar(stats[:, 108:120], mvs[:, :, 1], GN_EPS, None, ALU.add), gn_var)
        chunk("fq0")
        evac_z("ga1")
        dve.wait_ge(gn_std, 1)
        st(V.reciprocal(stats[:, 132:144], stats[:, 120:132]))
        st.settle()
        for t in range(3):
            rows = P if t < 2 else DEC
            for h in range(RH):
                q = RH * t + h
                oo = o_ret[0:rows, t, DV * h:DV * h + DV]
                st(V.tensor_scalar(oo, oo, mvs[0:rows, q, 0:1], stats[0:rows, 132 + q:133 + q], ALU.subtract, ALU.mult))
        chunk("fq1")
        dve.wait_ge(aug_ready, 1)
        evac_z("fq0")
        dve.wait_ge(gn_in, 32)
        dve.wait_ge(gact, 4)
        for w_, op in ((gnw, ALU.mult), (gnb, ALU.add)):
            st.settle()
            for t in range(3):
                rows = P if t < 2 else DEC
                st(V.tensor_tensor(o_ret[0:rows, t, :], o_ret[0:rows, t, :], w_[0:rows, :], op))
        chunk("fk0")
        evac_z("fq1")
        for t in range(3):
            rows = P if t < 2 else DEC
            st(V.tensor_tensor(o_ret[0:rows, t, :], o_ret[0:rows, t, :], rg[0:rows, t, :], ALU.mult), ret_ready)
        chunk("fk1")
        evac_z("fk0")
        split_lo("ret", 0, retH, retL)
        chunk("pr0")
        evac_z("fk1")
        chunk("pr1")
        evac_ret_proj("pr0")
        chunk("fv0")
        evac_ret_proj("pr1")
        dve.wait_ge(aug_ready, 2)
        chunk("fv1")
        evac_z("fv0")
        lo(2 * CI["gb0"])
        evac_z("fv1")
        dve.wait_ge(cachek_in, 16)
        dve.wait_ge(fox_out, 16 * 6)
        dve.wait_ge(ret_out, 48)
        with dve.Fori(0, FH) as h:
            V.tensor_copy(kst[:], kaug[:, :, bass.ds(h, 1), :].rearrange("p t a d -> p t (a d)")).then_inc(k_st, 1)
            dve.wait_ge(qk_tr, h + 1)
            V.tensor_copy(kTh[:], bank[1][0:DH + 2, 0:T + PAST]).then_inc(kT_cp, 1)
            dve.wait_ge(scored, h + 1)
            V.tensor_reduce(nmax[:, 0:1], bank[2][:, 0:P], AX.X, ALU.max, negate=True)
            V.tensor_reduce(nmax[:, 1:2], bank[2][:, P:384], AX.X, ALU.max, negate=True)
            V.tensor_reduce(nmax[0:DEC, 2:3], bank[3][0:DEC, 0:192], AX.X, ALU.max, negate=True).then_inc(maxed, 1)
            dve.wait_ge(exped, h + 1)
            V.reciprocal(pinv[:], psums[:]).then_inc(r_fox, 1)
            dve.wait_ge(p_tr, h + 1)
            V.tensor_copy(prT[:, 256:448], bank[6][:, 0:192])
            V.tensor_copy(prT[0:DEC, 448:512], bank[6][0:DEC, 192:SEQ]).then_inc(pT_d, 1)
            dve.wait_ge(pv_ok, h + 1)
            dve.wait_ge(r_fox, h + 1)
            for t in range(3):
                rows = P if t < 2 else DEC
                ins = V.tensor_scalar(fv[0:rows, t, bass.ds(h * DH, DH)],
                                      bank[5][0:rows, DH * t:DH * t + DH], pinv[0:rows, t:t + 1], None, ALU.mult)
            ins.then_inc(o_ok, 1)
        lo(2 * CI["gb0"] + 1)
        split_lo("fox", 1, foxH, foxL)
        chunk("gb1")
        evac_z("gb0")
        chunk("pf0")
        evac_z("gb1")
        chunk("pf1")
        evac_fox_proj("pf0")
        lo(2 * CI["wo0"])
        evac_fox_proj("pf1")
        split_lo("mix", 2, mixH, mixL)
        lo(2 * CI["wo0"] + 1)
        chunk("wo1")
        evac_wo("wo0")
        lo(N0)
        evac_wo("wo1")

        def norm(stat_sem, wait_in, w_, b_):
            st(V.memset(mv[:], 1.0))
            for t in range(3):
                rows = P if t < 2 else DEC
                for q in range(2):
                    st(V.bn_stats(st1[0:rows, q, :], x1[0:rows, t, 512 * q:512 * q + 512]))
                st.settle()
                st(V.bn_aggr(mv[0:rows, t, :], st1[0:rows, :, :]))
                st.settle()
            st.settle()
            st(V.tensor_scalar(mv[:, :, 1], mv[:, :, 1], LN_EPS, None, ALU.add), stat_sem)

        norm(ln_var, ln_in, l1w, l1b)
        dve.wait_ge(ln_std, 1)
        st(V.reciprocal(mv[:, :, 1], mv[:, :, 1]))
        st.settle()
        dve.wait_ge(ln_in, 32)
        dve.wait_ge(m2_ready, 2)
        for t in range(3):
            rows = P if t < 2 else DEC
            xt = x1[0:rows, t, :]
            m2 = m2p if t < 2 else m2s
            st(V.tensor_scalar(xt, xt, mv[0:rows, t, 0:1], mv[0:rows, t, 1:2], ALU.subtract, ALU.mult))
            st.settle()
            st(V.tensor_tensor(xt, xt, l1w[0:rows, :], ALU.mult))
            st.settle()
            st(V.tensor_tensor(xt, xt, l1b[0:rows, :], ALU.add))
            st.settle()
            st(V.tensor_tensor(h2[0:rows, t, :], xt, m2[0:rows, 1, :], ALU.mult))
            st.settle()
            st(V.tensor_tensor(h2[0:rows, t, :], h2[0:rows, t, :], m2[0:rows, 0, :], ALU.add), h2_ready)

        iota = const("iota")
        dve.wait_ge(wr_in, 64)
        st(V.memset(lg[:], 0.0))
        st(V.memset(g8[:], NEG))
        st(V.memset(oneb[:], 1.0))
        st(V.memset(one32[:], 1.0))
        st(V.tensor_copy(befb[:], const("before")))
        st.settle()
        b, d = filled_of("lg")
        bl = b[:, 0:3 * (NG + NE)].rearrange("p (t n) -> p t n", t=3)
        brr = br[:, :].unsqueeze(1).to_broadcast([P, 2, NG + NE])
        st(V.tensor_tensor(lg[:, 0:2, :], bl[:, 0:2, :], brr, ALU.add))
        st(V.tensor_tensor(lg[0:DEC, 2, :], bl[0:DEC, 2, :], br[0:DEC, :], ALU.add), d)
        st.settle()
        st(V.tensor_copy(g8[:, :, 0:NG], lg[:, :, 0:NG]))
        st.settle()
        for t in range(3):
            st(V.max(gmx[:, t, :], g8[:, t, :]))
        st.settle()
        for t in range(3):
            st(V.max_index(gix[:, t, :], gmx[:, t, :], g8[:, t, :]))
        st(V.tensor_tensor(gex[:], lg[:, :, 0:NG], gmx[:, :, 0:1].to_broadcast([P, 3, NG]), ALU.subtract), r_dve)
        st.settle()
        st(V.tensor_copy(gid[:], gix[:, :, 0:1]))
        st.settle()
        st(V.tensor_tensor(goh[:], iota[:, 0:NG].unsqueeze(1).to_broadcast([P, 3, NG]), gid[:].to_broadcast([P, 3, NG]), ALU.is_equal))
        st.settle()
        ev = lg[:, :, NG:].rearrange("p t (g e) -> p t g e", g=NG)
        for g in range(NG):
            dst = el if g == 0 else elt
            st(V.tensor_tensor(dst[:], ev[:, :, g, :], goh[:, :, g:g + 1].to_broadcast([P, 3, EG]), ALU.mult))
            st.settle()
            if g:
                st(V.tensor_tensor(el[:], el[:], elt[:], ALU.add))
                st.settle()
        for t in range(3):
            st(V.max(emx[:, t, :], el[:, t, :]))
        st.settle()
        for t in range(3):
            st(V.max_index(eix[:, t, :], emx[:, t, :], el[:, t, :]))
        st(V.tensor_tensor(ga_t[:, :, 0:1], emx[:, :, 1:2], emx[:, :, 0:1], ALU.subtract), r_dve)
        st.settle()
        st(V.tensor_copy(eid[:], eix[:, :, 0:2]))
        st.settle()
        st(V.scalar_tensor_tensor(eid[:], gid[:].to_broadcast([P, 3, 2]), float(EG), eid[:], ALU.mult, ALU.add))
        st.settle()
        i32b = iota[:, 0:NE].unsqueeze(1).to_broadcast([P, 2, NE])
        for t in range(3):
            st(V.tensor_tensor(oh[:, t], i32b, eid[:, t, :].unsqueeze(2).to_broadcast([P, 2, NE]), ALU.is_equal))
        st.settle()
        va = PACK["valid"][0]
        for t in range(3):
            st(V.tensor_scalar(oh[:, t], oh[:, t], pack[:, va + t:va + t + 1], None, ALU.mult))
        st.settle()
        st(V.tensor_tensor(msk[:], oh[:, :, 0, :], oh[:, :, 1, :], ALU.add), msk_done)
        dve.wait_ge(r_act, 2)
        st(V.tensor_reduce(gpr[:], gex[:], AX.X, ALU.add))
        st(V.tensor_scalar(ga_t[:, :, 0:1], ga_t[:, :, 1:2], 1.0, None, ALU.add))
        st.settle()
        st(V.tensor_tensor(gpr[:], gpr[:], ga_t[:, :, 0:1], ALU.mult))
        st.settle()
        st(V.reciprocal(gates[:, :, 0:1], gpr[:]))
        st.settle()
        st(V.tensor_tensor(gates[:, :, 1:2], gates[:, :, 0:1], ga_t[:, :, 1:2], ALU.mult))
        b, d = filled_of("pos")
        st(V.tensor_copy(pos[:], b[:, 0:3 * NE].rearrange("p (t n) -> p t n", t=3)), d)
        b, d = filled_of("cnt")
        st(V.tensor_copy(cnt[:], b[:, 0:NE]), d)
        st.settle()
        st(V.tensor_scalar(ext[:], cnt[:], float(SLOTS), None, ALU.is_gt))
        for m in range(2, -(-T // SLOTS)):
            st(V.tensor_scalar(extt[:], cnt[:], float(SLOTS * m), None, ALU.is_gt))
            st.settle()
            st(V.tensor_tensor(ext[:], ext[:], extt[:], ALU.add))
            st.settle()
        st(V.tensor_tensor_scan(cum[:], one32[:], ext[:], 0.0, ALU.mult, ALU.add))
        st.settle()
        st(V.tensor_tensor(exc[:], cum[:], ext[:], ALU.subtract))
        st.settle()
        for t in range(3):
            st(V.tensor_tensor(oht[:, t], oh[:, t], pos[:, t, :].unsqueeze(1).to_broadcast([P, 2, NE]), ALU.mult))
        st.settle()
        st(V.tensor_reduce(ch_pos[:], oht[:], AX.X, ALU.add))
        st.settle()
        for t in range(3):
            st(V.tensor_tensor(oht[:, t], oh[:, t], exc[:, :].unsqueeze(1).to_broadcast([P, 2, NE]), ALU.mult))
        st.settle()
        st(V.tensor_reduce(ch_exc[:], oht[:], AX.X, ALU.add))
        st(V.tensor_scalar(ch_q[:], ch_pos[:], float(SLOTS), None, ALU.is_ge))
        st.settle()
        st(V.scalar_tensor_tensor(ch_t[:], ch_exc[:], float(NE - 1), eid[:], ALU.add, ALU.subtract))
        st.settle()
        st(V.tensor_tensor(ch_t[:], ch_t[:], ch_q[:], ALU.mult))
        st.settle()
        st(V.tensor_tensor(item[:], ch_t[:], eid[:], ALU.add))
        st.settle()
        for m in range(2, -(-T // SLOTS)):
            st(V.tensor_scalar(ch_t[:], ch_pos[:], float(SLOTS * m), None, ALU.is_ge))
            st.settle()
            st(V.tensor_tensor(ch_q[:], ch_q[:], ch_t[:], ALU.add))
            st.settle()
        st(V.tensor_tensor(item[:], item[:], ch_q[:], ALU.add))
        st(V.scalar_tensor_tensor(ch_pos[:], ch_q[:], -float(SLOTS), ch_pos[:], ALU.mult, ALU.add))
        st.settle()
        t1 = PACK["tok1"][0]
        io_i = iota[:, 0:ITEMS].unsqueeze(1).to_broadcast([P, 2, ITEMS])
        io_s = iota[:, 0:SLOTS].unsqueeze(1).to_broadcast([P, 2, SLOTS])
        for t in range(3):
            st(V.tensor_tensor(oh_s[:, t], io_s, ch_pos[:, t, :].unsqueeze(2).to_broadcast([P, 2, SLOTS]), ALU.is_equal))
            st(V.tensor_tensor(oh_i[:, t], io_i, item[:, t, :].unsqueeze(2).to_broadcast([P, 2, ITEMS]), ALU.is_equal))
        st.settle()
        for t in range(3):
            st(V.tensor_scalar(oh_i[:, t], oh_i[:, t], pack[:, t1 + t:t1 + t + 1], pack[:, va + t:va + t + 1], ALU.mult, ALU.mult), slots_ready)
        b, d = filled_of("slt")
        st(V.tensor_copy(slt[:], b[0:SLOTS, 0:2 * SLOTS].rearrange("p (a n) -> p a n", a=2)[:, :, 0:ITEMS]), slt_done)
        st.settle()
        st(V.tensor_scalar(slt2[:, 0, :], slt[:, 0, :], 0.0, SKIP, ALU.is_equal, ALU.mult))
        st(V.tensor_scalar(slt2[:, 1, :], slt[:, 1, :], 0.0, None, ALU.is_gt))
        st(V.tensor_scalar(slt[:, 0, :], slt[:, 0, :], -1.0, None, ALU.add))
        st.settle()
        st(V.tensor_tensor(slt[:, 0, :], slt[:, 0, :], slt2[:, 0, :], ALU.add))
        st.settle()
        st(V.tensor_copy(idx[:], slt[:, 0, :]))
        st(V.scalar_tensor_tensor(slt[:, 1, :], slt[:, 0, :], 2.0, slt2[:, 1, :], ALU.mult, ALU.add))
        st.settle()
        st(V.tensor_copy(row[:], slt[:, 1, :]))
        st(V.tensor_copy(exf[:, 0:NE], iota[0:1, 0:NE]))
        st(V.tensor_tensor(exm[:], cum[0:1, :].unsqueeze(1).to_broadcast([1, EXTRA, NE]),
                           iota[0:1, 0:EXTRA].unsqueeze(2).to_broadcast([1, EXTRA, NE]), ALU.is_le))
        st.settle()
        st(V.tensor_reduce(exf[:, NE:].unsqueeze(2), exm[:], AX.X, ALU.add))
        st.settle()
        st(V.tensor_scalar(exf[:, NE:], exf[:, NE:], float(NE - 1), None, ALU.min))
        st.settle()
        st(V.tensor_copy(exi[:], exf[:]))
        st(V.tensor_copy(nit[:], cum[0:1, NE - 1:NE]))
        st.settle()
        st(V.memset(stats[:, 0:1], 0.0), idx_ready)

        def item_lo(e, j):
            rs, ss = slot_of(j)
            dve.wait_ge(hi_done, sub(e, j) + 1)
            V.tensor_tensor(wlo[ss][:], raw[rs][:], whi[ss][:].bitcast(F32), ALU.subtract).then_inc(lo_done, 1)

        def x_low(e):
            dve.wait_ge(x_hi, e + 1)
            V.tensor_tensor(xT[:, :, SLOTS:], bank[4][:, :].rearrange("p (k c) -> p k c", k=KD),
                            xT[:, :, 0:SLOTS].bitcast(F32), ALU.subtract).then_inc(x_split, 1)

        def add_low(e, copied, dst, b, low, done):
            dve.wait_ge(copied, e + 1)
            V.tensor_tensor(dst[:], bank[b][0:SLOTS, :], low[:], ALU.add).then_inc(done, 1)

        def hidden(e):
            dve.wait_ge(silu_ok, e + 1)
            dve.wait_ge(u_drained, e + 1)
            V.tensor_tensor(hid[:], aA[:], uS[:], ALU.mult).then_inc(hid_ok, 1)

        def hidden_low(e):
            dve.wait_ge(hh_hi, e + 1)
            V.tensor_tensor(hdT[:, :, SLOTS:], bank[5][:, 0:4 * SLOTS].rearrange("p (k c) -> p k c", k=4),
                            hdT[:, :, 0:SLOTS].bitcast(F32), ALU.subtract).then_inc(hh_split, 1)

        def y_sum(e, written):
            if written:
                dve.wait_ge(y_written, e * 16)
            for j in range(2):
                dve.wait_ge(y_lo, 2 * e + j + 1)
                V.tensor_tensor(ySb[:, j, :], bank[2 + j][0:SLOTS, :], yLo[:, j, :], ALU.add).then_inc(y_drained, 1)

        x_low(0)
        for n in range(1, 4):
            lo(N0 + n)
        add_low(0, a_lo, aS, 0, aLo, a_drained)
        add_low(0, u_lo, uS, 1, uLo, u_drained)
        x_low(1)

        def item_steps(e, second, third):
            item_lo(e, 0)
            hidden(e - 1)
            item_lo(e, 1)
            if second:
                y_sum(e - 2, third)
            item_lo(e, 2)
            hidden_low(e - 1)
            item_lo(e, 3)
            add_low(e, a_lo, aS, 0, aLo, a_drained)
            item_lo(e, 4)
            item_lo(e, 5)
            add_low(e, u_lo, uS, 1, uLo, u_drained)
            x_low(e + 1)

        item_steps(1, False, False)
        item_steps(2, True, False)
        n_items = NE + dve.value_load(nit[0:1, 0:1], min_val=0, max_val=EXTRA - 1)
        with dve.Fori(3, n_items) as e:
            item_steps(e, True, True)
        item_lo(n_items, 0)
        hidden(n_items - 1)
        item_lo(n_items, 1)
        y_sum(n_items - 2, True)
        hidden_low(n_items - 1)
        y_sum(n_items - 1, True)
        dve.wait_ge(g2_ready, 2)
        dve.wait_ge(yg_in, 16 * 2)
        for t in range(3):
            rows = P if t < 2 else DEC
            ya, yb = yg[0:rows, t, 0, :], yg[0:rows, t, 1, :]
            g2 = g2p if t < 2 else g2s
            st(V.tensor_scalar(ya, ya, gates[0:rows, t, 0:1], None, ALU.mult))
            st.settle()
            st(V.scalar_tensor_tensor(ya, yb, gates[0:rows, t, 1:2], ya, ALU.mult, ALU.add))
            st.settle()
            st(V.tensor_tensor(ya, ya, g2[0:rows, :], ALU.mult))
            st.settle()
            st(V.scalar_tensor_tensor(x1[0:rows, t, :], x1[0:rows, t, :], ALPHA, ya, ALU.mult, ALU.add))
        st.settle()
        norm(fin_std, tail_in, l2w, l2b)
        dve.wait_ge(ln_std, 2)
        st(V.reciprocal(mv[:, :, 1], mv[:, :, 1]))
        st.settle()
        for t in range(3):
            rows = P if t < 2 else DEC
            xt = x1[0:rows, t, :]
            st(V.tensor_scalar(xt, xt, mv[0:rows, t, 0:1], mv[0:rows, t, 1:2], ALU.subtract, ALU.mult))
            st.settle()
            st(V.tensor_tensor(xt, xt, l2w[0:rows, :], ALU.mult))
            st.settle()
            st(V.tensor_tensor(xt, xt, l2b[0:rows, :], ALU.add), fin_ready)

    @block.tensor
    def _(pe):
        mm, tr = nc.tensor.matmul, nc.tensor.transpose

        def take(key):
            b, before, f, _ = use[key]
            if before is not None:
                pe.wait_ge(*before)
            return b, f[0]

        def dense(name, H, L):
            c = CI[name]
            for s in range(2):
                n = 2 * c + s
                pe.wait_ge(hi_done, n + 1)
                for t in range(3):
                    b = take((name, t))[0] if s == 0 else use[(name, t)][0]
                    cols = slice(P * t, P * t + P)
                    for kk in range(4):
                        k = 4 * s + kk
                        mm(b[:, :], H[:, k, cols], whi[n % NSPL][:, kk, :], start=(k == 0), stop=False)
                        if t < 2:
                            mm(b[:, :], L[:, k, cols], whi[n % NSPL][:, kk, :], start=False, stop=False)
                    if t == 0:
                        pe.wait_ge(lo_done, n + 1)
                    for kk in range(4):
                        last = mm(b[:, :], H[:, 4 * s + kk, cols], wlo[n % NSPL][:, kk, :], start=False,
                                  stop=(s == 1 and kk == 3))
                    if t == 2:
                        last.then_inc(used, 1)
                    elif s == 1:
                        last.then_inc(use[(name, t)][2][0], 1)

        def ada(j):
            c = CI[f"ada{j}"]
            b, _ = take((f"ada{j}", 0))
            for s in range(2):
                n = 2 * c + s
                pe.wait_ge(hi_done, n + 1)
                for kk in range(4):
                    mm(b[0:64, :], cst[:, 4 * s + kk, :], whi[n % NSPL][:, kk, :], start=(s == 0 and kk == 0), stop=False)
                pe.wait_ge(lo_done, n + 1)
                for kk in range(4):
                    last = mm(b[0:64, :], cst[:, 4 * s + kk, :], wlo[n % NSPL][:, kk, :], start=False,
                              stop=(s == 1 and kk == 3))
                last.then_inc(used, 1)

        def blocks_T(kind, src):
            for k in range(KD):
                b, f = take((kind, k))
                for t in range(3):
                    rows = P if t < 2 else DEC
                    last = tr(b[:, P * t:P * t + rows], src(t, rows, k), ident[0:rows, 0:rows])
                last.then_inc(f, 1)

        pe.wait_ge(pack_in, 16)
        pe.wait_ge(x_in, 32)
        blocks_T("xT", lambda t, rows, k: x_tok[0:rows, t, P * k:P * k + P])
        pe.wait_ge(c_silu, 1)
        b, f = take("cT")
        for k in range(KD):
            last = tr(b[:, 2 * k:2 * k + 2], cs2[:, P * k:P * k + P], ident[0:2, 0:2])
        last.then_inc(f, 1)
        pe.wait_ge(c_parts, 1)
        for j in range(5):
            ada(j)
        b, f = take("modT")
        pe.wait_ge(evacuated, 4)
        for a in range(2):
            for k in range(KD):
                q = a * KD + k
                last = tr(b[:, 2 * q:2 * q + 2], mod[:, P * q:P * q + P], ident[0:2, 0:2])
        last.then_inc(f, 1)
        for j in range(5, 12):
            ada(j)
        b, f = take("zf")
        pe.wait_ge(h_split, KD)
        pe.wait_ge(wf_l, 1)
        for k in range(KD):
            mm(b[0:FH, 0:T], wf_hi[:, k, :], actH[:, k, 0:T], start=(k == 0), stop=False)
            mm(b[0:FH, 0:T], wf_lo[:, k, :], actH[:, k, 0:T], start=False, stop=False)
            mm(b[0:FH, 0:SEQ], wf_hi[:, k, :], actL[:, k, :], start=False, stop=False)
            last = mm(b[0:FH, SEQ:T], wf_hi[:, k, :], actH[:, k, T:384], start=False, stop=(k == KD - 1))
        last.then_inc(f, 1)
        b, f = take("cfT")
        pe.wait_ge(cf_in, 16)
        tr(b[0:FH, 0:PAST], cf_tok[:], ident).then_inc(f, 1)
        dense("rq", actH, actL)
        dense("rk", actH, actL)
        b, f = take("ftok")
        pe.wait_ge(fs_ready, 1)
        idf = ident[0:FH, 0:FH]
        for t in range(3):
            tr(b[:, FH * t:FH * t + FH], fsT[:, P * t:P * t + P], idf)
        tr(b[0:DEC, 3 * FH:4 * FH], fsT[:, SEQ + PAST:T + PAST], idf)
        for t in range(2):
            tr(b[:, FH * (4 + t):FH * (5 + t)], lfT[:, P * t:P * t + P], idf)
        tr(b[0:DEC, 6 * FH:7 * FH], lfT[:, SEQ:T], idf).then_inc(f, 1)
        dense("rv0", actH, actL)
        dense("rv1", actH, actL)
        pe.wait_ge(rot_done, 3)
        for j in range(2 * RH):
            b, f = take(("qkT", j))
            for t in range(3):
                rows = P if t < 2 else DEC
                last = tr(b[:, P * t:P * t + rows], rot[0:rows, t, P * j:P * j + P], ident[0:rows, 0:rows])
            last.then_inc(f, 1)
        dense("rg0", actH, actL)
        dense("rg1", actH, actL)
        dense("ga0", actH, actL)
        pe.wait_ge(evacuated, CI["rv1"] + 1)
        pe.wait_ge(kdec_done, 3)
        pe.wait_ge(qd_done, 1)
        pe.wait_ge(dec_in, 32)
        S = slice(SEQ, T)
        for h in range(RH):
            b, f = take(("sc", h))
            mm(b[:, 0:SEQ], kT[:, h, 0:P], qT[:, h, 0:SEQ], start=True, stop=True)
            mm(b[:, SEQ:384], kT[:, h, P:SEQ], qT[:, h, P:SEQ], start=True, stop=True)
            mm(b[0:DEC, 384:448], kT[:, h, S], qT[:, h, S], start=True, stop=True).then_inc(f, 1)
            vs = slice(DV * h, DV * h + DV)
            bp, fp = take(("op", h))
            pe.wait_ge(*use[("sc", h)][3])
            mm(bp[:, 0:DV], sT[:, 0:P], rv[:, 0, vs], start=True, stop=True)
            mm(bp[:, DV:512], sT[:, P:SEQ], rv[:, 0, vs], start=True, stop=False)
            mm(bp[:, DV:512], sT[:, SEQ:384], rv[:, 1, vs], start=False, stop=True).then_inc(fp, 1)
            bs, fs = take(("os", h))
            ks = slice(512 + DK * h, 512 + DK * h + DK)
            mm(bs[0:DEC, 0:DV], sTs, rv[0:DEC, 2, vs], start=True, stop=False)
            mm(bs[0:DEC, 0:DV], qdT[:, h, :], s0[:, h, :], start=False, stop=True)
            mm(bs[:, DV:512], rot[:, 0, ks], rv[:, 0, vs], start=True, stop=False)
            mm(bs[:, DV:512], rot[:, 1, ks], rv[:, 1, vs], start=False, stop=True).then_inc(fs, 1)
            b2, f2 = take(("ss", h))
            mm(b2[:, 0:DV], rot[0:DEC, 2, ks], rv[0:DEC, 2, vs], start=True, stop=True).then_inc(f2, 1)
        for n in ("ga1", "fq0", "fq1", "fk0", "fk1"):
            dense(n, actH, actL)
        pe.wait_ge(ret_ready, 3)
        blocks_T("ret", lambda t, rows, k: o_ret[0:rows, t, P * k:P * k + P])

        def split_ready(kind):
            for k in range(KD):
                pe.wait_ge(*use[(kind, k)][3])

        split_ready("ret")
        dense("pr0", retH, retL)
        dense("pr1", retH, retL)
        dense("fv0", actH, actL)
        dense("fv1", actH, actL)
        pe.wait_ge(evacuated, CI["fv1"] + 1)
        for b in range(8):
            if b in fox_start:
                pe.wait_ge(*fox_start[b])
        with pe.Fori(0, FH) as h:
            pe.wait_ge(q_st, h + 1)
            for t in range(3):
                rows = P if t < 2 else DEC
                tr(bank[0][0:DH + 2, P * t:P * t + rows], qst[0:rows, t, :], ident[0:rows, 0:rows])
            pe.wait_ge(k_st, h + 1)
            for t in range(4):
                rows = P if t < 3 else DEC
                last = tr(bank[1][0:DH + 2, P * t:P * t + rows], kst[0:rows, t, :], ident[0:rows, 0:rows])
            last.then_inc(qk_tr, 1)
            pe.wait_ge(qT_cp, h + 1)
            pe.wait_ge(kT_cp, h + 1)
            mm(bank[2][:, 0:P], qTh[:, 0:P], kTh[:, 0:P], start=True, stop=False)
            mm(bank[2][:, 0:P], identb[:], causalb[:], start=False, stop=True)
            mm(bank[2][:, P:384], qTh[:, P:SEQ], kTh[:, 0:SEQ], start=True, stop=False)
            mm(bank[2][:, SEQ:384], identb[:], causalb[:], start=False, stop=True)
            mm(bank[3][0:DEC, 0:192], qTh[:, SEQ:T], kTh[:, SEQ:T + PAST], start=True, stop=False)
            mm(bank[3][0:DEC, P:192], identb[0:DEC, 0:DEC], causalb[0:DEC, 0:DEC], start=False, stop=True).then_inc(scored, 1)
            pe.wait_ge(exped, h + 1)
            tr(bank[4][:, 0:P], pr[:, 0, 0:P], ident)
            tr(bank[4][:, P:SEQ], pr[:, 1, 0:P], ident)
            tr(bank[6][:, 0:P], pr[:, 1, P:SEQ], ident)
            tr(bank[6][:, P:192], pr[0:DEC, 2, 0:P], ident[0:DEC, 0:DEC])
            tr(bank[6][0:DEC, 192:SEQ], pr[0:DEC, 2, P:192], ident[0:DEC, 0:DEC]).then_inc(p_tr, 1)
            pe.wait_ge(v_st, h + 1)
            pe.wait_ge(pT_a, h + 1)
            mm(bank[5][:, 0:DH], prT[:, 0:P], vst[:, 0, :], start=True, stop=True)
            mm(bank[5][:, DH:2 * DH], prT[:, P:SEQ], vst[:, 0, :], start=True, stop=False)
            pe.wait_ge(pT_d, h + 1)
            mm(bank[5][:, DH:2 * DH], prT[:, SEQ:384], vst[:, 1, :], start=False, stop=True)
            mm(bank[5][0:DEC, 2 * DH:3 * DH], prT[:, 384:448], vst[:, 2, :], start=True, stop=False)
            mm(bank[5][0:DEC, 2 * DH:3 * DH], prT[0:DEC, 448:512], vst[0:DEC, 3, :], start=False, stop=True).then_inc(pv_ok, 1)
        blocks_T("fox", lambda t, rows, k: fv[0:rows, t, P * k:P * k + P])
        dense("gb0", actH, actL)
        dense("gb1", actH, actL)
        split_ready("fox")
        dense("pf0", foxH, foxL)
        dense("pf1", foxH, foxL)
        pe.wait_ge(evacuated, CI["pf1"] + 1)
        blocks_T("mix", lambda t, rows, k: gate[0:rows, t, P * k:P * k + P])
        split_ready("mix")
        dense("wo0", mixH, mixL)
        dense("wo1", mixH, mixL)
        for t in range(3):
            rows = P if t < 2 else DEC
            pe.wait_ge(h2_ready, t + 1)
            for q in range(2):
                b, f = take(("h2T", t, q))
                if t:
                    pe.wait_ge(h2T_done, 2 * t - 1 + q)
                for kk in range(4):
                    last = tr(b[:, rows * kk:rows * kk + rows], h2[0:rows, t, P * (4 * q + kk):P * (4 * q + kk) + P], ident[0:rows, 0:rows])
                last.then_inc(f, 1)
        b, f = take("lgT")
        pe.wait_ge(wr_in, 64)
        pe.wait_ge(h2T_done, 6)
        for k in range(KD):
            last = mm(b[0:NG + NE, 0:T], wr[:, k, :], h2T[:, k, :], start=(k == 0), stop=(k == KD - 1))
        last.then_inc(f, 1)
        pe.wait_ge(*use["lgT"][3])
        b, f = take("lg")
        nr = NG + NE
        for t in range(3):
            rows = P if t < 2 else DEC
            last = tr(b[0:rows, nr * t:nr * t + nr], lgT[:, P * t:P * t + rows], ident[0:nr, 0:nr])
        last.then_inc(f, 1)
        pe.wait_ge(msk_done, 1)
        b, f = take("pos")
        for t in range(3):
            for u in range(t + 1):
                last = mm(b[:, NE * t:NE * t + NE], (befb if u == t else oneb)[:], msk[:, u, :], start=(u == 0), stop=(u == t))
        last.then_inc(f, 1)
        b, f = take("cnt")
        for t in range(3):
            last = mm(b[:, 0:NE], oneb[:], msk[:, t, :], start=(t == 0), stop=(t == 2))
        last.then_inc(f, 1)
        b, f = take("slt")
        pe.wait_ge(slots_ready, 3)
        for t in range(3):
            for ch in range(2):
                mm(b[0:SLOTS, 0:ITEMS], oh_s[:, t, ch, :], oh_i[:, t, ch, :], start=(t == 0 and ch == 0),
                   stop=(t == 2 and ch == 1))
        for t in range(3):
            last = mm(b[0:SLOTS, SLOTS:SLOTS + ITEMS], oh_s[:, t, 1, :], oh_i[:, t, 1, :], start=(t == 0), stop=(t == 2))
        last.then_inc(f, 1)

        def x_transpose(e):
            pe.wait_ge(x_landed, 16 * (e + 1))
            for k in range(KD):
                step = tr if k else mm
                last = step(bank[4][:, SLOTS * k:SLOTS * k + SLOTS], xg[:, P * k:P * k + P], ident[0:SLOTS, 0:SLOTS])
            last.then_inc(x_trans, 1)

        def product(n, ss, b, X, kof, first, final):
            pe.wait_ge(hi_done, n + 1)
            for kk in range(4):
                mm(bank[b][:, :], X[:, kof + kk, :], whi[ss][:, kk, :], start=(first and kk == 0), stop=False)
            pe.wait_ge(lo_done, n + 1)
            for kk in range(4):
                last = mm(bank[b][:, :], X[:, kof + kk, :], wlo[ss][:, kk, :], start=False, stop=(final and kk == 3))
            last.then_inc(used, 1)

        def hidden_T(e):
            pe.wait_ge(hid_ok, e + 1)
            for k in range(4):
                step = tr if k else mm
                last = step(bank[5][:, SLOTS * k:SLOTS * k + SLOTS], hid[:, P * k:P * k + P], ident[0:SLOTS, 0:SLOTS])
            last.then_inc(h_tr, 1)

        def out_product(e, n0_, j0):
            pe.wait_ge(hh_split, e + 1)
            for j in range(2):
                product(n0_ + j, slot_of(j0 + j)[1], 2 + j, hdT, 0, True, True)

        x_transpose(0)
        pe.wait_ge(x_split, 1)
        pe.wait_ge(slt_done, 1)
        for n in range(4):
            product(N0 + n, (N0 + n) % NSPL, n // 2, xT, 4 * (n % 2), n % 2 == 0, n % 2 == 1)
        x_transpose(1)

        def item_products(e, second):
            pe.wait_ge(x_split, e + 1)
            pe.wait_ge(a_drained, e)
            for j in range(2):
                product(sub(e, j), slot_of(j)[1], 0, xT, 4 * j, j == 0, j == 1)
            hidden_T(e - 1)
            pe.wait_ge(u_drained, e)
            for j in range(2):
                product(sub(e, 2 + j), slot_of(2 + j)[1], 1, xT, 4 * j, j == 0, j == 1)
            x_transpose(e + 1)
            if second:
                pe.wait_ge(y_drained, (e - 1) * 2)
            out_product(e - 1, sub(e, 4), 4)

        item_products(1, False)
        n_items = NE + pe.value_load(nit[0:1, 0:1], min_val=0, max_val=EXTRA - 1)
        with pe.Fori(2, n_items) as e:
            item_products(e, True)
        hidden_T(n_items - 1)
        pe.wait_ge(y_drained, (n_items - 1) * 2)
        out_product(n_items - 1, sub(n_items, 0), 0)

    ctx.close()


_INS = ["x_prompt", "x_sample", "state_ret", "cache_fox_k", "cache_fox_v", "cache_fox_logf", "c_prompt", "c_sample",
        "w_ada", "b_ada", "w_in", "b_in", "ret_gn_w", "ret_gn_b", "w_ret_proj", "w_fox_proj", "w_o", "ln1_w", "ln1_b",
        "w_rg", "b_rg", "w_re", "b_re", "w_e_in", "w_e_out", "ln2_w", "ln2_b"]
_OUTS = [("y_p", (1, SEQ, D)), ("y_s", (1, DEC, D)), ("p_s", (1, 1, RH, DK, DV)), ("p_k", (1, 1, SEQ, FH, DH)),
         ("p_v", (1, 1, SEQ, FH, DH)), ("p_f", (1, 1, SEQ, FH)), ("s_s", (1, 1, RH, DK, DV)),
         ("s_k", (1, 1, DEC, FH, DH)), ("s_v", (1, 1, DEC, FH, DH)), ("s_f", (1, 1, DEC, FH))]


def kernel(**inputs):
    import concourse.bacc as bacc
    from concourse.bass_utils import run_bass_kernel_spmd

    nc = bacc.Bacc("TRN2", target_bir_lowering=False, num_devices=1)
    arrays = {n: np.ascontiguousarray(inputs[n]) for n in _INS}
    arrays["pack"], arrays["decay"] = shape_tables()
    ins = {n: nc.dram_tensor(f"in_{n}", a.shape, mybir.dt.from_np(a.dtype), kind="ExternalInput").ap() for n, a in arrays.items()}
    outs = {n: nc.dram_tensor(f"out_{n}", s, F32, kind="ExternalOutput").ap() for n, s in _OUTS}
    scratch = {n: nc.dram_tensor(f"scratch_{n}", s, F32, kind="Internal").ap()
               for n, s in (("mod", (2, 6 * D)), ("h2", (T, D)), ("y", (2 * T, D)))}
    build_layer(nc, ins, outs, scratch)
    r = run_bass_kernel_spmd(nc, [{f"in_{n}": a for n, a in arrays.items()}], core_ids=[0])
    return tuple(r.results[0][f"out_{n}"] for n, _ in _OUTS)
```

```python
import math
from contextlib import ExitStack

import numpy as np

import concourse.bass as bass
from concourse import mybir

F32 = mybir.dt.float32
F32R = mybir.dt.float32r
BF16 = mybir.dt.bfloat16
I32 = mybir.dt.int32
U32 = mybir.dt.uint32
ALU = mybir.AluOpType
ACT = mybir.ActivationFunctionType
AX = mybir.AxisListType

D = 1024
SEQ, DEC, PAST = 256, 64, 128
T = SEQ + DEC
P = 128
KD = D // P
RH, DK, DV = 4, 128, 256
FH, DH = 16, 64
NG, EG, NE = 4, 8, 32
FE = 512
FGATE = 2 * RH * DK + 2 * RH * DV + 3 * FH * DH
NIN = FGATE + FH + 2 * D
ALPHA = 2.0 ** 0.25
LN_EPS, GN_EPS = 1e-5, 1e-6
SLOTS = 64
EXTRA = 2 * T // SLOTS
ITEMS = NE + EXTRA
SKIP = 1.0e6
NEG = -3.0e38

PACK = {}
_at = 0
for _name, _w in (("ident", P), ("causal", P), ("before", P), ("rot", 3 * 2 * 64), ("qdec", RH * 64),
                  ("kdec", 3 * RH), ("iota", SLOTS), ("tok1", 3), ("valid", 3), ("multiples", 4)):
    PACK[_name] = (_at, _at + _w)
    _at += _w
PACK_W = _at


def log_gamma():
    return np.log1p(-np.exp(np.linspace(math.log(1.0 / 32), math.log(1.0 / 512), RH, dtype=np.float32))).astype(np.float64)


def shape_tables():
    pack = np.zeros((P, PACK_W), np.float32)

    def put(name, value):
        a, b = PACK[name]
        pack[:, a:b] = np.asarray(value, np.float32).reshape(P, b - a)

    p = np.arange(P)
    put("ident", np.eye(P))
    put("causal", np.where(p[:, None] >= p[None, :], 0.0, NEG))
    put("before", p[:, None] < p[None, :])
    half = DK // 2
    inv = np.float32(10000.0) ** (-np.linspace(0.0, 1.0, half, dtype=np.float32))
    pos = np.stack([p, P + p, PAST + p], 1).astype(np.float32)
    ang = (pos[:, :, None] * inv[None, None, :]).astype(np.float32).astype(np.float64)
    put("rot", np.stack([np.cos(ang), np.sin(ang)], 2))
    g = log_gamma()
    put("qdec", np.broadcast_to(np.exp((np.arange(DEC) + 1.0)[None, :] * g[:, None])[None], (P, RH, DEC)))
    back = np.stack([SEQ - 1 - p, SEQ - 1 - P - p, DEC - 1 - np.minimum(p, DEC - 1)], 1)
    put("kdec", np.exp(back[:, :, None] * g[None, None, :]) * DK ** -0.5)
    put("iota", np.broadcast_to(np.arange(SLOTS), (P, SLOTS)))
    put("tok1", np.stack([1 + p, 1 + P + p, 1 + SEQ + p], 1))
    put("multiples", np.broadcast_to(SLOTS * np.arange(1, 5), (P, 4)))
    put("valid", np.stack([p >= 0, p >= 0, p < DEC], 1))
    n = np.arange(SEQ)[None, :] - p[:, None]
    decay = np.where(n[:, None] >= 0, np.exp(np.maximum(n, 0)[:, None] * g[None, :, None]), 0.0) * DK ** -0.5
    return pack, decay.astype(np.float32)


class Steps:

    def __init__(self, eng, own):
        self.eng, self.own, self.count, self.last = eng, own, {}, None

    def __call__(self, ins, sem=None):
        if isinstance(sem, tuple):
            ins.then_inc(sem[0], 1)
            self.last = sem
            return
        sem = self.own if sem is None else sem
        ins.then_inc(sem, 1)
        self.count[sem.name] = self.count.get(sem.name, 0) + 1
        self.last = (sem, self.count[sem.name])

    def settle(self):
        self.eng.wait_ge(*self.last)


def build_layer(nc, i, o, scratch):
    ctx = ExitStack()
    base = 16512
    off = {"next": base}

    def fixed(name, shape, dt):
        size = int(np.prod(shape[1:])) * (2 if dt == BF16 else 4)
        t = nc.alloc_sbuf_tensor_at(name, shape, dt, offset=off["next"])
        off["next"] += (size + 31) // 32 * 32
        return t

    NRAW, NSPL = 6, 3
    raw = [fixed(f"w_raw{s}", [P, 4, 512], F32) for s in range(NRAW)]
    whi = [fixed(f"w_hi{s}", [P, 4, 512], F32R) for s in range(NSPL)]
    wlo = [fixed(f"w_lo{s}", [P, 4, 512], F32R) for s in range(NSPL)]
    pack = fixed("pack", [P, PACK_W], F32)
    identb = fixed("identb", [P, P], BF16)
    causalb = fixed("causalb", [P, P], BF16)
    bias = fixed("bias_rows", [P, 2, 512], F32)
    low_s = fixed("low_sum", [DEC, 512], F32)
    f_tok = fixed("forget_sums", [P, 4, FH], F32)
    lf_tok = fixed("log_forgets", [P, 3, FH], F32)
    PH = off["next"]
    END = 229368

    def at(name, shape, dt, offset):
        size = int(np.prod(shape[1:])) * (2 if dt == BF16 else 4)
        assert PH + offset + size <= END, (name, PH, offset, size)
        return nc.alloc_sbuf_tensor_at(name, shape, dt, offset=PH + offset)

    def const(name, rows=P):
        a, b = PACK[name]
        return pack[0:rows, a:b]

    ident = const("ident")
    actH = at("h_hi", [P, KD, 384], F32R, 0)
    actL = at("h_lo", [P, KD, 256], F32R, 12288)
    gate = at("gate", [P, 3, D], F32, 20480)
    rqk = at("ret_qk", [P, 3, D], F32, 32768)
    o_ret = at("o_ret", [P, 3, D], F32, 32768)
    rg = at("ret_gate", [P, 3, D], F32, 45056)
    rot = at("ret_rot", [P, 3, D], F32, 65536)
    rv = at("ret_v", [P, 3, D], F32, 77824)
    decay = at("decay", [P, RH, SEQ], F32, 57344)
    s0 = at("state_in", [P, RH, DV], F32, 61440)
    gnw = at("gn_w", [P, D], F32, 57344)
    gnb = at("gn_b", [P, D], F32, 61440)
    qT = at("ret_qT", [P, RH, T], F32, 90112)
    kT = at("ret_kT", [P, RH, T], F32, 95232)
    qdT = at("ret_qdT", [P, RH, DEC], F32, 100352)
    sT = at("ret_sT", [P, 384], F32, 101376)
    small = PACK["rot"][0]
    stats = pack[:, small:small + 192]
    sTs = pack[0:DEC, small + 192:small + 256]
    rot_t = at("rot_tmp", [P, 2, 512], F32, 20480)
    retH = at("ret_hi", [P, KD, 384], F32R, 45056)
    retL = at("ret_lo", [P, KD, 256], F32R, 57344)
    x_tok = at("x_tok", [P, 3, D], F32, 32768)
    hT = at("hT", [P, KD, T], F32, 45056)
    cst = at("c_parts", [P, KD, 64], F32R, 57344)
    c2 = at("c_rows", [2, D], F32, 90112)
    cs2 = at("c_silu", [2, D], F32, 94208)
    mod = at("mod_rows", [2, 2 * D], F32, 65536)
    mrow = at("mod_chunk_rows", [2, 2, 512], F32, 61440)
    modT = at("mod_cols", [P, 2, KD, 2], F32, 59392)
    wf_raw = at("wf_raw", [P, KD, FH], F32, 90112)
    wf_hi = at("wf_hi", [P, KD, FH], F32R, 90624)
    wf_lo = at("wf_lo", [P, KD, FH], F32R, 91136)
    zf = at("zf", [FH, T], F32, 91648)
    za = at("zf_abs", [FH, T], F32, 92928)
    zl = at("zf_log", [FH, T], F32, 94208)
    lfT = at("lfT", [FH, T], F32, 95488)
    fsT = at("fsT", [FH, T + PAST], F32, 96768)
    onesT = at("onesT", [FH, T], F32, 98560)
    cf_tok = at("cache_lf", [P, FH], F32, 99840)
    cfT = at("cache_lfT", [FH, PAST], F32, 99904)
    bf_col = at("b_f", [FH, 1], F32, 100416)
    kaug = at("fox_k", [P, 4, FH, DH + 2], F32, 65536)
    qaug = at("fox_q", [P, 3, FH, DH + 2], F32, 82432)
    fv = at("fox_v", [P, 4, D], F32, 32768)
    qst = at("q_head", [P, 3, DH + 2], F32, 49152)
    kst = at("k_head", [P, 4, DH + 2], F32, 49152 + 800)
    vst = at("v_head", [P, 4, DH], F32, 49152 + 1888)
    qTh = at("qT_head", [DH + 2, T], F32, 49152 + 2912)
    kTh = at("kT_head", [DH + 2, T + PAST], F32, 49152 + 4192)
    pr = at("probs", [P, 3, SEQ], F32, 49152 + 5984)
    prT = at("probsT", [P, 512], F32, 49152 + 9056)
    nmax = at("neg_max", [P, 3], F32, 49152 + 11104)
    psums = at("prob_sums", [P, 3], F32, 49152 + 11136)
    pinv = at("prob_inv", [P, 3], F32, 49152 + 11168)
    fox_o = [at("fox_out0", [P, D], F32, 60416)[:], at("fox_out1", [P, D], F32, 95232)[:], fv[:, 2, :]]
    foxH = at("fox_hi", [P, KD, 384], F32R, 49152)
    foxL = at("fox_lo", [P, KD, 256], F32R, 65536)
    gate_b = at("gate_b", [P, 3, D], F32, 82432)
    mixH = at("mix_hi", [P, KD, 384], F32R, 82432)
    mixL = at("mix_lo", [P, KD, 256], F32R, 94720)
    x1 = at("x1", [P, 3, D], F32, 32768)
    xres = at("x_again", [P, 3, D], F32, 45056)
    h2 = at("h2", [P, 3, D], F32, 45056)
    g1p = at("g1_prompt", [P, D], F32, 57344)
    g1s = at("g1_sample", [DEC, D], F32, 61440)
    l1w = at("ln1_w", [P, D], F32, 65536)
    l1b = at("ln1_b", [P, D], F32, 69632)
    m2p = at("mod2_prompt", [P, 2, D], F32, 0)
    m2s = at("mod2_sample", [DEC, 2, D], F32, 8192)
    g1x = at("affine_tmp", [P, D], F32, 16384)
    h2T = at("h2T", [P, KD, T], F32, 73728)
    R0 = 20480
    ro = {"n": R0}

    def rt(name, shape, dt=F32):
        t = at(name, shape, dt, ro["n"])
        ro["n"] += (int(np.prod(shape[1:])) * (2 if dt == BF16 else 4) + 31) // 32 * 32
        assert ro["n"] <= 32768
        return t

    wr = rt("w_router", [P, KD, NG + NE])
    br = rt("b_router", [P, NG + NE])
    lg = rt("logits", [P, 3, NG + NE])
    g8 = rt("group8", [P, 3, 8])
    gmx = rt("group_max", [P, 3, 8])
    gix = rt("group_ix", [P, 3, 8], U32)
    gid = rt("group_id", [P, 3, 1])
    gex = rt("group_exp", [P, 3, NG])
    gpr = rt("group_p", [P, 3, 1])
    goh = rt("group_onehot", [P, 3, NG])
    el = rt("expert_logits", [P, 3, EG])
    emx = rt("expert_max", [P, 3, 8])
    eix = rt("expert_ix", [P, 3, 8], U32)
    eid = rt("expert_id", [P, 3, 2])
    gates = rt("gates", [P, 3, 2])
    ga_t = rt("gates_tmp", [P, 3, 2])
    oh = rt("expert_onehot", [P, 3, 2, NE])
    oht = rt("onehot_tmp", [P, 3, 2, NE])
    msk = rt("expert_mask", [P, 3, NE], BF16)
    befb = rt("before_b", [P, P], BF16)
    oneb = rt("ones_b", [P, P], BF16)
    pos = rt("positions", [P, 3, NE])
    cnt = rt("counts", [P, NE])
    ext = rt("extra_items", [P, NE])
    one32 = rt("ones32", [P, NE])
    cum = rt("extra_cum", [P, NE])
    exc = rt("extra_before", [P, NE])
    ch_pos = rt("choice_pos", [P, 3, 2])
    ch_exc = rt("choice_before", [P, 3, 2])
    ch_q = rt("choice_q", [P, 3, 2])
    ch_t = rt("choice_tmp", [P, 3, 2])
    item = rt("choice_item", [P, 3, 2])
    slt = rt("slot_tokens", [SLOTS, 2, ITEMS])
    slt2 = rt("slot_tmp", [SLOTS, 2, ITEMS])
    idx = rt("slot_token", [SLOTS, ITEMS], I32)
    idx1 = rt("slot_token_now", [SLOTS, 1], I32)
    row = rt("slot_row", [SLOTS, ITEMS], I32)
    row1 = rt("slot_row_now", [SLOTS, 1], I32)
    exm = rt("item_expert_cmp", [1, EXTRA, NE])
    exf = rt("item_expert_f", [1, ITEMS])
    exi = rt("item_expert", [1, ITEMS], I32)
    nit = rt("n_extra", [1, 1], I32)
    turn = rt("turn", [1, 2])
    st1 = pack[:, small + 256:small + 292].rearrange("p (t q s) -> p t q s", t=3, q=2)
    elx = rt("expert_masked", [P, 3, NG, EG])
    cnx = rt("count_cmp", [P, NE, 4])
    chx = rt("choice_cmp", [P, 6, 4])
    mv = rt("ln_mean_var", [P, 3, 2])
    oh_s = at("slot_onehot", [P, 3, 2, SLOTS], F32, 57344)
    oh_i = at("item_onehot", [P, 3, 2, ITEMS], F32, 57344 + 1536)
    xg = at("x_item", [SLOTS, D], F32, 0)
    xT = at("xT_item", [P, KD, 2 * SLOTS], F32R, 4096)
    aLo = at("a_low", [SLOTS, FE], F32, 8192)
    uLo = at("u_low", [SLOTS, FE], F32, 10240)
    aS = at("a_sum", [SLOTS, FE], F32, 12288)
    aA = at("a_silu", [SLOTS, FE], F32, 14336)
    uS = at("u_sum", [SLOTS, FE], F32, 16384)
    hid = at("hidden", [SLOTS, FE], F32, 18432)
    hdT = at("hiddenT", [P, 4, 2 * SLOTS], F32R, 45056)
    yLo = at("y_low", [SLOTS, 2, 512], F32, 47104)
    ySb = at("y_item", [SLOTS, 2, 512], F32, 51200)
    yg = at("y_choice", [P, 3, 2, D], F32, 57344)
    g2p = at("g2_prompt", [P, D], F32, 81920)
    g2s = at("g2_sample", [DEC, D], F32, 86016)
    l2w = at("ln2_w", [P, D], F32, 90112)
    l2b = at("ln2_b", [P, D], F32, 94208)

    bank = [ctx.enter_context(nc.psum_tensor(f"bank{b}", [P, 512], F32)) for b in range(8)]

    def sem(name):
        return ctx.enter_context(nc.semaphore(name))

    raw_landed = [sem(f"raw_landed{s}") for s in range(NRAW)]
    hi_done, lo_done, used = sem("hi_done"), sem("lo_done"), sem("stream_used")
    filled = [sem(f"bank_filled{b}") for b in range(8)]
    drained = [sem(f"bank_drained{b}") for b in range(8)]
    evacuated = sem("chunk_evacuated")
    bias_landed = [sem("bias_landed0"), sem("bias_landed1")]
    own_act, own_dve, own_pool = sem("own_act"), sem("own_dve"), sem("own_pool")
    pack_in, x_in, c_in, modb_in, wf_in, cf_in = (sem(n) for n in ("pack_in", "x_in", "c_in", "modb_in", "wf_in", "cf_in"))
    consts_ready, c_silu, c_hi, c_parts = sem("consts_ready"), sem("c_silu"), sem("c_hi"), sem("c_parts")
    h_ready, h_hi, h_split = sem("h_ready"), sem("h_hi"), sem("h_split")
    mod_out = [sem("mod_out0"), sem("mod_out1")]
    mrow_in = [sem("mod_bias_in0"), sem("mod_bias_in1")]
    wf_h, wf_l, zf_done, zf_act, lf_ready, fs_ready, ftok_done = (
        sem(n) for n in ("wf_h", "wf_l", "zf_done", "zf_act", "lf_ready", "fs_ready", "ftok_done"))
    rot_done, kdec_done, qkT_done, qd_done = sem("rot_done"), sem("kdec_done"), sem("qkT_done"), sem("qd_done")
    dec_in, oret_act, state_done, ret_out = sem("dec_in"), sem("oret_act"), sem("state_done"), sem("ret_out")
    gact, gn_in, gn_var, gn_std, ret_ready = sem("gate_act"), sem("gn_in"), sem("gn_var"), sem("gn_std"), sem("ret_ready")
    ts_hi, r_fox = sem("split_hi"), sem("prob_inverse")
    cachek_in, cachev_in, aug_ready, fox_out = sem("cachek_in"), sem("cachev_in"), sem("aug_ready"), sem("fox_out")
    q_st, k_st, v_st, qk_tr, qT_cp, kT_cp, scored, maxed, exped, p_tr, pT_a, pT_d, pv_ok, o_ok = (
        sem(n) for n in ("q_staged", "k_staged", "v_staged", "qk_transposed", "qT_copied", "kT_copied", "scored",
                         "maxed", "exped", "p_transposed", "pT_copied_a", "pT_copied_d", "pv_done", "o_done"))
    res_in, ln_in, ln_var, ln_std, h2_ready, h2_out, h2T_done = (
        sem(n) for n in ("res_in", "ln_in", "ln_var", "ln_std", "h2_ready", "h2_out", "h2T_done"))
    m2_in, m2_ready, wr_in, r_dve, r_act, msk_done, slots_ready, slt_done, idx_ready = (
        sem(n) for n in ("m2_in", "m2_ready", "wr_in", "r_dve", "r_act", "mask_done",
                         "slots_ready", "slt_done", "idx_ready"))
    nb_ready, xn_ready = sem("shift_ready"), sem("normalised")
    row_cp, x_norm, x1_ready, nit_ready = sem("row_copied"), sem("x_normalised"), sem("x1_ready"), sem("items_counted")
    idx_cp, x_landed, x_trans, x_hi, x_split, a_lo, u_lo, a_drained, u_drained, silu_ok, hid_ok = (
        sem(n) for n in ("idx_copied", "x_landed", "x_transposed", "x_hi", "x_split", "a_low_copied",
                         "u_low_copied", "a_drained", "u_drained", "silu_done", "hidden_done"))
    h_tr, hh_hi, hh_split, y_lo, y_drained, y_written, fills_done = (
        sem(n) for n in ("hidden_transposed", "hidden_hi", "hidden_split", "y_low_copied", "y_drained", "y_written", "fills_done"))
    yg_in = [sem(f"y_rows_in{t}") for t in range(3)]
    tail_in, comb, fin_std, fin_ready, y_out = (
        sem(n) for n in ("tail_in", "comb", "fin_std", "fin_ready", "y_out"))

    CH = ["ada0", "ada1", "ada2", "ada3", "ada4", "ada5", "ada6", "rq", "ada7", "ada8", "rk", "ada9", "ada10", "rv0",
          "ada11", "rv1", "rg0", "rg1", "ga0", "ga1", "fq0", "fq1", "fk0", "fk1", "pr0", "pr1", "fv0", "fv1",
          "gb0", "gb1", "pf0", "pf1", "wo0", "wo1"]
    CI = {n: c for c, n in enumerate(CH)}
    zcol = {}
    for n, c0 in (("rq", 0), ("rk", 512), ("rv", 1024), ("rg", 2048), ("fq", 3072), ("fk", 4096), ("fv", 5120),
                  ("ga", FGATE + FH), ("gb", FGATE + FH + D)):
        if n in ("rq", "rk"):
            zcol[n] = c0
        else:
            zcol[n + "0"], zcol[n + "1"] = c0, c0 + 512
    ZCH = [n for n in CH if n in zcol]
    N0 = 2 * len(CH)

    use, free_at, fills, drains = {}, {}, [0] * 8, [0] * 8

    def plan(key, b, filled_at=None, drained_at=None):
        before = free_at.get(b)
        if filled_at is None:
            fills[b] += 1
            filled_at = (filled[b], fills[b])
        if drained_at is None:
            drains[b] += 1
            drained_at = (drained[b], drains[b])
        use[key] = (bank[b], before, filled_at, drained_at)
        free_at[b] = drained_at

    def dense_banks(c):
        return (0, 1, 2) if c % 2 == 0 else (3, 4, 5)

    def plan_dense(n):
        c = CI[n]
        b = dense_banks(c)
        if n.startswith("ada"):
            plan((n, 0), b[0], (used, 2 * c + 2), (evacuated, c + 1))
            return
        plan((n, 0), b[0])
        plan((n, 1), b[1])
        plan((n, 2), b[2], (used, 2 * c + 2), (evacuated, c + 1))

    def spare(after):
        return tuple(dense_banks(CI[after] + 1)) + (6, 7)

    plan("cT", 6, drained_at=(c_parts, 1))
    plan_dense("ada0")
    plan_dense("ada1")
    for k in range(KD):
        plan(("xT", k), (1, 2, 4, 5, 7)[k % 5])
    plan_dense("ada2")
    plan_dense("ada3")
    plan("modT", 7)
    plan_dense("ada4")
    plan_dense("ada5")
    plan_dense("ada6")
    plan("zf", 6)
    plan("cfT", 7)
    for n in ("rq", "ada7", "ada8"):
        plan_dense(n)
    plan("ftok", 6, drained_at=(ftok_done, 2))
    for n in ("rk", "ada9", "ada10", "rv0", "ada11", "rv1"):
        plan_dense(n)
    for j in range(2 * RH):
        plan(("qkT", j), spare("rv1")[j % 5], drained_at=(qkT_done, j + 1))
    for n in ("rg0", "rg1", "ga0"):
        plan_dense(n)
    for h in range(RH):
        s = spare("ga0")
        plan(("sc", h), s[3 + h % 2])
        plan(("op", h), s[0])
        plan(("os", h), s[1], drained_at=(state_done, 2 * h + 1))
        plan(("ss", h), s[2], drained_at=(state_done, 2 * h + 2))
    for n in ("ga1", "fq0", "fq1", "fk0", "fk1"):
        plan_dense(n)
    for k in range(KD):
        plan(("ret", k), spare("fk1")[k % 5])
    for n in ("pr0", "pr1", "fv0", "fv1"):
        plan_dense(n)
    fox_start = dict(free_at)
    for b in range(8):
        free_at[b] = (o_ok, FH)
    for k in range(KD):
        plan(("fox", k), k)
    for n in ("gb0", "gb1", "pf0", "pf1"):
        plan_dense(n)
    for k in range(KD):
        plan(("mix", k), spare("pf1")[k % 5])
    for n in ("wo0", "wo1"):
        plan_dense(n)
    for t in range(3):
        for q in range(2):
            plan(("h2T", t, q), (6, 7)[q], drained_at=(h2T_done, 2 * t + q + 1))
    plan("lg", 3)
    plan("pos", 6)
    plan("cnt", 7)
    plan("slt", 0, drained_at=(slt_done, 1))

    block = ctx.enter_context(nc.Block())

    def weight_source(n):
        if n.startswith("ada"):
            w, c0 = i["w_ada"][0], 512 * int(n[3:])
        elif n in zcol:
            w, c0 = i["w_in"][0], zcol[n]
        else:
            w, c0 = i[{"pr": "w_ret_proj", "pf": "w_fox_proj", "wo": "w_o"}[n[:2]]][0], 512 * int(n[2])
        return w.rearrange("(k p) n -> p k n", p=P)[:, :, c0:c0 + 512]

    def bcast(ap1d, rows):
        return ap1d.partition_broadcast(rows)

    w_in_e = i["w_e_in"][0].rearrange("e (k p) n -> e p k n", p=P)
    w_out_e = i["w_e_out"][0].rearrange("e (k p) n -> e p k n", p=P)
    E0 = N0 + 4

    def sub(e, j):
        return E0 + 6 * (e - 1) + j

    def slot_of(j):
        return (E0 + j) % NRAW, (E0 + j) % NSPL

    @block.sync
    def _(sp):
        sp.dma_start(c2[0:1, :], i["c_prompt"][0:1, :]).then_inc(c_in, 16)
        sp.dma_start(c2[1:2, :], i["c_sample"][0:1, :]).then_inc(c_in, 16)
        sp.dma_start(pack[:], i["pack"][:, :]).then_inc(pack_in, 16)
        sp.dma_start(mod[:, :], bcast(i["b_ada"][0, 0:2 * D], 2)).then_inc(modb_in, 16)

        def send(n, src):
            if n >= NRAW:
                sp.wait_ge(lo_done, n - NRAW + 1)
            sp.dma_start(raw[n % NRAW][:], src).then_inc(raw_landed[n % NRAW], 16)

        for c, name in enumerate(CH):
            src = weight_source(name)
            if name in zcol:
                m = ZCH.index(name)
                if m >= 2:
                    sp.wait_ge(evacuated, CI[ZCH[m - 2]] + 1)
                sp.dma_start(bias[:, m % 2, :], bcast(i["b_in"][0, zcol[name]:zcol[name] + 512], P)).then_inc(bias_landed[m % 2], 16)
            for s in range(2):
                send(2 * c + s, src[:, 4 * s:4 * s + 4, :])
            if name == "ada0":
                sp.dma_start(x_tok[:, 0:2, :], i["x_prompt"][0].rearrange("(t p) d -> p t d", p=P)).then_inc(x_in, 16)
                sp.dma_start(x_tok[0:DEC, 2, :], i["x_sample"][0]).then_inc(x_in, 16)
            if name == "ada3":
                sp.wait_ge(c_hi, 1)
                sp.wait_ge(c_parts, 1)
                sp.dma_start(wf_raw[:], i["w_in"][0].rearrange("(k p) n -> p k n", p=P)[:, :, FGATE:FGATE + FH]).then_inc(wf_in, 16)
                sp.dma_start(cf_tok[:], i["cache_fox_logf"][0, 0]).then_inc(cf_in, 16)
                sp.dma_start(bf_col[:], i["b_in"][0, FGATE:FGATE + FH].rearrange("(p a) -> p a", a=1)).then_inc(wf_in, 16)
        for n in range(4):
            send(N0 + n, w_in_e[0, :, 4 * (n % 2):4 * (n % 2) + 4, 512 * (n // 2):512 * (n // 2) + 512])

        def item_weights(e, expert, before):
            for j in range(6):
                src = (w_in_e[expert, :, 4 * (j % 2):4 * (j % 2) + 4, 512 * (j // 2):512 * (j // 2) + 512] if j < 4
                       else w_out_e[before, :, :, 512 * (j - 4):512 * (j - 4) + 512])
                if not isinstance(e, int):
                    src = src.rearrange("e p k n -> (e p) k n")
                sp.wait_ge(lo_done, sub(e, j) - NRAW + 1)
                sp.dma_start(raw[slot_of(j)[0]][:], src).then_inc(raw_landed[slot_of(j)[0]], 16)

        item_weights(1, 1, 0)
        with sp.Fori(2, NE) as e:
            item_weights(e, bass.ds(e, 1), bass.ds(e - 1, 1))
        sp.wait_ge(nit_ready, 1)
        items = NE + sp.value_load(nit[0:1, 0:1], min_val=0, max_val=EXTRA - 1)
        with sp.If(items > NE):
            with sp.Fori(NE, items) as e:
                ex = sp.value_load(exi[0:1, bass.ds(e, 1)], min_val=0, max_val=NE - 1)
                bf = sp.value_load(exi[0:1, bass.ds(e - 1, 1)], min_val=0, max_val=NE - 1)
                item_weights(e, bass.ds(ex, 1), bass.ds(bf, 1))
        last = sp.value_load(exi[0:1, bass.ds(items - 1, 1)], min_val=0, max_val=NE - 1)
        for j in range(2):
            sp.wait_ge(lo_done, sub(items, j) - NRAW + 1)
            sp.dma_start(raw[slot_of(j)[0]][:],
                         w_out_e[bass.ds(last, 1), :, :, 512 * j:512 * j + 512].rearrange("e p k n -> (e p) k n")
                         ).then_inc(raw_landed[slot_of(j)[0]], 16)
        y3 = scratch["y"].rearrange("(t c) d -> t c d", c=2)
        sp.wait_ge(y_written, items * 16)
        for t in range(2):
            sp.dma_start(yg[:, t, :, :], y3[P * t:P * t + P]).then_inc(yg_in[t], 16)
        sp.dma_start(yg[0:DEC, 2, :, :], y3[SEQ:T]).then_inc(yg_in[2], 16)
        for t in range(2):
            sp.wait_ge(fin_ready, t + 1)
            sp.dma_start(o["y_p"][0][P * t:P * t + P, :], x1[:, t, :]).then_inc(y_out, 16)
        sp.wait_ge(fin_ready, 3)
        sp.dma_start(o["y_s"][0], x1[0:DEC, 2, :]).then_inc(y_out, 16)
        sp.wait_ge(ret_out, 32)
        sp.wait_ge(fox_out, 16 * 6)
        sp.wait_ge(y_out, 48)

    @block.gpsimd
    def _(pool):
        st = Steps(pool, own_pool)
        nc.gpsimd.memset(cst[:].bitcast(F32), 0.0).then_inc(fills_done, 1)
        nc.gpsimd.memset(onesT[:], 1.0).then_inc(fills_done, 1)
        def mod_bias(j):
            pool.dma_start(mrow[:, j % 2, :], bcast(i["b_ada"][0, 512 * j:512 * j + 512], 2)).then_inc(mrow_in[j % 2], 16)

        rr = const("rot").rearrange("p (t f c) -> p t f c", t=3, f=2)

        def rotary(t):
            rows = P if t < 2 else DEC
            src = rqk[0:rows, t, :].rearrange("p (h a c) -> p h a c", h=2 * RH, a=2)
            out = rot[0:rows, t, :].rearrange("p (h a c) -> p h a c", h=2 * RH, a=2)
            tmp = rot_t[0:rows, :, :].rearrange("p a (h c) -> p a h c", h=2 * RH)
            cos = rr[0:rows, t, 0, :].unsqueeze(1).to_broadcast([rows, 2 * RH, 64])
            sin = rr[0:rows, t, 1, :].unsqueeze(1).to_broadcast([rows, 2 * RH, 64])
            pool.wait_ge(evacuated, CI["rk"] + 1)
            st(nc.gpsimd.tensor_tensor(out[:, :, 0, :], src[:, :, 0, :], cos, ALU.mult))
            st(nc.gpsimd.tensor_tensor(tmp[:, 0], src[:, :, 1, :], sin, ALU.mult))
            st(nc.gpsimd.tensor_tensor(out[:, :, 1, :], src[:, :, 0, :], sin, ALU.mult))
            st(nc.gpsimd.tensor_tensor(tmp[:, 1], src[:, :, 1, :], cos, ALU.mult))
            st.settle()
            st(nc.gpsimd.tensor_tensor(out[:, :, 0, :], out[:, :, 0, :], tmp[:, 0], ALU.subtract))
            st(nc.gpsimd.tensor_tensor(out[:, :, 1, :], out[:, :, 1, :], tmp[:, 1], ALU.add), rot_done)
            st.settle()

        mod_bias(4)
        mod_bias(5)
        for k in range(KD):
            pool.wait_ge(h_hi, k + 1)
            st(nc.gpsimd.tensor_tensor(actL[:, k, :], hT[:, k, 0:SEQ], actH[:, k, 0:SEQ].bitcast(F32), ALU.subtract))
            st(nc.gpsimd.tensor_tensor(actH[:, k, T:384], hT[:, k, SEQ:T], actH[:, k, SEQ:T].bitcast(F32), ALU.subtract), h_split)
        for j in range(4, 12):
            pool.wait_ge(evacuated, CI[f"ada{j}"] + 1)
            pool.dma_start(scratch["mod"][:, 512 * (j - 4):512 * (j - 3)], mrow[:, j % 2, :]).then_inc(mod_out[j % 2], 16)
            if 8 <= j <= 10:
                rotary(j - 8)
            if j < 10:
                pool.wait_ge(mod_out[j % 2], 16 * (j // 2 - 1))
                mod_bias(j + 2)
        pool.wait_ge(h_split, KD)
        pool.wait_ge(used, 2 * CI["ada11"] + 2)
        pool.dma_start(decay[:], i["decay"][:, :, :]).then_inc(dec_in, 16)
        pool.wait_ge(mod_out[0], 16 * 4)
        pool.wait_ge(mod_out[1], 16 * 4)
        pool.dma_start(s0[:], i["state_ret"][0, 0].rearrange("h k v -> k h v")).then_inc(dec_in, 16)
        pool.wait_ge(ftok_done, 2)
        pool.dma_start(o["p_f"][0, 0].rearrange("(t p) h -> p t h", p=P), lf_tok[:, 0:2, :]).then_inc(fox_out, 16)
        pool.dma_start(o["s_f"][0, 0], lf_tok[0:DEC, 2, :]).then_inc(fox_out, 16)
        pool.wait_ge(qkT_done, 2 * RH)
        a, b = PACK["kdec"]
        for t in range(3):
            rows = P if t < 2 else DEC
            kk = rot[0:rows, t, 512:1024].rearrange("p (h d) -> p h d", h=RH)
            dd = pack[0:rows, a + RH * t:a + RH * t + RH].unsqueeze(2).to_broadcast([rows, RH, DK])
            st(nc.gpsimd.tensor_tensor(kk, kk, dd, ALU.mult), kdec_done)
        pool.wait_ge(state_done, 2 * RH)
        pool.dma_start(o["p_s"][0, 0].rearrange("h k v -> k h v"), qT[:, :, 0:DV]).then_inc(ret_out, 16)
        pool.dma_start(o["s_s"][0, 0].rearrange("h k v -> k h v"), s0[:]).then_inc(ret_out, 16)
        pool.wait_ge(ret_out, 32)
        pool.dma_start(gnw[:], bcast(i["ret_gn_w"][0], P)).then_inc(gn_in, 16)
        pool.dma_start(gnb[:], bcast(i["ret_gn_b"][0], P)).then_inc(gn_in, 16)
        pool.dma_start(kaug[:, 2, :, 0:DH], i["cache_fox_k"][0, 0]).then_inc(cachek_in, 16)
        st(nc.gpsimd.memset(qaug[DEC:P, 2, :, :], 0.0))
        st.settle()
        st(nc.gpsimd.memset(kaug[DEC:P, 3, :, :], 0.0))
        st.settle()
        st(nc.gpsimd.memset(qaug[:, 0:2, :, DH + 1:DH + 2], 8.0))
        st(nc.gpsimd.memset(qaug[0:DEC, 2, :, DH + 1:DH + 2], 8.0))
        st(nc.gpsimd.memset(kaug[:, 0:3, :, DH:DH + 1], 1.0))
        st(nc.gpsimd.memset(kaug[0:DEC, 3, :, DH:DH + 1], 1.0))
        st.settle()
        q_slots = (0, 1, 3)
        for t in range(3):
            rows = P if t < 2 else DEC
            st(nc.gpsimd.tensor_scalar(qaug[0:rows, t, :, DH], f_tok[0:rows, q_slots[t], :], 8.0, None, ALU.mult))
        for t in range(4):
            rows = P if t < 3 else DEC
            st(nc.gpsimd.tensor_scalar(kaug[0:rows, t, :, DH + 1], f_tok[0:rows, t, :], -1.0, None, ALU.mult),
               aug_ready if t == 3 else None)
        pool.wait_ge(used, 2 * CI["pr1"] + 2)
        pool.dma_start(fv[:, 2, :], i["cache_fox_v"][0, 0].rearrange("t h d -> t (h d)")).then_inc(cachev_in, 16)
        st(nc.gpsimd.memset(fv[DEC:P, 3, :], 0.0))
        st.settle()
        st(nc.gpsimd.memset(psums[:], 1.0), aug_ready)
        pool.wait_ge(evacuated, CI["fk1"] + 1)
        pool.dma_start(o["p_k"][0, 0].rearrange("(t p) h d -> p t h d", p=P)[:, 0], kaug[:, 0, :, 0:DH]).then_inc(fox_out, 16)
        pool.dma_start(o["p_k"][0, 0].rearrange("(t p) h d -> p t h d", p=P)[:, 1], kaug[:, 1, :, 0:DH]).then_inc(fox_out, 16)
        pool.dma_start(o["s_k"][0, 0], kaug[0:DEC, 3, :, 0:DH]).then_inc(fox_out, 16)
        def stage_k(h):
            nc.gpsimd.tensor_copy(kst[:], kaug[:, :, bass.ds(h, 1), :].rearrange("p t a d -> p t (a d)")).then_inc(k_st, 1)

        def stage_v(h):
            nc.gpsimd.tensor_copy(vst[:], fv[:, :, bass.ds(h * DH, DH)]).then_inc(v_st, 1)

        pool.wait_ge(cachek_in, 16)
        stage_k(0)
        pool.wait_ge(evacuated, CI["fv1"] + 1)
        pool.wait_ge(cachev_in, 16)
        stage_v(0)
        pool.wait_ge(qk_tr, 1)
        stage_k(1)
        pool.dma_start(o["p_v"][0, 0].rearrange("(t p) h d -> p t (h d)", p=P), fv[:, 0:2, :]).then_inc(ret_out, 16)
        pool.dma_start(o["s_v"][0, 0].rearrange("p h d -> p (h d)"), fv[0:DEC, 3, :]).then_inc(fox_out, 16)

        with pool.Fori(1, FH - 1) as h:
            pool.wait_ge(qk_tr, h + 1)
            stage_k(h + 1)
            pool.wait_ge(pv_ok, h)
            stage_v(h)
        pool.wait_ge(pv_ok, FH - 1)
        stage_v(FH - 1)
        pool.wait_ge(fox_out, 16 * 6)
        pool.wait_ge(ret_out, 48)
        pool.wait_ge(used, 2 * CI["pf1"] + 2)
        pool.dma_start(xres[:, 0:2, :], i["x_prompt"][0].rearrange("(t p) d -> p t d", p=P)).then_inc(res_in, 16)
        pool.dma_start(xres[0:DEC, 2, :], i["x_sample"][0]).then_inc(res_in, 16)
        md = scratch["mod"]
        pool.dma_start(g1p[:], bcast(md[0, 0:D], P)).then_inc(res_in, 16)
        pool.dma_start(g1s[:], bcast(md[1, 0:D], DEC)).then_inc(res_in, 16)
        pool.wait_ge(evacuated, CI["pf1"] + 1)
        pool.dma_start(l1w[:], bcast(i["ln1_w"][0], P)).then_inc(ln_in, 16)
        pool.dma_start(l1b[:], bcast(i["ln1_b"][0], P)).then_inc(ln_in, 16)
        pool.dma_start(m2p[:, :, :], bcast(md[0, D:3 * D].rearrange("(a d) -> a d", a=2), P)).then_inc(m2_in, 16)
        pool.dma_start(m2s[:, :, :], bcast(md[1, D:3 * D].rearrange("(a d) -> a d", a=2), DEC)).then_inc(m2_in, 16)
        pool.wait_ge(m2_in, 32)
        pool.wait_ge(ln_in, 32)
        for m2, rows in ((m2p, P), (m2s, DEC)):
            st(nc.gpsimd.tensor_scalar(m2[:, 1, :], m2[:, 1, :], 1.0, None, ALU.add))
            st.settle()
            tmp = g1x[0:rows, :]
            st(nc.gpsimd.tensor_tensor(tmp, m2[:, 1, :], l1b[0:rows, :], ALU.mult))
            st(nc.gpsimd.tensor_tensor(m2[:, 1, :], m2[:, 1, :], l1w[0:rows, :], ALU.mult))
            st.settle()
            st(nc.gpsimd.tensor_tensor(m2[:, 0, :], m2[:, 0, :], tmp, ALU.add), m2_ready)
            st.settle()
        pool.wait_ge(evacuated, CI["wo0"] + 1)
        pool.dma_start(wr[:, :, 0:NG], i["w_rg"][0].rearrange("(k p) n -> p k n", p=P)).then_inc(wr_in, 16)
        pool.dma_start(wr[:, :, NG:], i["w_re"][0].rearrange("(k p) n -> p k n", p=P)).then_inc(wr_in, 16)
        pool.dma_start(br[:, 0:NG], bcast(i["b_rg"][0], P)).then_inc(wr_in, 16)
        pool.dma_start(br[:, NG:], bcast(i["b_re"][0], P)).then_inc(wr_in, 16)
        h2d = scratch["h2"]
        pool.wait_ge(h2_ready, 2)
        pool.dma_start(h2d[0:SEQ, :].rearrange("(t p) d -> p t d", p=P), h2[:, 0:2, :]).then_inc(h2_out, 16)
        pool.wait_ge(h2_ready, 3)
        pool.dma_start(h2d[SEQ:T, :], h2[0:DEC, 2, :]).then_inc(h2_out, 16)
        st(nc.gpsimd.memset(xg[:], 0.0))
        st.settle()
        pool.wait_ge(h2_out, 32)
        pool.wait_ge(idx_ready, 1)

        def gather(col):
            nc.gpsimd.tensor_copy(idx1[:], idx[:, col]).then_inc(idx_cp, 1)

        gather(slice(0, 1))
        pool.wait_ge(idx_cp, 1)
        nc.gpsimd.indirect_dma_start(xg[:], None, h2d[:, :], bass.IndirectOffsetOnAxis(ap=idx1[:, 0:1], axis=0),
                                     bounds_check=T - 1, oob_is_err=False).then_inc(x_landed, 16)
        yd = scratch["y"]

        def hold(place=0):
            nc.gpsimd.tensor_tensor(turn[:, place:place + 1], ident[0:1, 0:1], ident[0:1, 0:1], ALU.mult)

        def next_gather(e):
            pool.wait_ge(x_landed, 16 * (e + 1))
            nc.gpsimd.tensor_copy(idx1[:], idx[:, bass.ds(e + 1, 1)]).then_inc(idx_cp, 1)
            pool.wait_ge(idx_cp, e + 2)
            pool.wait_ge(x_trans, e + 1)
            hold()
            nc.gpsimd.indirect_dma_start(xg[:], None, h2d[:, :], bass.IndirectOffsetOnAxis(ap=idx1[:, 0:1], axis=0),
                                         bounds_check=T - 1, oob_is_err=False).then_inc(x_landed, 16)

        def store_item(e):
            if not isinstance(e, int) or e > 0:
                pool.wait_ge(y_written, 16 * e)
            nc.gpsimd.tensor_copy(row1[:], row[:, bass.ds(e, 1)]).then_inc(row_cp, 1)
            pool.wait_ge(row_cp, e + 1)
            pool.wait_ge(y_drained, 2 * (e + 1))
            hold(1)
            nc.gpsimd.indirect_dma_start(yd[:, :], bass.IndirectOffsetOnAxis(ap=row1[:, 0:1], axis=0),
                                         ySb[:].rearrange("p a b -> p (a b)"), None,
                                         bounds_check=2 * T - 1, oob_is_err=False).then_inc(y_written, 16)

        next_gather(0)
        pool.dma_start(g2p[:], bcast(md[0, 3 * D:4 * D], P)).then_inc(tail_in, 16)
        pool.dma_start(g2s[:], bcast(md[1, 3 * D:4 * D], DEC)).then_inc(tail_in, 16)
        pool.dma_start(l2w[:], bcast(i["ln2_w"][0], P)).then_inc(tail_in, 16)
        pool.dma_start(l2b[:], bcast(i["ln2_b"][0], P)).then_inc(tail_in, 16)
        next_gather(1)
        pool.wait_ge(nit_ready, 1)
        n_items = NE + pool.value_load(nit[0:1, 0:1], min_val=0, max_val=EXTRA - 1)
        for t in range(3):
            rows = P if t < 2 else DEC
            st(nc.gpsimd.tensor_tensor(x1[0:rows, t, :], x1[0:rows, t, :], l1w[0:rows, :], ALU.mult))
            st.settle()
            st(nc.gpsimd.tensor_tensor(x1[0:rows, t, :], x1[0:rows, t, :], l1b[0:rows, :], ALU.add), x1_ready)
        next_gather(2)
        store_item(0)
        with pool.Fori(3, n_items) as e:
            next_gather(e)
            store_item(e - 2)
        store_item(n_items - 2)
        store_item(n_items - 1)

    TS = [("ret", 0), ("fox", 1), ("mix", 2)]

    @block.scalar
    def _(act):
        st = Steps(act, own_act)

        def hi(n):
            act.wait_ge(raw_landed[n % NRAW], 16 * (n // NRAW + 1))
            if n >= NSPL:
                act.wait_ge(used, n - NSPL + 1)
            nc.scalar.activation(whi[n % NSPL][:], raw[n % NRAW][:], ACT.Copy).then_inc(hi_done, 1)

        def chunk(name):
            hi(2 * CI[name])
            hi(2 * CI[name] + 1)

        def copy_bank(key, dst, src):
            b, _, f, d = use[key]
            act.wait_ge(*f)
            st(nc.scalar.activation(dst, src(b), ACT.Copy), d)

        def gate_fn(name, buf, fn):
            act.wait_ge(evacuated, CI[name] + 1)
            h = slice(512 * int(name[2]), 512 * int(name[2]) + 512)
            st(nc.scalar.activation(buf[:, 0:2, h], buf[:, 0:2, h], fn), gact)
            st(nc.scalar.activation(buf[0:DEC, 2, h], buf[0:DEC, 2, h], fn), gact)

        def split_hi(kind, dst):
            for k in range(KD):
                b, _, f, _ = use[(kind, k)]
                act.wait_ge(*f)
                st(nc.scalar.activation(dst[:, k, 0:T], b[:, 0:T], ACT.Copy), ts_hi)

        act.wait_ge(c_in, 32)
        st(nc.scalar.activation(cs2[:], c2[:], ACT.Silu), c_silu)
        b, _, f, _ = use["cT"]
        act.wait_ge(*f)
        act.wait_ge(fills_done, 1)
        st(nc.scalar.activation(cst[:, :, 0:2], b[:, 0:2 * KD].rearrange("p (k c) -> p k c", c=2), ACT.Copy), c_hi)
        for n in range(4):
            hi(n)
        for k in range(KD):
            b, _, f, d = use[("xT", k)]
            act.wait_ge(*f)
            st(nc.scalar.activation(hT[:, k, :], b[:, 0:T], ACT.Copy), d)
        for j in range(2, 5):
            chunk(f"ada{j}")
        for k in range(KD):
            act.wait_ge(h_ready, 2 * k + 2)
            st(nc.scalar.activation(actH[:, k, 0:T], hT[:, k, :], ACT.Copy), h_hi)
        chunk("ada5")
        chunk("ada6")
        act.wait_ge(wf_in, 32)
        st(nc.scalar.activation(wf_hi[:], wf_raw[:], ACT.Copy), wf_h)
        chunk("rq")
        act.wait_ge(zf_done, 1)
        st(nc.scalar.activation(zl[:], za[:], ACT.Exp, scale=-1.0))
        st.settle()
        st(nc.scalar.activation(zl[:], zl[:], ACT.Ln, bias=1.0), zf_act)
        copy_bank("cfT", cfT[:], lambda b: b[0:FH, 0:PAST])
        for n in ("ada7", "ada8", "rk", "ada9", "ada10", "rv0", "ada11", "rv1", "rg0"):
            chunk(n)
        for j in range(2 * RH):
            dst = (qT if j < RH else kT)[:, j % RH, :]
            b, _, f, d = use[("qkT", j)]
            act.wait_ge(*f)
            act.wait_ge(ftok_done, 2)
            act.wait_ge(fox_out, 16 * 2)
            st(nc.scalar.activation(dst, b[:, 0:T], ACT.Copy), qkT_done)
        chunk("rg1")
        gate_fn("rg0", rg, ACT.Silu)
        chunk("ga0")
        gate_fn("rg1", rg, ACT.Silu)
        for h in range(RH):
            hs = slice(DV * h, DV * h + DV)
            copy_bank(("op", h), o_ret[:, 0:2, hs], lambda b: b[:, 0:512].rearrange("p (t v) -> p t v", t=2))
            b, _, f, _ = use[("os", h)]
            act.wait_ge(*f)
            st(nc.scalar.activation(o_ret[0:DEC, 2, hs], b[0:DEC, 0:DV], ACT.Copy), oret_act)
        chunk("ga1")
        gate_fn("ga0", gate, ACT.Sigmoid)
        chunk("fq0")
        gate_fn("ga1", gate, ACT.Sigmoid)
        act.wait_ge(gn_var, 1)
        st(nc.scalar.activation(stats[:, 120:132], stats[:, 108:120], ACT.Sqrt), gn_std)
        for n in ("fq1", "fk0", "fk1"):
            chunk(n)
        split_hi("ret", retH)
        for n in ("pr0", "pr1", "fv0", "fv1"):
            chunk(n)
        hi(2 * CI["gb0"])
        act.wait_ge(aug_ready, 2)
        act.wait_ge(used, 2 * CI["pr1"] + 2)

        def stage_q(h):
            nc.scalar.activation(qst[:], qaug[:, :, bass.ds(h, 1), :].rearrange("p t a d -> p t (a d)"), ACT.Copy,
                                 scale=DH ** -0.5).then_inc(q_st, 1)

        def copy_q(h):
            act.wait_ge(qk_tr, h + 1)
            nc.scalar.activation(qTh[:], bank[0][0:DH + 2, 0:T], ACT.Copy).then_inc(qT_cp, 1)

        def exponentials(h):
            act.wait_ge(maxed, h + 1)
            nc.scalar.activation(pr[:, 0, 0:P], bank[2][:, 0:P], ACT.Exp, bias=nmax[:, 0:1], accum_out=psums[:, 0:1])
            nc.scalar.activation(pr[:, 1, :], bank[2][:, P:384], ACT.Exp, bias=nmax[:, 1:2], accum_out=psums[:, 1:2])
            nc.scalar.activation(pr[0:DEC, 2, 0:192], bank[3][0:DEC, 0:192], ACT.Exp, bias=nmax[0:DEC, 2:3],
                                 accum_out=psums[0:DEC, 2:3]).then_inc(exped, 1)

        def copy_p(h):
            act.wait_ge(p_tr, h + 1)
            nc.scalar.activation(prT[:, 0:256], bank[4][:, 0:256], ACT.Copy).then_inc(pT_a, 1)

        stage_q(0)
        copy_q(0)
        stage_q(1)
        exponentials(0)
        copy_q(1)
        stage_q(2)
        copy_p(0)
        with act.Fori(1, FH - 2) as h:
            exponentials(h)
            copy_q(h + 1)
            stage_q(h + 2)
            copy_p(h)
        exponentials(FH - 2)
        copy_q(FH - 1)
        copy_p(FH - 2)
        exponentials(FH - 1)
        copy_p(FH - 1)
        hi(2 * CI["gb0"] + 1)
        split_hi("fox", foxH)
        chunk("gb1")
        gate_fn("gb0", gate_b, ACT.Sigmoid)
        chunk("pf0")
        gate_fn("gb1", gate_b, ACT.Sigmoid)
        chunk("pf1")
        hi(2 * CI["wo0"])
        split_hi("mix", mixH)
        hi(2 * CI["wo0"] + 1)
        chunk("wo1")
        hi(N0)
        hi(N0 + 1)
        act.wait_ge(ln_var, 1)
        st(nc.scalar.activation(mv[:, :, 1], mv[:, :, 1], ACT.Sqrt), ln_std)
        hi(N0 + 2)
        for t in range(3):
            for q in range(2):
                b, _, f, d = use[("h2T", t, q)]
                rows = P if t < 2 else DEC
                act.wait_ge(*f)
                st(nc.scalar.activation(h2T[:, 4 * q:4 * q + 4, P * t:P * t + rows],
                                        b[:, 0:4 * rows].rearrange("p (k c) -> p k c", k=4), ACT.Copy), h2T_done)
        act.wait_ge(r_dve, 1)
        st(nc.scalar.activation(gex[:], gex[:], ACT.Exp), r_act)
        act.wait_ge(r_dve, 2)
        st(nc.scalar.activation(ga_t[:, :, 1:2], ga_t[:, :, 0:1], ACT.Exp), r_act)

        def item_hi(e, j):
            rs, ss = slot_of(j)
            act.wait_ge(raw_landed[rs], 16 * ((E0 + j - rs) // NRAW + e))
            act.wait_ge(used, sub(e, j) - NSPL + 1)
            nc.scalar.activation(whi[ss][:], raw[rs][:], ACT.Copy).then_inc(hi_done, 1)

        def x_high(e):
            act.wait_ge(x_trans, e + 1)
            nc.scalar.activation(xT[:, :, 0:SLOTS], bank[4][:, :].rearrange("p (k c) -> p k c", k=KD), ACT.Copy).then_inc(x_hi, 1)

        def silu(e):
            act.wait_ge(a_drained, e + 1)
            nc.scalar.activation(aA[:], aS[:], ACT.Silu).then_inc(silu_ok, 1)

        def y_low(e, first_sub):
            for j in range(2):
                act.wait_ge(used, first_sub + j + 1)
                nc.scalar.activation(yLo[:, j, :], bank[2 + j][SLOTS:P, :], ACT.Copy).then_inc(y_lo, 1)

        def hidden_high(e):
            act.wait_ge(h_tr, e + 1)
            nc.scalar.activation(hdT[:, :, 0:SLOTS], bank[5][:, 0:4 * SLOTS].rearrange("p (k c) -> p k c", k=4), ACT.Copy).then_inc(hh_hi, 1)

        def low_copy(after, dst, b, done):
            act.wait_ge(used, after + 1)
            nc.scalar.activation(dst[:], bank[b][SLOTS:P, :], ACT.Copy).then_inc(done, 1)

        x_high(0)
        hi(N0 + 3)
        low_copy(N0 + 1, aLo, 0, a_lo)
        low_copy(N0 + 3, uLo, 1, u_lo)
        x_high(1)

        def item(e, second):
            item_hi(e, 0)
            silu(e - 1)
            item_hi(e, 1)
            if second:
                y_low(e - 2, sub(e - 1, 4))
            item_hi(e, 2)
            hidden_high(e - 1)
            item_hi(e, 3)
            act.wait_ge(a_drained, e)
            low_copy(sub(e, 1), aLo, 0, a_lo)
            item_hi(e, 4)
            item_hi(e, 5)
            act.wait_ge(u_drained, e)
            low_copy(sub(e, 3), uLo, 1, u_lo)
            x_high(e + 1)

        item(1, False)
        act.wait_ge(nit_ready, 1)
        n_items = NE + act.value_load(nit[0:1, 0:1], min_val=0, max_val=EXTRA - 1)
        with act.Fori(2, n_items) as e:
            item(e, True)
        item_hi(n_items, 0)
        silu(n_items - 1)
        item_hi(n_items, 1)
        y_low(n_items - 2, sub(n_items - 1, 4))
        hidden_high(n_items - 1)
        act.wait_ge(y_drained, (n_items - 1) * 2)
        y_low(n_items - 1, sub(n_items, 0))
        def first_gate(t):
            rows = P if t < 2 else DEC
            act.wait_ge(yg_in[t], 16)
            nc.scalar.activation(yg[0:rows, t, 0, :], yg[0:rows, t, 0, :], ACT.Copy, scale=gates[0:rows, t, 0:1]).then_inc(comb, 1)

        def deviation(t):
            act.wait_ge(fin_std, t + 1)
            nc.scalar.activation(mv[:, t, 1:2], mv[:, t, 1:2], ACT.Sqrt).then_inc(ln_std, 1)

        def normalise(t):
            rows = P if t < 2 else DEC
            act.wait_ge(nb_ready, t + 1)
            nc.scalar.activation(x1[0:rows, t, :], x1[0:rows, t, :], ACT.Identity, bias=mv[0:rows, t, 0:1],
                                 scale=mv[0:rows, t, 1:2]).then_inc(xn_ready, 1)

        first_gate(0)
        first_gate(1)
        deviation(0)
        first_gate(2)
        deviation(1)
        normalise(0)
        deviation(2)
        normalise(1)
        normalise(2)

    @block.vector
    def _(dve):
        st = Steps(dve, own_dve)
        V = nc.vector

        def lo(n):
            dve.wait_ge(hi_done, n + 1)
            V.tensor_tensor(wlo[n % NSPL][:], raw[n % NRAW][:], whi[n % NSPL][:].bitcast(F32), ALU.subtract).then_inc(lo_done, 1)

        def chunk(name):
            lo(2 * CI[name])
            lo(2 * CI[name] + 1)

        def filled_of(key):
            b, _, f, d = use[key]
            dve.wait_ge(*f)
            return b, d

        def destination(name):
            h = int(name[2]) if name[2:] else 0
            cols = slice(512 * h, 512 * h + 512)
            if name == "rq":
                return [rqk[:, t, 0:512] for t in range(3)]
            if name == "rk":
                return [rqk[:, t, 512:1024] for t in range(3)]
            if name[:2] == "fq":
                return [qaug[:, t, 8 * h:8 * h + 8, 0:DH] for t in range(3)]
            if name[:2] == "fk":
                return [kaug[:, t, 8 * h:8 * h + 8, 0:DH] for t in (0, 1, 3)]
            if name[:2] == "fv":
                return [fv[:, t, cols] for t in (0, 1, 3)]
            buf = {"rv": rv, "rg": rg, "ga": gate, "gb": gate_b}[name[:2]]
            return [buf[:, t, cols] for t in range(3)]

        def like(ap, dst):
            return ap.rearrange("p (h d) -> p h d", d=DH) if len(dst.shape) == 3 else ap

        def evac_z(name):
            m = ZCH.index(name)
            dst = destination(name)
            dve.wait_ge(evacuated, CI[name])
            dve.wait_ge(bias_landed[m % 2], 16 * (m // 2 + 1))
            for t in range(2):
                b, d = filled_of((name, t))
                st(V.tensor_tensor(dst[t], like(b[:, :], dst[t]), like(bias[:, m % 2, :], dst[t]), ALU.add), d)
            b, d = filled_of((name, 2))
            st(V.tensor_tensor(low_s[:], b[DEC:P, :], bias[0:DEC, m % 2, :], ALU.add))
            st.settle()
            ds = dst[2][0:DEC]
            st(V.tensor_tensor(ds, like(b[0:DEC, :], ds), like(low_s[:], ds), ALU.add), evacuated)

        def sample_sum(name):
            b, d = filled_of((name, 2))
            st(V.tensor_copy(low_s[:], b[DEC:P, :]))
            st.settle()
            st(V.tensor_tensor(low_s[:], b[0:DEC, :], low_s[:], ALU.add))
            st.settle()

        def evac_ret_proj(name):
            cols = slice(512 * int(name[2]), 512 * int(name[2]) + 512)
            dve.wait_ge(gact, 4 + 4)
            dve.wait_ge(evacuated, CI[name])
            for t in range(2):
                b, d = filled_of((name, t))
                st(V.tensor_tensor(gate[:, t, cols], b[:, :], gate[:, t, cols], ALU.mult), d)
            sample_sum(name)
            st(V.tensor_tensor(gate[0:DEC, 2, cols], low_s[:], gate[0:DEC, 2, cols], ALU.mult), evacuated)

        def evac_fox_proj(name):
            cols = slice(512 * int(name[2]), 512 * int(name[2]) + 512)
            dve.wait_ge(gact, 8 + 4)
            dve.wait_ge(evacuated, CI[name])
            for t in range(2):
                b, d = filled_of((name, t))
                st(V.tensor_tensor(bias[:, t, :], b[:, :], gate_b[:, t, cols], ALU.mult), d)
                st.settle()
                st(V.tensor_tensor(gate[:, t, cols], bias[:, t, :], gate[:, t, cols], ALU.add))
            sample_sum(name)
            st(V.tensor_tensor(low_s[:], low_s[:], gate_b[0:DEC, 2, cols], ALU.mult))
            st.settle()
            st(V.tensor_tensor(gate[0:DEC, 2, cols], low_s[:], gate[0:DEC, 2, cols], ALU.add), evacuated)

        def evac_wo(name):
            cols = slice(512 * int(name[2]), 512 * int(name[2]) + 512)
            dve.wait_ge(res_in, 64)
            dve.wait_ge(evacuated, CI[name])
            for t in range(2):
                b, d = filled_of((name, t))
                st(V.scalar_tensor_tensor(x1[:, t, cols], g1p[:, cols], 1.0, b[:, :], ALU.add, ALU.mult), d)
                st.settle()
                st(V.scalar_tensor_tensor(x1[:, t, cols], xres[:, t, cols], ALPHA, x1[:, t, cols], ALU.mult, ALU.add))
                st.settle()
                st(V.bn_stats(st1[:, t, int(name[2]), :], x1[:, t, cols]))
            sample_sum(name)
            st(V.scalar_tensor_tensor(low_s[:], g1s[:, cols], 1.0, low_s[:], ALU.add, ALU.mult))
            st.settle()
            st(V.scalar_tensor_tensor(x1[0:DEC, 2, cols], xres[0:DEC, 2, cols], ALPHA, low_s[:], ALU.mult, ALU.add), evacuated)
            st.settle()
            st(V.bn_stats(st1[0:DEC, 2, int(name[2]), :], x1[0:DEC, 2, cols]))

        def evac_ada(j):
            cols = slice(512 * j, 512 * j + 512)
            b, d = filled_of((f"ada{j}", 0))
            rows = mod[:, cols] if j < 4 else mrow[:, j % 2, :]
            if j >= 4:
                dve.wait_ge(mrow_in[j % 2], 16 * (j // 2 - 1))
            st(V.tensor_tensor(rows, b[32:34, :], rows, ALU.add))
            st.settle()
            st(V.tensor_tensor(rows, b[0:2, :], rows, ALU.add), evacuated)

        def split_lo(kind, index, hi_, lo_):
            for k in range(KD):
                b, _, f, d = use[(kind, k)]
                dve.wait_ge(ts_hi, KD * index + k + 1)
                st(V.tensor_tensor(lo_[:, k, :], b[:, 0:SEQ], hi_[:, k, 0:SEQ].bitcast(F32), ALU.subtract))
                st(V.tensor_tensor(hi_[:, k, T:384], b[:, SEQ:T], hi_[:, k, SEQ:T].bitcast(F32), ALU.subtract), d)

        dve.wait_ge(pack_in, 16)
        st(V.tensor_copy(identb[:], ident))
        st(V.tensor_copy(causalb[:], const("causal")), consts_ready)
        b, d = filled_of("cT")
        dve.wait_ge(c_hi, 1)
        st(V.tensor_tensor(cst[:, :, 32:34], b[:, 0:2 * KD].rearrange("p (k c) -> p k c", c=2),
                           cst[:, :, 0:2].bitcast(F32), ALU.subtract), c_parts)
        lo(0)
        lo(1)
        for j in range(1, 4):
            chunk(f"ada{j}")
            if j == 1:
                dve.wait_ge(modb_in, 16)
            evac_ada(j - 1)
        evac_ada(3)
        lo(2 * CI["ada4"])
        b, d = filled_of("modT")
        bm = b[:, 0:4 * KD].rearrange("p (a k c) -> p a k c", a=2, k=KD)
        st(V.tensor_copy(modT[:, 0], bm[:, 0]))
        st(V.tensor_scalar(modT[:, 1], bm[:, 1], 1.0, None, ALU.add), d)
        st.settle()
        for k in range(KD):
            dve.wait_ge(*use[("xT", k)][3])
            st(V.tensor_scalar(hT[:, k, 0:SEQ], hT[:, k, 0:SEQ], modT[:, 1, k, 0:1], modT[:, 0, k, 0:1], ALU.mult, ALU.add), h_ready)
            st(V.tensor_scalar(hT[:, k, SEQ:T], hT[:, k, SEQ:T], modT[:, 1, k, 1:2], modT[:, 0, k, 1:2], ALU.mult, ALU.add), h_ready)
        lo(2 * CI["ada4"] + 1)
        for j in range(5, 7):
            chunk(f"ada{j}")
            evac_ada(j - 1)
        dve.wait_ge(wf_h, 1)
        st(V.tensor_tensor(wf_lo[:], wf_raw[:], wf_hi[:].bitcast(F32), ALU.subtract), wf_l)
        chunk("rq")
        evac_ada(6)
        b, d = filled_of("zf")
        st(V.tensor_scalar(zf[:], b[0:FH, 0:T], bf_col[:, 0:1], None, ALU.add), d)
        st.settle()
        st(V.scalar_tensor_tensor(za[:], zf[:], -1.0, zf[:], ALU.mult, ALU.max), zf_done)
        chunk("ada7")
        evac_z("rq")
        dve.wait_ge(zf_act, 1)
        st(V.tensor_scalar(lfT[:], zf[:], 0.0, None, ALU.min))
        st.settle()
        st(V.tensor_tensor(lfT[:], lfT[:], zl[:], ALU.subtract), lf_ready)
        st.settle()
        dve.wait_ge(fills_done, 2)
        dve.wait_ge(use["cfT"][3][0], use["cfT"][3][1])
        st(V.tensor_tensor_scan(fsT[:, 0:SEQ], onesT[:, 0:SEQ], lfT[:, 0:SEQ], 0.0, ALU.mult, ALU.add))
        st(V.tensor_tensor_scan(fsT[:, SEQ:SEQ + PAST], onesT[:, 0:PAST], cfT[:], 0.0, ALU.mult, ALU.add))
        st.settle()
        st(V.tensor_tensor_scan(fsT[:, T + PAST - DEC:T + PAST], onesT[:, 0:DEC], lfT[:, SEQ:T],
                                fsT[:, SEQ + PAST - 1:SEQ + PAST], ALU.mult, ALU.add), fs_ready)
        chunk("ada8")
        evac_ada(7)
        chunk("rk")
        evac_ada(8)
        chunk("ada9")
        evac_z("rk")
        b, d = filled_of("ftok")
        bt = b[:, 0:7 * FH].rearrange("p (t h) -> p t h", h=FH)
        st(V.tensor_copy(f_tok[:, 0:3, :], bt[:, 0:3, :]))
        st(V.tensor_copy(f_tok[0:DEC, 3, :], bt[0:DEC, 3, :]))
        st(V.tensor_copy(lf_tok[:, 0:2, :], bt[:, 4:6, :]), ftok_done)
        st(V.tensor_copy(lf_tok[0:DEC, 2, :], bt[0:DEC, 6, :]), ftok_done)
        chunk("ada10")
        evac_ada(9)
        chunk("rv0")
        evac_ada(10)
        chunk("ada11")
        evac_z("rv0")
        chunk("rv1")
        evac_ada(11)
        chunk("rg0")
        evac_z("rv1")
        dve.wait_ge(qkT_done, 2 * RH)
        st(V.tensor_tensor(qdT[:], qT[:, :, SEQ:T], const("qdec").rearrange("p (h n) -> p h n", h=RH), ALU.mult), qd_done)
        chunk("rg1")
        evac_z("rg0")
        chunk("ga0")
        evac_z("rg1")
        dve.wait_ge(dec_in, 32)
        gam = [float(np.exp(DEC * g)) for g in log_gamma()]

        def decayed(h):
            b, d = filled_of(("sc", h))
            if h:
                dve.wait_ge(*use[("op", h - 1)][2])
                dve.wait_ge(*use[("os", h - 1)][2])
            st(V.tensor_tensor(sT[:, 0:SEQ], b[:, 0:SEQ], decay[:, h, :], ALU.mult))
            st(V.tensor_tensor(sT[:, SEQ:384], b[:, SEQ:384], decay[:, h, 0:P], ALU.mult))
            st(V.tensor_tensor(sTs, b[0:DEC, 384:448], decay[0:DEC, h, 0:DEC], ALU.mult), d)

        def states(h):
            b, d = filled_of(("os", h))
            dve.wait_ge(oret_act, h + 1)
            st(V.tensor_copy(qT[:, h, 0:DV], b[:, DV:2 * DV]), state_done)
            b2, d2 = filled_of(("ss", h))
            st(V.scalar_tensor_tensor(s0[:, h, :], s0[:, h, :], gam[h], b2[:, 0:DV], ALU.mult, ALU.add), state_done)

        for h in range(RH):
            decayed(h)
            states(h)
        chunk("ga1")
        evac_z("ga0")
        for t in range(3):
            rows = P if t < 2 else DEC
            for h in range(RH):
                st(V.bn_stats(stats[0:rows, 6 * (RH * t + h):6 * (RH * t + h) + 6], o_ret[0:rows, t, DV * h:DV * h + DV]))
        st(V.memset(stats[:, 84:120], 1.0))
        st.settle()
        for t in range(3):
            rows = P if t < 2 else DEC
            for h in range(RH):
                q = RH * t + h
                st(V.bn_aggr(stats[0:rows, 84 + 2 * q:86 + 2 * q], stats[0:rows, 6 * q:6 * q + 6]))
        st.settle()
        mvs = stats[:, 84:108].rearrange("p (q c) -> p q c", c=2)
        st(V.tensor_scalar(stats[:, 108:120], mvs[:, :, 1], GN_EPS, None, ALU.add), gn_var)
        chunk("fq0")
        evac_z("ga1")
        dve.wait_ge(gn_std, 1)
        st(V.reciprocal(stats[:, 132:144], stats[:, 120:132]))
        st.settle()
        for t in range(3):
            rows = P if t < 2 else DEC
            for h in range(RH):
                q = RH * t + h
                oo = o_ret[0:rows, t, DV * h:DV * h + DV]
                st(V.tensor_scalar(oo, oo, mvs[0:rows, q, 0:1], stats[0:rows, 132 + q:133 + q], ALU.subtract, ALU.mult))
        chunk("fq1")
        dve.wait_ge(aug_ready, 1)
        evac_z("fq0")
        dve.wait_ge(gn_in, 32)
        dve.wait_ge(gact, 4)
        for w_, op in ((gnw, ALU.mult), (gnb, ALU.add)):
            st.settle()
            for t in range(3):
                rows = P if t < 2 else DEC
                st(V.tensor_tensor(o_ret[0:rows, t, :], o_ret[0:rows, t, :], w_[0:rows, :], op))
        chunk("fk0")
        evac_z("fq1")
        for t in range(3):
            rows = P if t < 2 else DEC
            st(V.tensor_tensor(o_ret[0:rows, t, :], o_ret[0:rows, t, :], rg[0:rows, t, :], ALU.mult), ret_ready)
        chunk("fk1")
        evac_z("fk0")
        split_lo("ret", 0, retH, retL)
        chunk("pr0")
        evac_z("fk1")
        chunk("pr1")
        evac_ret_proj("pr0")
        chunk("fv0")
        evac_ret_proj("pr1")
        dve.wait_ge(aug_ready, 2)
        chunk("fv1")
        evac_z("fv0")
        lo(2 * CI["gb0"])
        evac_z("fv1")

        def copy_k(h):
            dve.wait_ge(qk_tr, h + 1)
            V.tensor_copy(kTh[:], bank[1][0:DH + 2, 0:T + PAST]).then_inc(kT_cp, 1)

        def maxima(h):
            dve.wait_ge(scored, h + 1)
            V.tensor_reduce(nmax[:, 0:1], bank[2][:, 0:P], AX.X, ALU.max, negate=True)
            V.tensor_reduce(nmax[:, 1:2], bank[2][:, P:384], AX.X, ALU.max, negate=True)
            V.tensor_reduce(nmax[0:DEC, 2:3], bank[3][0:DEC, 0:192], AX.X, ALU.max, negate=True).then_inc(maxed, 1)

        def copy_p(h, first=False):
            dve.wait_ge(exped, h + 1)
            if not first:
                dve.wait_ge(o_ok, h)
            V.reciprocal(pinv[:], psums[:]).then_inc(r_fox, 1)
            dve.wait_ge(p_tr, h + 1)
            V.tensor_copy(prT[:, 256:448], bank[6][:, 0:192])
            V.tensor_copy(prT[0:DEC, 448:512], bank[6][0:DEC, 192:SEQ]).then_inc(pT_d, 1)

        def head_out(h):
            dve.wait_ge(pv_ok, h + 1)
            dve.wait_ge(r_fox, h + 1)
            for t in range(3):
                rows = P if t < 2 else DEC
                ins = V.tensor_scalar(fox_o[t][0:rows, bass.ds(h * DH, DH)],
                                      bank[5][0:rows, DH * t:DH * t + DH], pinv[0:rows, t:t + 1], None, ALU.mult)
            ins.then_inc(o_ok, 1)

        copy_k(0)
        maxima(0)
        copy_k(1)
        copy_p(0, True)
        maxima(1)
        head_out(0)
        with dve.Fori(1, FH - 1) as h:
            copy_k(h + 1)
            copy_p(h)
            maxima(h + 1)
            head_out(h)
        copy_p(FH - 1)
        head_out(FH - 1)
        lo(2 * CI["gb0"] + 1)
        dve.wait_ge(fox_out, 16 * 6)
        split_lo("fox", 1, foxH, foxL)
        chunk("gb1")
        evac_z("gb0")
        chunk("pf0")
        evac_z("gb1")
        chunk("pf1")
        evac_fox_proj("pf0")
        lo(2 * CI["wo0"])
        evac_fox_proj("pf1")
        split_lo("mix", 2, mixH, mixL)
        lo(2 * CI["wo0"] + 1)
        chunk("wo1")
        evac_wo("wo0")
        lo(N0)
        evac_wo("wo1")

        def deviations(stat_sem):
            st(V.memset(mv[:], 1.0))
            st.settle()
            for t in range(3):
                rows = P if t < 2 else DEC
                st(V.bn_aggr(mv[0:rows, t, :], st1[0:rows, t, :, :]))
            st.settle()
            st(V.tensor_scalar(mv[:, :, 1], mv[:, :, 1], LN_EPS, None, ALU.add), stat_sem)

        deviations(ln_var)
        dve.wait_ge(ln_std, 1)
        st(V.reciprocal(mv[:, :, 1], mv[:, :, 1]))
        st.settle()
        dve.wait_ge(m2_ready, 2)
        for t in range(3):
            rows = P if t < 2 else DEC
            xt, ht = x1[0:rows, t, :], h2[0:rows, t, :]
            m2 = m2p if t < 2 else m2s
            st(V.tensor_scalar(xt, xt, mv[0:rows, t, 0:1], mv[0:rows, t, 1:2], ALU.subtract, ALU.mult), x_norm)
            st.settle()
            st(V.tensor_tensor(ht, xt, m2[0:rows, 1, :], ALU.mult))
            st.settle()
            st(V.tensor_tensor(ht, ht, m2[0:rows, 0, :], ALU.add), h2_ready)

        iota = const("iota")
        dve.wait_ge(wr_in, 64)
        st(V.memset(lg[:], 0.0))
        st(V.memset(g8[:], NEG))
        st(V.memset(oneb[:], 1.0))
        st(V.memset(one32[:], 1.0))
        st(V.tensor_copy(befb[:], const("before")))
        st.settle()
        lo(N0 + 1)
        lo(N0 + 2)
        b, d = filled_of("lg")
        bl = b[:, 0:3 * (NG + NE)].rearrange("p (t n) -> p t n", t=3)
        brr = br[:, :].unsqueeze(1).to_broadcast([P, 2, NG + NE])
        st(V.tensor_tensor(lg[:, 0:2, :], bl[:, 0:2, :], brr, ALU.add))
        st(V.tensor_tensor(lg[0:DEC, 2, :], bl[0:DEC, 2, :], br[0:DEC, :], ALU.add), d)
        st.settle()
        st(V.tensor_copy(g8[:, :, 0:NG], lg[:, :, 0:NG]))
        st.settle()
        for t in range(3):
            st(V.max(gmx[:, t, :], g8[:, t, :]))
        st.settle()
        for t in range(3):
            st(V.max_index(gix[:, t, :], gmx[:, t, :], g8[:, t, :]))
        st(V.tensor_tensor(gex[:], lg[:, :, 0:NG], gmx[:, :, 0:1].to_broadcast([P, 3, NG]), ALU.subtract), r_dve)
        st.settle()
        st(V.tensor_copy(gid[:], gix[:, :, 0:1]))
        st.settle()
        st(V.tensor_tensor(goh[:], iota[:, 0:NG].unsqueeze(1).to_broadcast([P, 3, NG]), gid[:].to_broadcast([P, 3, NG]), ALU.is_equal))
        st.settle()
        ev = lg[:, :, NG:].rearrange("p t (g e) -> p t g e", g=NG)
        st(V.tensor_tensor(elx[:], ev, goh[:].unsqueeze(3).to_broadcast([P, 3, NG, EG]), ALU.mult))
        st.settle()
        st(V.tensor_reduce(el[:], elx[:].rearrange("p t g e -> p t e g"), AX.X, ALU.add))
        st.settle()
        for t in range(3):
            st(V.max(emx[:, t, :], el[:, t, :]))
        st.settle()
        for t in range(3):
            st(V.max_index(eix[:, t, :], emx[:, t, :], el[:, t, :]))
        st(V.tensor_tensor(ga_t[:, :, 0:1], emx[:, :, 1:2], emx[:, :, 0:1], ALU.subtract), r_dve)
        st.settle()
        st(V.tensor_copy(eid[:], eix[:, :, 0:2]))
        st.settle()
        st(V.scalar_tensor_tensor(eid[:], gid[:].to_broadcast([P, 3, 2]), float(EG), eid[:], ALU.mult, ALU.add))
        st.settle()
        i32b = iota[:, 0:NE].unsqueeze(1).to_broadcast([P, 2, NE])
        for t in range(3):
            st(V.tensor_tensor(oh[:, t], i32b, eid[:, t, :].unsqueeze(2).to_broadcast([P, 2, NE]), ALU.is_equal))
        st.settle()
        va = PACK["valid"][0]
        st(V.tensor_scalar(oh[:, 2], oh[:, 2], pack[:, va + 2:va + 3], None, ALU.mult))
        st.settle()
        st(V.tensor_tensor(msk[:], oh[:, :, 0, :], oh[:, :, 1, :], ALU.add), msk_done)
        dve.wait_ge(r_act, 2)
        st(V.tensor_reduce(gpr[:], gex[:], AX.X, ALU.add))
        st(V.tensor_scalar(ga_t[:, :, 0:1], ga_t[:, :, 1:2], 1.0, None, ALU.add))
        st.settle()
        st(V.tensor_tensor(gpr[:], gpr[:], ga_t[:, :, 0:1], ALU.mult))
        st.settle()
        st(V.reciprocal(gates[:, :, 0:1], gpr[:]))
        st.settle()
        st(V.tensor_tensor(gates[:, :, 1:2], gates[:, :, 0:1], ga_t[:, :, 1:2], ALU.mult))
        b, d = filled_of("pos")
        st(V.tensor_copy(pos[:], b[:, 0:3 * NE].rearrange("p (t n) -> p t n", t=3)), d)
        b, d = filled_of("cnt")
        st(V.tensor_copy(cnt[:], b[:, 0:NE]), d)
        st.settle()
        mu = const("multiples")
        st(V.tensor_tensor(cnx[:], cnt[:].unsqueeze(2).to_broadcast([P, NE, 4]), mu.unsqueeze(1).to_broadcast([P, NE, 4]), ALU.is_gt))
        st.settle()
        st(V.tensor_reduce(ext[:], cnx[:], AX.X, ALU.add))
        st.settle()
        st(V.tensor_tensor_scan(cum[:], one32[:], ext[:], 0.0, ALU.mult, ALU.add))
        st.settle()
        st(V.tensor_tensor(exc[:], cum[:], ext[:], ALU.subtract))
        st.settle()
        for t in range(3):
            st(V.tensor_tensor(oht[:, t], oh[:, t], pos[:, t, :].unsqueeze(1).to_broadcast([P, 2, NE]), ALU.mult))
        st.settle()
        st(V.tensor_reduce(ch_pos[:], oht[:], AX.X, ALU.add))
        st.settle()
        for t in range(3):
            st(V.tensor_tensor(oht[:, t], oh[:, t], exc[:, :].unsqueeze(1).to_broadcast([P, 2, NE]), ALU.mult))
        st.settle()
        st(V.tensor_reduce(ch_exc[:], oht[:], AX.X, ALU.add))
        cp6 = ch_pos[:].rearrange("p t c -> p (t c)")
        st(V.tensor_tensor(chx[:], cp6.unsqueeze(2).to_broadcast([P, 6, 4]), mu.unsqueeze(1).to_broadcast([P, 6, 4]), ALU.is_ge))
        st.settle()
        st(V.scalar_tensor_tensor(ch_t[:], ch_exc[:], float(NE - 1), eid[:], ALU.add, ALU.subtract))
        st.settle()
        st(V.tensor_tensor(ch_t[:], ch_t[:], chx[:, :, 0:1].rearrange("p (t c) a -> p t (c a)", c=2), ALU.mult))
        st(V.tensor_reduce(ch_q[:].rearrange("p t c -> p (t c)"), chx[:], AX.X, ALU.add))
        st.settle()
        st(V.tensor_tensor(item[:], ch_t[:], eid[:], ALU.add))
        st.settle()
        st(V.tensor_tensor(item[:], item[:], ch_q[:], ALU.add))
        st(V.scalar_tensor_tensor(ch_pos[:], ch_q[:], -float(SLOTS), ch_pos[:], ALU.mult, ALU.add))
        st.settle()
        t1 = PACK["tok1"][0]
        io_i = iota[:, 0:ITEMS].unsqueeze(1).to_broadcast([P, 2, ITEMS])
        io_s = iota[:, 0:SLOTS].unsqueeze(1).to_broadcast([P, 2, SLOTS])
        for t in range(3):
            st(V.tensor_tensor(oh_s[:, t], io_s, ch_pos[:, t, :].unsqueeze(2).to_broadcast([P, 2, SLOTS]), ALU.is_equal))
            st(V.tensor_tensor(oh_i[:, t], io_i, item[:, t, :].unsqueeze(2).to_broadcast([P, 2, ITEMS]), ALU.is_equal))
        st.settle()
        for t in range(3):
            st(V.tensor_scalar(oh_i[:, t], oh_i[:, t], pack[:, t1 + t:t1 + t + 1], pack[:, va + t:va + t + 1], ALU.mult, ALU.mult), slots_ready)
        b, d = filled_of("slt")
        st(V.tensor_copy(slt[:], b[0:SLOTS, 0:2 * SLOTS].rearrange("p (a n) -> p a n", a=2)[:, :, 0:ITEMS]), slt_done)
        st.settle()
        st(V.tensor_scalar(slt2[:, 0, :], slt[:, 0, :], 0.0, SKIP, ALU.is_equal, ALU.mult))
        st(V.tensor_scalar(slt2[:, 1, :], slt[:, 1, :], 0.0, None, ALU.is_gt))
        st(V.tensor_scalar(slt[:, 0, :], slt[:, 0, :], -1.0, None, ALU.add))
        st.settle()
        st(V.tensor_tensor(slt[:, 0, :], slt[:, 0, :], slt2[:, 0, :], ALU.add))
        st.settle()
        st(V.tensor_copy(idx[:], slt[:, 0, :]))
        st(V.scalar_tensor_tensor(slt[:, 1, :], slt[:, 0, :], 2.0, slt2[:, 1, :], ALU.mult, ALU.add))
        st.settle()
        st(V.tensor_copy(row[:], slt[:, 1, :]), idx_ready)
        st(V.tensor_copy(exf[:, 0:NE], iota[0:1, 0:NE]))
        st(V.tensor_tensor(exm[:], cum[0:1, :].unsqueeze(1).to_broadcast([1, EXTRA, NE]),
                           iota[0:1, 0:EXTRA].unsqueeze(2).to_broadcast([1, EXTRA, NE]), ALU.is_le))
        st.settle()
        st(V.tensor_reduce(exf[:, NE:].unsqueeze(2), exm[:], AX.X, ALU.add))
        st.settle()
        st(V.tensor_scalar(exf[:, NE:], exf[:, NE:], float(NE - 1), None, ALU.min))
        st.settle()
        st(V.tensor_copy(exi[:], exf[:]))
        st(V.tensor_copy(nit[:], cum[0:1, NE - 1:NE]))
        st.settle()
        st(V.memset(stats[:, 0:1], 0.0), nit_ready)

        def item_lo(e, j):
            rs, ss = slot_of(j)
            dve.wait_ge(hi_done, sub(e, j) + 1)
            V.tensor_tensor(wlo[ss][:], raw[rs][:], whi[ss][:].bitcast(F32), ALU.subtract).then_inc(lo_done, 1)

        def x_low(e):
            dve.wait_ge(x_hi, e + 1)
            V.tensor_tensor(xT[:, :, SLOTS:], bank[4][:, :].rearrange("p (k c) -> p k c", k=KD),
                            xT[:, :, 0:SLOTS].bitcast(F32), ALU.subtract).then_inc(x_split, 1)

        def add_low(e, copied, dst, b, low, done):
            dve.wait_ge(copied, e + 1)
            V.tensor_tensor(dst[:], bank[b][0:SLOTS, :], low[:], ALU.add).then_inc(done, 1)

        def hidden(e):
            dve.wait_ge(silu_ok, e + 1)
            dve.wait_ge(u_drained, e + 1)
            V.tensor_tensor(hid[:], aA[:], uS[:], ALU.mult).then_inc(hid_ok, 1)

        def hidden_low(e):
            dve.wait_ge(hh_hi, e + 1)
            V.tensor_tensor(hdT[:, :, SLOTS:], bank[5][:, 0:4 * SLOTS].rearrange("p (k c) -> p k c", k=4),
                            hdT[:, :, 0:SLOTS].bitcast(F32), ALU.subtract).then_inc(hh_split, 1)

        def y_sum(e, written):
            if written:
                dve.wait_ge(y_written, e * 16)
            for j in range(2):
                dve.wait_ge(y_lo, 2 * e + j + 1)
                V.tensor_tensor(ySb[:, j, :], bank[2 + j][0:SLOTS, :], yLo[:, j, :], ALU.add).then_inc(y_drained, 1)

        x_low(0)
        lo(N0 + 3)
        add_low(0, a_lo, aS, 0, aLo, a_drained)
        add_low(0, u_lo, uS, 1, uLo, u_drained)
        x_low(1)

        def item_steps(e, second, third):
            item_lo(e, 0)
            hidden(e - 1)
            item_lo(e, 1)
            if second:
                y_sum(e - 2, third)
            item_lo(e, 2)
            hidden_low(e - 1)
            item_lo(e, 3)
            add_low(e, a_lo, aS, 0, aLo, a_drained)
            item_lo(e, 4)
            item_lo(e, 5)
            add_low(e, u_lo, uS, 1, uLo, u_drained)
            x_low(e + 1)

        item_steps(1, False, False)
        item_steps(2, True, False)
        n_items = NE + dve.value_load(nit[0:1, 0:1], min_val=0, max_val=EXTRA - 1)
        with dve.Fori(3, n_items) as e:
            item_steps(e, True, True)
        item_lo(n_items, 0)
        hidden(n_items - 1)
        item_lo(n_items, 1)
        y_sum(n_items - 2, True)
        hidden_low(n_items - 1)
        y_sum(n_items - 1, True)
        dve.wait_ge(tail_in, 64)
        dve.wait_ge(x1_ready, 3)
        st(V.memset(mv[:], 1.0))

        def combine(t):
            rows = P if t < 2 else DEC
            ya, yb = yg[0:rows, t, 0, :], yg[0:rows, t, 1, :]
            g2 = g2p if t < 2 else g2s
            dve.wait_ge(yg_in[t], 16)
            dve.wait_ge(comb, t + 1)
            st(V.scalar_tensor_tensor(ya, yb, gates[0:rows, t, 1:2], ya, ALU.mult, ALU.add))
            st.settle()
            st(V.scalar_tensor_tensor(ya, g2[0:rows, :], 1.0, ya, ALU.add, ALU.mult))
            st.settle()
            st(V.scalar_tensor_tensor(x1[0:rows, t, :], x1[0:rows, t, :], ALPHA, ya, ALU.mult, ALU.add))
            st.settle()
            for q in range(2):
                st(V.bn_stats(st1[0:rows, t, q, :], x1[0:rows, t, 512 * q:512 * q + 512]))
            st.settle()
            st(V.bn_aggr(mv[0:rows, t, :], st1[0:rows, t, :, :]))
            st.settle()
            st(V.tensor_scalar(mv[:, t, 1:2], mv[:, t, 1:2], LN_EPS, None, ALU.add), fin_std)

        def scale_shift(t):
            dve.wait_ge(ln_std, t + 2)
            st(V.reciprocal(mv[:, t, 1:2], mv[:, t, 1:2]))
            st.settle()
            st(V.scalar_tensor_tensor(mv[:, t, 0:1], mv[:, t, 0:1], -1.0, mv[:, t, 1:2], ALU.mult, ALU.mult), nb_ready)

        def affine(t):
            rows = P if t < 2 else DEC
            xt = x1[0:rows, t, :]
            dve.wait_ge(xn_ready, t + 1)
            st(V.tensor_tensor(xt, xt, l2w[0:rows, :], ALU.mult))
            st.settle()
            st(V.tensor_tensor(xt, xt, l2b[0:rows, :], ALU.add), fin_ready)

        combine(0)
        combine(1)
        scale_shift(0)
        combine(2)
        scale_shift(1)
        affine(0)
        scale_shift(2)
        affine(1)
        affine(2)

    @block.tensor
    def _(pe):
        mm, tr = nc.tensor.matmul, nc.tensor.transpose

        def take(key):
            b, before, f, _ = use[key]
            if before is not None:
                pe.wait_ge(*before)
            return b, f[0]

        def dense(name, H, L):
            c = CI[name]
            for s in range(2):
                n = 2 * c + s
                pe.wait_ge(hi_done, n + 1)
                for t in range(3):
                    b = take((name, t))[0] if s == 0 else use[(name, t)][0]
                    cols = slice(P * t, P * t + P)
                    for kk in range(4):
                        k = 4 * s + kk
                        mm(b[:, :], H[:, k, cols], whi[n % NSPL][:, kk, :], start=(k == 0), stop=False)
                        if t < 2:
                            mm(b[:, :], L[:, k, cols], whi[n % NSPL][:, kk, :], start=False, stop=False)
                    if t == 0:
                        pe.wait_ge(lo_done, n + 1)
                    for kk in range(4):
                        last = mm(b[:, :], H[:, 4 * s + kk, cols], wlo[n % NSPL][:, kk, :], start=False,
                                  stop=(s == 1 and kk == 3))
                    if t == 2:
                        last.then_inc(used, 1)
                    elif s == 1:
                        last.then_inc(use[(name, t)][2][0], 1)

        def ada(j):
            c = CI[f"ada{j}"]
            b, _ = take((f"ada{j}", 0))
            for s in range(2):
                n = 2 * c + s
                pe.wait_ge(hi_done, n + 1)
                for kk in range(4):
                    mm(b[0:64, :], cst[:, 4 * s + kk, :], whi[n % NSPL][:, kk, :], start=(s == 0 and kk == 0), stop=False)
                pe.wait_ge(lo_done, n + 1)
                for kk in range(4):
                    last = mm(b[0:64, :], cst[:, 4 * s + kk, :], wlo[n % NSPL][:, kk, :], start=False,
                              stop=(s == 1 and kk == 3))
                last.then_inc(used, 1)

        def blocks_T(kind, src):
            for k in range(KD):
                b, f = take((kind, k))
                for t in range(3):
                    rows = P if t < 2 else DEC
                    last = tr(b[:, P * t:P * t + rows], src(t, rows, k), ident[0:rows, 0:rows])
                last.then_inc(f, 1)

        pe.wait_ge(pack_in, 16)
        pe.wait_ge(c_silu, 1)
        b, f = take("cT")
        for k in range(KD):
            last = tr(b[:, 2 * k:2 * k + 2], cs2[:, P * k:P * k + P], ident[0:2, 0:2])
        last.then_inc(f, 1)
        pe.wait_ge(c_parts, 1)
        ada(0)
        ada(1)
        pe.wait_ge(x_in, 32)
        blocks_T("xT", lambda t, rows, k: x_tok[0:rows, t, P * k:P * k + P])
        ada(2)
        ada(3)
        b, f = take("modT")
        pe.wait_ge(evacuated, 4)
        for a in range(2):
            for k in range(KD):
                q = a * KD + k
                last = tr(b[:, 2 * q:2 * q + 2], mod[:, P * q:P * q + P], ident[0:2, 0:2])
        last.then_inc(f, 1)
        for j in range(4, 7):
            ada(j)
        b, f = take("zf")
        pe.wait_ge(h_split, KD)
        pe.wait_ge(wf_l, 1)
        for k in range(KD):
            mm(b[0:FH, 0:T], wf_hi[:, k, :], actH[:, k, 0:T], start=(k == 0), stop=False)
            mm(b[0:FH, 0:T], wf_lo[:, k, :], actH[:, k, 0:T], start=False, stop=False)
            mm(b[0:FH, 0:SEQ], wf_hi[:, k, :], actL[:, k, :], start=False, stop=False)
            last = mm(b[0:FH, SEQ:T], wf_hi[:, k, :], actH[:, k, T:384], start=False, stop=(k == KD - 1))
        last.then_inc(f, 1)
        b, f = take("cfT")
        pe.wait_ge(cf_in, 16)
        tr(b[0:FH, 0:PAST], cf_tok[:], ident).then_inc(f, 1)
        dense("rq", actH, actL)
        ada(7)
        ada(8)
        b, f = take("ftok")
        pe.wait_ge(fs_ready, 1)
        idf = ident[0:FH, 0:FH]
        for t in range(3):
            tr(b[:, FH * t:FH * t + FH], fsT[:, P * t:P * t + P], idf)
        tr(b[0:DEC, 3 * FH:4 * FH], fsT[:, SEQ + PAST:T + PAST], idf)
        for t in range(2):
            tr(b[:, FH * (4 + t):FH * (5 + t)], lfT[:, P * t:P * t + P], idf)
        tr(b[0:DEC, 6 * FH:7 * FH], lfT[:, SEQ:T], idf).then_inc(f, 1)
        dense("rk", actH, actL)
        ada(9)
        ada(10)
        dense("rv0", actH, actL)
        ada(11)
        dense("rv1", actH, actL)
        pe.wait_ge(rot_done, 3)
        for j in range(2 * RH):
            b, f = take(("qkT", j))
            for t in range(3):
                rows = P if t < 2 else DEC
                last = tr(b[:, P * t:P * t + rows], rot[0:rows, t, P * j:P * j + P], ident[0:rows, 0:rows])
            last.then_inc(f, 1)
        dense("rg0", actH, actL)
        dense("rg1", actH, actL)
        dense("ga0", actH, actL)
        pe.wait_ge(evacuated, CI["rv1"] + 1)
        pe.wait_ge(kdec_done, 3)
        pe.wait_ge(qd_done, 1)
        pe.wait_ge(dec_in, 32)
        S = slice(SEQ, T)
        for h in range(RH):
            b, f = take(("sc", h))
            mm(b[:, 0:SEQ], kT[:, h, 0:P], qT[:, h, 0:SEQ], start=True, stop=True)
            mm(b[:, SEQ:384], kT[:, h, P:SEQ], qT[:, h, P:SEQ], start=True, stop=True)
            mm(b[0:DEC, 384:448], kT[:, h, S], qT[:, h, S], start=True, stop=True).then_inc(f, 1)
            vs = slice(DV * h, DV * h + DV)
            bp, fp = take(("op", h))
            pe.wait_ge(*use[("sc", h)][3])
            mm(bp[:, 0:DV], sT[:, 0:P], rv[:, 0, vs], start=True, stop=True)
            mm(bp[:, DV:512], sT[:, P:SEQ], rv[:, 0, vs], start=True, stop=False)
            mm(bp[:, DV:512], sT[:, SEQ:384], rv[:, 1, vs], start=False, stop=True).then_inc(fp, 1)
            bs, fs = take(("os", h))
            ks = slice(512 + DK * h, 512 + DK * h + DK)
            mm(bs[0:DEC, 0:DV], sTs, rv[0:DEC, 2, vs], start=True, stop=False)
            mm(bs[0:DEC, 0:DV], qdT[:, h, :], s0[:, h, :], start=False, stop=True)
            mm(bs[:, DV:512], rot[:, 0, ks], rv[:, 0, vs], start=True, stop=False)
            mm(bs[:, DV:512], rot[:, 1, ks], rv[:, 1, vs], start=False, stop=True).then_inc(fs, 1)
            b2, f2 = take(("ss", h))
            mm(b2[:, 0:DV], rot[0:DEC, 2, ks], rv[0:DEC, 2, vs], start=True, stop=True).then_inc(f2, 1)
        for n in ("ga1", "fq0", "fq1", "fk0", "fk1"):
            dense(n, actH, actL)
        pe.wait_ge(ret_ready, 3)
        blocks_T("ret", lambda t, rows, k: o_ret[0:rows, t, P * k:P * k + P])

        def split_ready(kind):
            for k in range(KD):
                pe.wait_ge(*use[(kind, k)][3])

        split_ready("ret")
        dense("pr0", retH, retL)
        dense("pr1", retH, retL)
        dense("fv0", actH, actL)
        dense("fv1", actH, actL)
        for b in range(2):
            pe.wait_ge(*fox_start[b])

        def head_T(h):
            pe.wait_ge(q_st, h + 1)
            for t in range(3):
                rows = P if t < 2 else DEC
                tr(bank[0][0:DH + 2, P * t:P * t + rows], qst[0:rows, t, :], ident[0:rows, 0:rows])
            pe.wait_ge(k_st, h + 1)
            for t in range(4):
                rows = P if t < 3 else DEC
                last = tr(bank[1][0:DH + 2, P * t:P * t + rows], kst[0:rows, t, :], ident[0:rows, 0:rows])
            last.then_inc(qk_tr, 1)

        def scores(h):
            pe.wait_ge(qT_cp, h + 1)
            pe.wait_ge(kT_cp, h + 1)
            mm(bank[2][:, 0:P], qTh[:, 0:P], kTh[:, 0:P], start=True, stop=False)
            mm(bank[2][:, 0:P], identb[:], causalb[:], start=False, stop=True)
            mm(bank[2][:, P:384], qTh[:, P:SEQ], kTh[:, 0:SEQ], start=True, stop=False)
            mm(bank[2][:, SEQ:384], identb[:], causalb[:], start=False, stop=True)
            mm(bank[3][0:DEC, 0:192], qTh[:, SEQ:T], kTh[:, SEQ:T + PAST], start=True, stop=False)
            mm(bank[3][0:DEC, P:192], identb[0:DEC, 0:DEC], causalb[0:DEC, 0:DEC], start=False, stop=True).then_inc(scored, 1)

        def probs_T(h):
            pe.wait_ge(exped, h + 1)
            tr(bank[4][:, 0:P], pr[:, 0, 0:P], ident)
            tr(bank[4][:, P:SEQ], pr[:, 1, 0:P], ident)
            tr(bank[6][:, 0:P], pr[:, 1, P:SEQ], ident)
            tr(bank[6][:, P:192], pr[0:DEC, 2, 0:P], ident[0:DEC, 0:DEC])
            tr(bank[6][0:DEC, 192:SEQ], pr[0:DEC, 2, P:192], ident[0:DEC, 0:DEC]).then_inc(p_tr, 1)

        def weighted(h, first=False):
            if not first:
                pe.wait_ge(o_ok, h)
            pe.wait_ge(v_st, h + 1)
            pe.wait_ge(pT_a, h + 1)
            mm(bank[5][:, 0:DH], prT[:, 0:P], vst[:, 0, :], start=True, stop=True)
            mm(bank[5][:, DH:2 * DH], prT[:, P:SEQ], vst[:, 0, :], start=True, stop=False)
            pe.wait_ge(pT_d, h + 1)
            mm(bank[5][:, DH:2 * DH], prT[:, SEQ:384], vst[:, 1, :], start=False, stop=True)
            mm(bank[5][0:DEC, 2 * DH:3 * DH], prT[:, 384:448], vst[:, 2, :], start=True, stop=False)
            mm(bank[5][0:DEC, 2 * DH:3 * DH], prT[0:DEC, 448:512], vst[0:DEC, 3, :], start=False, stop=True).then_inc(pv_ok, 1)

        head_T(0)
        for b in range(2, 8):
            pe.wait_ge(*fox_start[b])
        scores(0)
        head_T(1)
        probs_T(0)
        scores(1)
        weighted(0, True)
        with pe.Fori(1, FH - 1) as h:
            head_T(h + 1)
            probs_T(h)
            scores(h + 1)
            weighted(h)
        probs_T(FH - 1)
        weighted(FH - 1)
        blocks_T("fox", lambda t, rows, k: fox_o[t][0:rows, P * k:P * k + P])
        dense("gb0", actH, actL)
        dense("gb1", actH, actL)
        split_ready("fox")
        dense("pf0", foxH, foxL)
        dense("pf1", foxH, foxL)
        pe.wait_ge(evacuated, CI["pf1"] + 1)
        blocks_T("mix", lambda t, rows, k: gate[0:rows, t, P * k:P * k + P])
        split_ready("mix")
        dense("wo0", mixH, mixL)
        dense("wo1", mixH, mixL)
        nr = NG + NE

        def logits(t):
            rows = P if t < 2 else DEC
            if t == 0:
                pe.wait_ge(*use["lg"][1])
                pe.wait_ge(wr_in, 64)
            pe.wait_ge(h2T_done, 2 * t + 2)
            for k in range(KD):
                last = mm(use["lg"][0][0:rows, nr * t:nr * t + nr], h2T[:, k, P * t:P * t + rows], wr[:, k, :],
                          start=(k == 0), stop=(k == KD - 1))
            if t == 2:
                last.then_inc(use["lg"][2][0], 1)

        for t in range(3):
            rows = P if t < 2 else DEC
            pe.wait_ge(h2_ready, t + 1)
            for q in range(2):
                b, f = take(("h2T", t, q))
                for kk in range(4):
                    last = tr(b[:, rows * kk:rows * kk + rows], h2[0:rows, t, P * (4 * q + kk):P * (4 * q + kk) + P], ident[0:rows, 0:rows])
                last.then_inc(f, 1)
            if t:
                logits(t - 1)
        logits(2)
        pe.wait_ge(msk_done, 1)
        b, f = take("pos")
        for t in range(3):
            for u in range(t + 1):
                last = mm(b[:, NE * t:NE * t + NE], (befb if u == t else oneb)[:], msk[:, u, :], start=(u == 0), stop=(u == t))
        last.then_inc(f, 1)
        b, f = take("cnt")
        for t in range(3):
            last = mm(b[:, 0:NE], oneb[:], msk[:, t, :], start=(t == 0), stop=(t == 2))
        last.then_inc(f, 1)
        b, f = take("slt")
        pe.wait_ge(slots_ready, 3)
        for t in range(3):
            for ch in range(2):
                mm(b[0:SLOTS, 0:ITEMS], oh_s[:, t, ch, :], oh_i[:, t, ch, :], start=(t == 0 and ch == 0),
                   stop=(t == 2 and ch == 1))
        for t in range(3):
            last = mm(b[0:SLOTS, SLOTS:SLOTS + ITEMS], oh_s[:, t, 1, :], oh_i[:, t, 1, :], start=(t == 0), stop=(t == 2))
        last.then_inc(f, 1)

        def x_transpose(e):
            pe.wait_ge(x_landed, 16 * (e + 1))
            for k in range(KD):
                step = tr if k else mm
                last = step(bank[4][:, SLOTS * k:SLOTS * k + SLOTS], xg[:, P * k:P * k + P], ident[0:SLOTS, 0:SLOTS])
            last.then_inc(x_trans, 1)

        def product(n, ss, b, X, kof, first, final):
            pe.wait_ge(hi_done, n + 1)
            for kk in range(4):
                mm(bank[b][:, :], X[:, kof + kk, :], whi[ss][:, kk, :], start=(first and kk == 0), stop=False)
            pe.wait_ge(lo_done, n + 1)
            for kk in range(4):
                last = mm(bank[b][:, :], X[:, kof + kk, :], wlo[ss][:, kk, :], start=False, stop=(final and kk == 3))
            last.then_inc(used, 1)

        def hidden_T(e):
            pe.wait_ge(hid_ok, e + 1)
            for k in range(4):
                step = tr if k else mm
                last = step(bank[5][:, SLOTS * k:SLOTS * k + SLOTS], hid[:, P * k:P * k + P], ident[0:SLOTS, 0:SLOTS])
            last.then_inc(h_tr, 1)

        def out_product(e, n0_, j0):
            pe.wait_ge(hh_split, e + 1)
            for j in range(2):
                product(n0_ + j, slot_of(j0 + j)[1], 2 + j, hdT, 0, True, True)

        x_transpose(0)
        pe.wait_ge(x_split, 1)
        pe.wait_ge(slt_done, 1)
        for n in range(4):
            product(N0 + n, (N0 + n) % NSPL, n // 2, xT, 4 * (n % 2), n % 2 == 0, n % 2 == 1)
        x_transpose(1)

        def item_products(e, second):
            pe.wait_ge(x_split, e + 1)
            pe.wait_ge(a_drained, e)
            for j in range(2):
                product(sub(e, j), slot_of(j)[1], 0, xT, 4 * j, j == 0, j == 1)
            hidden_T(e - 1)
            pe.wait_ge(u_drained, e)
            for j in range(2):
                product(sub(e, 2 + j), slot_of(2 + j)[1], 1, xT, 4 * j, j == 0, j == 1)
            x_transpose(e + 1)
            if second:
                pe.wait_ge(y_drained, (e - 1) * 2)
            out_product(e - 1, sub(e, 4), 4)

        item_products(1, False)
        pe.wait_ge(nit_ready, 1)
        n_items = NE + pe.value_load(nit[0:1, 0:1], min_val=0, max_val=EXTRA - 1)
        with pe.Fori(2, n_items) as e:
            item_products(e, True)
        hidden_T(n_items - 1)
        pe.wait_ge(y_drained, (n_items - 1) * 2)
        out_product(n_items - 1, sub(n_items, 0), 0)

    ctx.close()


_INS = ["x_prompt", "x_sample", "state_ret", "cache_fox_k", "cache_fox_v", "cache_fox_logf", "c_prompt", "c_sample",
        "w_ada", "b_ada", "w_in", "b_in", "ret_gn_w", "ret_gn_b", "w_ret_proj", "w_fox_proj", "w_o", "ln1_w", "ln1_b",
        "w_rg", "b_rg", "w_re", "b_re", "w_e_in", "w_e_out", "ln2_w", "ln2_b"]
_OUTS = [("y_p", (1, SEQ, D)), ("y_s", (1, DEC, D)), ("p_s", (1, 1, RH, DK, DV)), ("p_k", (1, 1, SEQ, FH, DH)),
         ("p_v", (1, 1, SEQ, FH, DH)), ("p_f", (1, 1, SEQ, FH)), ("s_s", (1, 1, RH, DK, DV)),
         ("s_k", (1, 1, DEC, FH, DH)), ("s_v", (1, 1, DEC, FH, DH)), ("s_f", (1, 1, DEC, FH))]


def kernel(**inputs):
    import concourse.bacc as bacc
    from concourse.bass_utils import run_bass_kernel_spmd

    nc = bacc.Bacc("TRN2", target_bir_lowering=False, num_devices=1)
    arrays = {n: np.ascontiguousarray(inputs[n]) for n in _INS}
    arrays["pack"], arrays["decay"] = shape_tables()
    ins = {n: nc.dram_tensor(f"in_{n}", a.shape, mybir.dt.from_np(a.dtype), kind="ExternalInput").ap() for n, a in arrays.items()}
    outs = {n: nc.dram_tensor(f"out_{n}", s, F32, kind="ExternalOutput").ap() for n, s in _OUTS}
    scratch = {n: nc.dram_tensor(f"scratch_{n}", s, F32, kind="Internal").ap()
               for n, s in (("mod", (2, 4 * D)), ("h2", (T, D)), ("y", (2 * T, D)))}
    build_layer(nc, ins, outs, scratch)
    r = run_bass_kernel_spmd(nc, [{f"in_{n}": a for n, a in arrays.items()}], core_ids=[0])
    return tuple(r.results[0][f"out_{n}"] for n, _ in _OUTS)
```
